# Optimizing a Trainium2 kernel written in Bass

```python
import jax, jax.numpy as jnp
from jax import lax
import numpy as np

D_MODEL = 1024
BATCH = 1
SEQ = 1024
DEPTH = 1
DEC_BATCH = 8
DEC_SEQ = 1
PAST_LEN = 2048
PAGE_SIZE = 128

N_HEADS = 4
QK_NOPE = 128
QK_ROPE = 64
V_DIM = 128
Q_RANK = 384
KV_RANK = 256
ATTN_WIDTH = N_HEADS * V_DIM
CONV_WIDTH = D_MODEL - ATTN_WIDTH
CONV_GROUPS = 4
CONV_K = 3
D_MIX = ATTN_WIDTH + CONV_WIDTH
D_IN = Q_RANK + KV_RANK + QK_ROPE + 3 * CONV_WIDTH
PEER_HEADS = 8
PEER_KEYS = 128
PEER_EXPERTS = PEER_KEYS * PEER_KEYS
PEER_DK = 256
PEER_TOPK = 16
PEER_CHUNK = 128
Q_BLOCK = 128
ROPE_THETA = 10000.0
EPS = 1e-6
SM_SCALE = (QK_NOPE + QK_ROPE) ** -0.5

kernel_name = "hymba_mla_shortconv_peer_step"

def rmsnorm(x, g):
    xf = x.astype(jnp.float32)
    y = xf * lax.rsqrt(jnp.mean(xf * xf, axis=-1, keepdims=True) + EPS)
    return (y * g.astype(jnp.float32)).astype(x.dtype)

def group_rmsnorm(x, g, groups):
    shp = x.shape
    xg = x.reshape(shp[:-1] + (groups, shp[-1] // groups))
    return rmsnorm(xg, g.reshape(groups, shp[-1] // groups)).reshape(shp)

def rope(x, pos):
    p = x.shape[-1]
    inv = ROPE_THETA ** (-jnp.arange(0, p, 2, dtype=jnp.float32) / p)
    ang = pos.astype(jnp.float32)[:, None] * inv[None, :]
    cos = jnp.cos(ang)[None, :, None, :]
    sin = jnp.sin(ang)[None, :, None, :]
    xf = x.astype(jnp.float32)
    x1, x2 = xf[..., : p // 2], xf[..., p // 2:]
    return jnp.concatenate([x1 * cos - x2 * sin, x2 * cos + x1 * sin], axis=-1).astype(x.dtype)

def project(xn, pos, w_in, g_q, w_uq, w_uk, g_kv):
    h = xn @ w_in
    o1 = Q_RANK
    o2 = o1 + KV_RANK
    o3 = o2 + QK_ROPE
    o4 = o3 + CONV_WIDTH
    o5 = o4 + CONV_WIDTH
    cq, ckv, kr, z_in, z_c, z_b = jnp.split(h, [o1, o2, o3, o4, o5], axis=-1)
    q = jnp.einsum('bsr,rhd->bshd', rmsnorm(cq, g_q), w_uq)
    q_nope, q_rope = q[..., :QK_NOPE], q[..., QK_NOPE:]
    q_rope = rope(q_rope, pos)
    q_lat = jnp.einsum('bshd,rhd->bshr', q_nope, w_uk)
    ckv = rmsnorm(ckv, g_kv)
    kr = rope(kr[:, :, None, :], pos)[:, :, 0, :]
    z = z_c * z_in
    return q_lat, q_rope, ckv, kr, z, z_b

def latent_attention(q_lat, q_rope, ckv, kr, mask):
    s = (jnp.einsum('bqhr,bkr->bhqk', q_lat, ckv)
         + jnp.einsum('bqhp,bkp->bhqk', q_rope, kr)).astype(jnp.float32) * SM_SCALE
    s = jnp.where(mask, s, -jnp.inf)
    p = jax.nn.softmax(s, axis=-1).astype(ckv.dtype)
    return jnp.einsum('bhqk,bkr->bqhr', p, ckv)

def prompt_attention(q_lat, q_rope, ckv, kr):
    b, s, h, r = q_lat.shape
    nb = s // Q_BLOCK
    ql = q_lat.reshape(b, nb, Q_BLOCK, h, r).swapaxes(0, 1)
    qr = q_rope.reshape(b, nb, Q_BLOCK, h, QK_ROPE).swapaxes(0, 1)
    kpos = jnp.arange(s)

    def blk(args):
        qlb, qrb, i = args
        qpos = i * Q_BLOCK + jnp.arange(Q_BLOCK)
        mask = kpos[None, :] <= qpos[:, None]
        return latent_attention(qlb, qrb, ckv, kr, mask)

    o = lax.map(blk, (ql, qr, jnp.arange(nb)))
    return o.swapaxes(0, 1).reshape(b, s, h, r)

def short_conv(z_ext, w):
    s = z_ext.shape[1] - (CONV_K - 1)
    y = w[0] * z_ext[:, 0:s]
    for k in range(1, CONV_K):
        y = y + w[k] * z_ext[:, k:k + s]
    return y

def mix_out(o_lat, y_conv, z_b, w_uv, g_attn_out, g_conv_out, w_o):
    b, s = o_lat.shape[:2]
    attn = jnp.einsum('bshr,rhv->bshv', o_lat, w_uv).reshape(b, s, ATTN_WIDTH)
    attn = group_rmsnorm(attn, g_attn_out, N_HEADS)
    conv = group_rmsnorm(z_b * y_conv, g_conv_out, CONV_GROUPS)
    return jnp.concatenate([attn, conv], axis=-1) @ w_o

def peer_block(x, w_query, sub_keys, expert_u, expert_v):
    t = x.shape[0]
    q = (x @ w_query).reshape(t, PEER_HEADS, 2, PEER_DK // 2)
    s = jnp.einsum('thcd,ckd->thck', q, sub_keys).astype(jnp.float32)
    sv, si = lax.top_k(s, PEER_TOPK)
    cand = (sv[:, :, 0, :, None] + sv[:, :, 1, None, :]).reshape(t, PEER_HEADS, PEER_TOPK * PEER_TOPK)
    cidx = (si[:, :, 0, :, None] * PEER_KEYS + si[:, :, 1, None, :]).reshape(t, PEER_HEADS, PEER_TOPK * PEER_TOPK)
    top_s, pos = lax.top_k(cand, PEER_TOPK)
    experts = jnp.take_along_axis(cidx, pos, axis=-1)
    g = jax.nn.softmax(top_s, axis=-1)
    u = expert_u[experts]
    v = expert_v[experts]
    a = jax.nn.gelu(jnp.einsum('td,thkd->thk', x, u).astype(jnp.float32), approximate=False)
    return jnp.einsum('thk,thkd->td', (g * a).astype(x.dtype), v)

def peer_prompt(xn, w_query, sub_keys, expert_u, expert_v):
    b, s, d = xn.shape
    xc = xn.reshape(-1, PEER_CHUNK, d)
    out = lax.map(lambda c: peer_block(c, w_query, sub_keys, expert_u, expert_v), xc)
    return out.reshape(b, s, d)

def setup_inputs(seed: int = 0) -> dict:
    key = jax.random.key(seed)
    ks = jax.random.split(key, 32)
    n_pages = PAST_LEN // PAGE_SIZE
    in_use = DEC_BATCH * n_pages
    n_pool = in_use + max(1, in_use // 4)
    f32 = jnp.float32

    def nrm(k, shape, scale):
        return jax.random.normal(k, shape, f32) * scale

    def gain(k, shape):
        return 1.0 + 0.02 * jax.random.normal(k, shape, f32)

    page_table = jax.random.permutation(ks[5], n_pool)[:in_use].reshape(DEC_BATCH, n_pages).astype(jnp.int32)
    return {
        "x_prompt": nrm(ks[0], (BATCH, SEQ, D_MODEL), 1.0),
        "x_sample": nrm(ks[1], (DEC_BATCH, DEC_SEQ, D_MODEL), 1.0),
        "cache_ckv": nrm(ks[2], (DEPTH, n_pool, PAGE_SIZE, KV_RANK), 1.0),
        "cache_krope": nrm(ks[3], (DEPTH, n_pool, PAGE_SIZE, QK_ROPE), 1.0),
        "state_conv": nrm(ks[4], (DEPTH, DEC_BATCH, CONV_K - 1, CONV_WIDTH), 1.0),
        "page_table": page_table,
        "g_mix_norm": gain(ks[6], (DEPTH, D_MODEL)),
        "w_in": nrm(ks[7], (DEPTH, D_MODEL, D_IN), D_MODEL ** -0.5),
        "g_q": gain(ks[8], (DEPTH, Q_RANK)),
        "w_uq": nrm(ks[9], (DEPTH, Q_RANK, N_HEADS, QK_NOPE + QK_ROPE), Q_RANK ** -0.5),
        "g_kv": gain(ks[10], (DEPTH, KV_RANK)),
        "w_uk": nrm(ks[11], (DEPTH, KV_RANK, N_HEADS, QK_NOPE), KV_RANK ** -0.5),
        "w_uv": nrm(ks[12], (DEPTH, KV_RANK, N_HEADS, V_DIM), KV_RANK ** -0.5),
        "conv_w": nrm(ks[13], (DEPTH, CONV_K, CONV_WIDTH), CONV_K ** -0.5),
        "g_attn_out": gain(ks[14], (DEPTH, ATTN_WIDTH)),
        "g_conv_out": gain(ks[15], (DEPTH, CONV_WIDTH)),
        "w_o": nrm(ks[16], (DEPTH, D_MIX, D_MODEL), D_MIX ** -0.5),
        "g_ffn_norm": gain(ks[17], (DEPTH, D_MODEL)),
        "w_query": nrm(ks[18], (DEPTH, D_MODEL, PEER_HEADS * PEER_DK), D_MODEL ** -0.5),
        "sub_keys": nrm(ks[19], (DEPTH, 2, PEER_KEYS, PEER_DK // 2), (PEER_DK // 2) ** -0.5),
        "expert_u": nrm(ks[20], (DEPTH, PEER_EXPERTS, D_MODEL), D_MODEL ** -0.5),
        "expert_v": nrm(ks[21], (DEPTH, PEER_EXPERTS, D_MODEL), 0.5),
        "g_final": gain(ks[22], (D_MODEL,)),
    }

def reference(x_prompt, x_sample, cache_ckv, cache_krope, state_conv, page_table,
              g_mix_norm, w_in, g_q, w_uq, g_kv, w_uk, w_uv, conv_w, g_attn_out, g_conv_out,
              w_o, g_ffn_norm, w_query, sub_keys, expert_u, expert_v, g_final):
    dec_b, n_pages = page_table.shape
    past = n_pages * PAGE_SIZE
    s_p = x_prompt.shape[1]
    s_d = x_sample.shape[1]
    pos_p = jnp.arange(s_p)
    pos_s = past + jnp.arange(s_d)
    mask_s = jnp.arange(past + s_d)[None, :] <= pos_s[:, None]

    xp, xs = x_prompt, x_sample
    ckv_p_l, kr_p_l, conv_p_l, ckv_s_l, kr_s_l, conv_s_l = [], [], [], [], [], []
    for l in range(DEPTH):
        eu, ev = expert_u[l], expert_v[l]
        xn = rmsnorm(xp, g_mix_norm[l])
        q_lat, q_rope, ckv, kr, z, z_b = project(xn, pos_p, w_in[l], g_q[l], w_uq[l], w_uk[l], g_kv[l])
        o_lat = prompt_attention(q_lat, q_rope, ckv, kr)
        z_ext = jnp.concatenate([jnp.zeros((z.shape[0], CONV_K - 1, CONV_WIDTH), z.dtype), z], axis=1)
        y_conv = short_conv(z_ext, conv_w[l])
        xp = xp + mix_out(o_lat, y_conv, z_b, w_uv[l], g_attn_out[l], g_conv_out[l], w_o[l])
        xp = xp + peer_prompt(rmsnorm(xp, g_ffn_norm[l]), w_query[l], sub_keys[l], eu, ev)
        ckv_p_l.append(ckv)
        kr_p_l.append(kr)
        conv_p_l.append(z_ext[:, -(CONV_K - 1):])
        xn = rmsnorm(xs, g_mix_norm[l])
        q_lat, q_rope, ckv, kr, z, z_b = project(xn, pos_s, w_in[l], g_q[l], w_uq[l], w_uk[l], g_kv[l])
        past_ckv = cache_ckv[l, page_table].reshape(dec_b, past, KV_RANK)
        past_kr = cache_krope[l, page_table].reshape(dec_b, past, QK_ROPE)
        keys_ckv = jnp.concatenate([past_ckv, ckv], axis=1)
        keys_kr = jnp.concatenate([past_kr, kr], axis=1)
        o_lat = latent_attention(q_lat, q_rope, keys_ckv, keys_kr, mask_s)
        z_ext = jnp.concatenate([state_conv[l], z], axis=1)
        y_conv = short_conv(z_ext, conv_w[l])
        xs = xs + mix_out(o_lat, y_conv, z_b, w_uv[l], g_attn_out[l], g_conv_out[l], w_o[l])
        xs2 = rmsnorm(xs, g_ffn_norm[l])
        xs = xs + peer_block(xs2.reshape(-1, D_MODEL), w_query[l], sub_keys[l], eu, ev).reshape(xs.shape)
        ckv_s_l.append(ckv)
        kr_s_l.append(kr)
        conv_s_l.append(z_ext[:, -(CONV_K - 1):])

    y_prompt = rmsnorm(xp, g_final)
    y_sample = rmsnorm(xs, g_final)
    return (y_prompt, y_sample,
            jnp.stack(ckv_p_l), jnp.stack(kr_p_l), jnp.stack(conv_p_l),
            jnp.stack(ckv_s_l), jnp.stack(kr_s_l), jnp.stack(conv_s_l))


_drawn_inputs = setup_inputs


def setup_inputs(seed=0):
    import zlib

    import numpy as np

    out = dict(_drawn_inputs(seed))
    spreads = {}
    factors = {'g_q': 2.844,
     'g_attn_out': 30.939,
     'g_conv_out': 24.453,
     'g_final': 22.617,
     'g_ffn_norm': 16.142}
    for name, (base, spread) in spreads.items():
        noise = np.random.default_rng([zlib.crc32(name.encode()), seed]).standard_normal(out[name].shape)
        drawn = base * np.exp(spread * noise) if base else spread * noise
        out[name] = __import__('jax').numpy.asarray(drawn.astype(out[name].dtype))
    for name, factor in factors.items():
        out[name] = (out[name] * factor).astype(out[name].dtype)
    return out
```

```python
from collections import namedtuple
from contextlib import ExitStack

import concourse.bass as bass
from concourse import mybir

F32 = mybir.dt.float32
U32 = mybir.dt.uint32
I32 = mybir.dt.int32
ALU = mybir.AluOpType
ACT = mybir.ActivationFunctionType
AX = mybir.AxisListType

P = 128
D = 1024
DC = D // P
SEQ = 1024
TILES = SEQ // P
SB = 8
PAGE = 128
NPAGES = 16
PAST = NPAGES * PAGE
H = 4
NOPE = 128
ROPE = 64
QR = 384
KV = 256
CW = 512
D_IN = QR + KV + ROPE + 3 * CW
PH = 8
KEYS = 128
TOPK = 16
SLOTS = PH * TOPK
EPS = 1e-6
SCALE = float(NOPE + ROPE) ** -0.5
BIG = 1e30
LOW = -3.0e38

PW = 256
IN_COLS = [(0, 256), (256, 256), (512, 192)] + [(704 + 256 * k, 256) for k in range(6)]
OUT_COLS = [(256 * k, 256) for k in range(4)]
QUERY_COLS = [(256 * k, 256) for k in range(PH)]
WR = 3
N_IN, N_OUT, N_QUERY = len(IN_COLS), len(OUT_COLS), len(QUERY_COLS)
PIECES = N_IN + N_OUT + N_QUERY
assert PIECES % WR == 0

G = 4
GROUPS = SLOTS // G
RING = 2 * G

HEAD_PIECES, SAMPLE_PIECES, QUERY_PIECES = H + 1, 3 * SB, PH + 1
PIECES_PROMPT = 7 + HEAD_PIECES + 3 + QUERY_PIECES + 1
PIECES_SAMPLE = 7 + SAMPLE_PIECES + 3 + QUERY_PIECES + 1
DVE_FRONT, DVE_PEER, ACT_FRONT, ACT_PEER = 129, 5, 5, 1

ROW_GMIX, ROW_GQ, ROW_GKV, ROW_GOUT, ROW_CONV, VEC_ROWS = 0, 8, 11, 13, 21, 33

EVENTS = """
vec_loaded consts_ready uk_loaded sub_loaded uq_loaded uv_loaded gains_loaded pages_table_loaded
vec_turned vec_kept uk_turned uk_kept sub_turned sub_kept zeroed state_loaded state_turned state_kept
x_loaded rope_loaded w_used
in_ms in_ln in_rs x_scaled x_turned xn_kept
lat_projected lat_kept lat_squared lat_summed lat_ms lat_ln lat_rs cq_normed kv_normed
kr_rotated kr_roped kv_turned kv_rows_kept kv_cols_kept kv_stored
zin_projected zin_kept zc_projected z_kept zb_projected zb_kept conv_done
q_projected q_kept qr_rotated q_roped qlat_projected qlat_kept
scores_made scores_masked max_made exp_made probs_made probs_turned_a probs_turned_b probs_kept_a probs_kept_b pv_made olat_kept
attn_projected attn_kept mix_squared mix_summed mix_ms mix_ln mix_rs mix_normed
mixed x1_kept ffn_ms ffn_ln ffn_rs xn2_made xn2_turned xn2_kept
pq_projected pq_kept key_scores_made key_scores_kept top_keys_done gate_max_made gate_exp_made picked picked_moved
u_free v_free gelu_done w_made diag_made residual_in y_ms y_ln y_rs y_made y_stored acc_free
z_tail_turned z_tail_kept conv_stored
s_new_made s_new_kept
page_turned page_kept page_scores_made page_scores_kept page_max_made page_gmax
page_gmax_spread page_shifted page_exp page_sums page_lsum page_probs page_pv
srow_stored srow_loaded s_turned s_slots s_dots s_gelu s_weights s_fan_free
dve_front dve_peer act_front act_peer dve_setup dve_tail
""".split()


def build(nc, a, out):
    with ExitStack() as ctx:
        def sb(name, shape, dt=F32):
            return ctx.enter_context(nc.sbuf_tensor(name, shape, dt))

        on = namedtuple("Events", EVENTS)(*[ctx.enter_context(nc.semaphore(n)) for n in EVENTS])
        w_loaded = [ctx.enter_context(nc.semaphore(f"w_loaded{r}")) for r in range(WR)]
        u_loaded = [ctx.enter_context(nc.semaphore(f"u_loaded{r}")) for r in range(RING)]
        v_loaded = [ctx.enter_context(nc.semaphore(f"v_loaded{r}")) for r in range(RING)]
        pages_loaded = ctx.enter_context(nc.semaphore("pages_loaded"))

        acc = ctx.enter_context(nc.psum_tensor("acc", [P, 2, 512], F32))
        F = [ctx.enter_context(nc.psum_tensor(f"front{i}", [P, 512], F32)) for i in range(6)]

        ident = sb("ident", [P, P])
        ones = sb("ones", [P, P])
        rot = sb("rot", [ROPE, ROPE])
        low_keys = sb("low_keys", [P, 512])
        q_limit = sb("q_limit", [P, TILES])
        iota16 = sb("iota16", [P, TOPK])
        own_row = sb("own_row", [SB, SB])
        vec_cols = sb("vec_cols", [P, VEC_ROWS])
        g_ffn = sb("g_ffn", [P, D])
        g_fin = sb("g_fin", [P, D])
        w_uq = sb("w_uq", [P, QR // P, H, NOPE + ROPE])
        w_ukT = sb("w_ukT", [P, H, KV])
        w_uv = sb("w_uv", [P, KV // P, H, P])
        sub_keysT = sb("sub_keysT", [P, 2, KEYS])
        w_ring = sb("w_ring", [P, WR, DC, PW])
        ckv_rows = sb("ckv_rows", [P, TILES, KV])
        ckvT = sb("ckvT", [P, 2, SEQ])
        krT = sb("krT", [ROPE, SEQ])
        u_ring = sb("u_ring", [P, RING, D])
        v_ring = sb("v_ring", [P, RING, D])
        diag = sb("diag", [P, RING, P])
        pick_cur = sb("pick_cur", [P, SLOTS], U32)
        pick_next = sb("pick_next", [P, SLOTS], U32)
        gate_cur = sb("gate_cur", [P, SLOTS])
        gate_next = sb("gate_next", [P, SLOTS])
        dots = sb("dots", [P, SLOTS])
        gelu = sb("gelu", [P, SLOTS])
        wgt = sb("wgt", [P, SLOTS])
        xn2_cur = sb("xn2_cur", [P, D])
        rows_next = sb("rows_next", [P, 2, D])
        mo = sb("mo", [P, 2, D])
        x_t = sb("x_t", [P, D])
        work = sb("work", [P, 5 * D])
        cos_t = sb("cos_t", [ROPE, P])
        sin_t = sb("sin_t", [ROPE, P])
        z_ext = sb("z_ext", [P, 4, P + 2])
        z_s = sb("z_s", [P, 4, 3, SB])
        q_ro = sb("q_ro", [ROPE, H, P])
        kr_t = sb("kr_t", [ROPE, 3, P])
        ck_t = sb("ck_t", [P, 2, P])
        kv_rows_t = sb("kv_rows_t", [P, KV + ROPE])
        small = sb("small", [P, 96])
        sv = sb("sv", [P, PH, 2, TOPK])
        si_u = sb("si_u", [P, PH, 2, TOPK], U32)
        si = sb("si", [P, PH, 2, TOPK])
        s_new = sb("s_new", [SB, H * SB])
        page_s = sb("page_s", [P, 4 * (NPAGES + 1)])
        page_p = sb("page_p", [P, 4 * (NPAGES + 1)])
        gm_rows = sb("gm_rows", [H, P])
        s_pick = sb("s_pick", [P, SB], U32)
        s_fan = sb("s_fan", [P, SB, SB])
        page_table_sb = sb("page_table_sb", [1, SB * NPAGES], I32)
        picked_ab = sb("picked_ab", [P, 2, PH, TOPK])

        W = [work[:, k * D:(k + 1) * D] for k in range(5)]
        y_t = W[3]
        zb = W[0][:, 512:1024].rearrange("p (c t) -> p c t", c=4)
        keys_s = W[2][:, 0:2 * KEYS].rearrange("p (c k) -> p c k", c=2)
        pos_f = W[4][:, 0:2 * SLOTS].rearrange("p (c h k) -> p c h k", c=2, h=PH)
        pos_ab = W[4][:, 2 * SLOTS:4 * SLOTS].bitcast(U32).rearrange("p (c h k) -> p c h k", c=2, h=PH)
        top_s = W[4][:, 4 * SLOTS:5 * SLOTS].rearrange("p (h k) -> p h k", h=PH)
        pos_u = W[4][:, 5 * SLOTS:6 * SLOTS].bitcast(U32).rearrange("p (h k) -> p h k", h=PH)
        x1_next, xn2_next = rows_next[:, 0, :], rows_next[:, 1, :]
        mix_raw, o_lat = mo[:, 0, :], mo[:, 1, :]
        cand = mo[:, :, :].rearrange("p a b -> p (a b)")
        pages = work[:, 0:NPAGES * KV].rearrange("p (n r) -> p n r", r=KV)
        pages_kr = work[:, NPAGES * KV:NPAGES * (KV + ROPE)].rearrange("p (n r) -> p n r", r=ROPE)
        pages_T = rows_next[:, :, :].rearrange("p a b -> p (a b)")[:, 0:3 * 512].rearrange("p (c k) -> p c k", c=3)

        SPREAD = [W[0], W[1], W[2], xn2_cur[:, :], W[4], mix_raw, o_lat, x_t[:, :]]

        all_rows = rows_next[:, :, :].rearrange("p a b -> p (a b)")
        q_lat = all_rows[:, D:2 * D].rearrange("p (c h t) -> p c h t", c=2, h=H)
        q_lat_s = all_rows[:, 3 * 512:3 * 512 + 2 * H * SB].rearrange("p (c h t) -> p c h t", c=2, h=H)

        def small_col(n, w=1, rows=P):
            return small[0:rows, n:n + w]

        (C_SS, C_MS, C_Y, C_T, C_SS2, C_MS2, C_Y2, C_T2, C_SS3, C_MS3, C_Y3, C_T3, C_MAX, C_NMAX,
         C_L, C_RL) = range(16)
        C_PM, C_GM, C_PL, C_PLS, C_LIM = 16, 20, 24, 28, 32
        C_GS, C_GR = 40, 48

        def b3(ap, shape):
            return ap.to_broadcast(shape)

        def after(eng, sem, value):
            if isinstance(value, int) and value <= 0:
                return
            eng.wait_ge(sem, value)


        def waited(eng):
            eng.nop(nofuse=True)

        class Own:

            def __init__(self, eng, sem, base):
                self.eng, self.sem, self.base, self.n = eng, sem, base, 0

            def __call__(self, ins, held=False):
                self.n += 1
                ins.then_inc(self.sem, 1)
                self.eng.wait_ge(self.sem, self.base + self.n)
                if held:
                    waited(self.eng)

            def check(self, count):
                assert self.n == count, (self.sem, self.n, count)

        block = ctx.enter_context(nc.Block())

        @block.sync
        def _(sp):
            for dst, src in ((ident, a["c_ident"]), (ones, a["c_ones"]), (rot, a["c_rot"]), (q_limit, a["c_limit"]),
                             (iota16, a["c_iota16"]), (own_row, a["c_own"])):
                sp.dma_start(dst[:], src).then_inc(on.consts_ready, 16)
            r = 0
            for name in ("g_mix_norm", "g_q", "g_kv", "g_attn_out", "g_conv_out"):
                n = a[name].shape[1] // P
                sp.dma_start(W[0][r:r + n, 0:P], a[name].rearrange("l (c p) -> (l c) p", p=P)).then_inc(on.vec_loaded, 16)
                r += n
            sp.dma_start(W[0][r:r + 12, 0:P], a["conv_w"].rearrange("l k (c p) -> (l k c) p", p=P)).then_inc(on.vec_loaded, 16)
            assert r + 12 == VEC_ROWS

            def load_x(f, T, row=0):
                after(sp, on.x1_kept, f)
                waited(sp)
                src = a["x_prompt"][0, bass.ds(row, P), :] if T == P else a["x_sample"].rearrange("b s d -> (b s) d")
                sp.dma_start(x_t[0:T, :], src).then_inc(on.x_loaded, 16)

            def load_rope(f, T, row=0):
                after(sp, on.q_roped, f)
                waited(sp)
                sp.dma_start(cos_t[:, 0:T], a["c_rope"][0, :, bass.ds(row, T)]).then_inc(on.rope_loaded, 16)
                sp.dma_start(sin_t[:, 0:T], a["c_rope"][1, :, bass.ds(row, T)]).then_inc(on.rope_loaded, 16)

            w_src = ([(a["w_in"], c) for c in IN_COLS] + [(a["w_o"], c) for c in OUT_COLS]
                     + [(a["w_query"], c) for c in QUERY_COLS])

            def load_w(f, k):
                after(sp, on.w_used, f * PIECES + k - WR + 1)
                src, (c0, n) = w_src[k]
                sp.dma_start(w_ring[:, k % WR, :, 0:n],
                             src[0].rearrange("(c p) n -> p c n", p=P)[:, :, c0:c0 + n]).then_inc(w_loaded[k % WR], 16)

            def load_tile(f, T):
                row = sp.snap(f * P)
                load_x(f, T, row)
                for k in range(PIECES):
                    load_w(f, k)
                    if k == 2:
                        load_rope(f, T, row)

            load_x(0, P)
            for k in range(WR):
                load_w(0, k)
            sp.dma_start(page_table_sb[:], a["page_table"].rearrange("b n -> (b n)").unsqueeze(0)).then_inc(on.pages_table_loaded, 16)
            sp.dma_start(work[0:2 * SB, 4 * D:4 * D + CW], a["state_conv"].rearrange("l b k c -> (l b k) c"))\
                .then_inc(on.state_loaded, 16)
            sp.dma_start(out["new_conv_sample"][0, :, 0, :], a["state_conv"][0, :, 1, :]).then_inc(on.conv_stored, 16)
            load_rope(0, P)
            sp.dma_start(w_uq[:], a["w_uq"][0].rearrange("(c p) h n -> p c h n", p=P)).then_inc(on.uq_loaded, 16)
            sp.dma_start(work[:, 2 * D:3 * D].rearrange("p (c n) -> p c n", c=2),
                         a["w_uk"][0].rearrange("(c p) h n -> p c (h n)", p=P)).then_inc(on.uk_loaded, 16)
            sp.dma_start(w_uv[:], a["w_uv"][0].rearrange("(c p) h n -> p c h n", p=P)).then_inc(on.uv_loaded, 16)
            sp.dma_start(work[:, 3 * D:3 * D + 256].rearrange("p (c n) -> p c n", c=2),
                         a["sub_keys"][0].rearrange("c k d -> k c d")).then_inc(on.sub_loaded, 16)
            sp.dma_start(low_keys[:], a["c_low"].partition_broadcast(P)).then_inc(on.gains_loaded, 16)
            sp.dma_start(g_ffn[:], a["g_ffn_norm"][0].partition_broadcast(P)).then_inc(on.gains_loaded, 16)
            sp.dma_start(g_fin[:], a["g_final"].partition_broadcast(P)).then_inc(on.gains_loaded, 16)
            for k in range(WR, PIECES):
                load_w(0, k)
            with sp.Fori(1, TILES) as f:
                load_tile(f, P)
            load_x(TILES, SB)
            for k in range(N_IN):
                load_w(TILES, k)
                if k == 2:
                    load_rope(TILES, SB, SEQ)
            for k in range(N_IN, N_IN + WR):
                load_w(TILES, k)
            for b in range(SB):
                if b == 0:
                    for event in (on.qlat_kept, on.q_roped, on.conv_done):
                        sp.wait_ge(event, TILES + 1)
                    sp.wait_ge(on.conv_stored, 3 * 16)
                    sp.wait_ge(on.pages_table_loaded, 16)
                else:
                    sp.wait_ge(on.page_pv, b)
                for n in range(NPAGES):
                    page = sp.value_load(page_table_sb[0:1, b * NPAGES + n:b * NPAGES + n + 1], min_val=0,
                                         max_val=a["cache_ckv"].shape[1] - 1)
                    sp.dma_start(pages[:, n, :], a["cache_ckv"][0, bass.ds(page, 1)].rearrange("a k r -> k (a r)"))\
                        .then_inc(pages_loaded, 16)
                    sp.dma_start(pages_kr[:, n, :], a["cache_krope"][0, bass.ds(page, 1)].rearrange("a k r -> k (a r)"))\
                        .then_inc(pages_loaded, 16)
            for k in range(N_IN + WR, PIECES):
                load_w(TILES, k)
            sp.wait_ge(on.picked, TILES + 1)
            sp.dma_start(a["scratch"], xn2_next[0:SB, :]).then_inc(on.srow_stored, 16)
            sp.wait_ge(on.srow_stored, 16)
            sp.wait_ge(on.u_free, TILES * SLOTS + RING)
            for t in range(SB):
                sp.dma_start(SPREAD[t], a["scratch"][t].partition_broadcast(P)).then_inc(on.srow_loaded, 16)
            sp.wait_ge(on.kv_stored, (TILES + 1) * 2 * 16)
            sp.wait_ge(on.conv_stored, 3 * 16)
            sp.wait_ge(on.y_stored, (TILES + 2) * 16)

        def schedule(g, pieces):
            return [i for i in range(pieces) if i * GROUPS // pieces == g]

        @block.tensor
        def _(pe):
            def weights(f, k):
                pe.wait_ge(w_loaded[k % WR], (f * (PIECES // WR) + k // WR + 1) * 16)
                return w_ring[:, k % WR]

            def project(dst, w, c0, m, xT, T):
                for k in range(DC):
                    last = nc.tensor.matmul(dst, w[:, k, c0:c0 + m], xT[:, k * T:(k + 1) * T],
                                            start=(k == 0), stop=(k == DC - 1))
                return last

            def turn_rows(src, banks, T):
                for c in range(DC):
                    last = nc.tensor.transpose(banks[c // 4][:, (c % 4) * T:(c % 4 + 1) * T],
                                               src[0:T, c * P:(c + 1) * P], ident[0:T, 0:T])
                return last

            def norm_in(f, T):
                pe.wait_ge(on.x_scaled, f + 1)
                turn_rows(W[0], F[0:2], T).then_inc(on.x_turned, 1)

            def proj_lat(f, T):
                xT = W[4]
                pe.wait_ge(on.xn_kept, f + 1)
                for k in range(3):
                    w = weights(f, k)
                    for m in range(2 * k, min(2 * k + 2, 5)):
                        dst = F[2][:, m * T:(m + 1) * T] if m < 3 else F[3][:, (m - 3) * T:(m - 2) * T]
                        last = project(dst, w, (m % 2) * P, P, xT, T)
                    if k < 2:
                        last.then_inc(on.w_used, 1)
                project(F[2][0:ROPE, 3 * T:4 * T], w, P, ROPE, xT, T).then_inc(on.w_used, 1)
                pe.wait_ge(on.lat_squared, f + 1)
                for c in range(3):
                    nc.tensor.matmul(F[4][:, 0:T], ones[:], W[2][:, c * T:(c + 1) * T], start=(c == 0), stop=(c == 2))
                for c in range(2):
                    last = nc.tensor.matmul(F[4][:, T:2 * T], ones[:], W[2][:, (3 + c) * T:(4 + c) * T],
                                            start=(c == 0), stop=(c == 1))
                last.then_inc(on.lat_summed, 1)
                nc.tensor.matmul(F[5][0:ROPE, 0:T], rot[:], kr_t[:, 0, 0:T], start=True, stop=True)\
                    .then_inc(on.kr_rotated, 1)

            def kv_rows(f, T):
                pe.wait_ge(on.kv_normed, f + 1)
                pe.wait_ge(on.kr_roped, f + 1)
                for c in range(2):
                    nc.tensor.transpose(F[2][0:T, c * P:(c + 1) * P], ck_t[:, c, 0:T], ident[:])
                nc.tensor.transpose(F[2][0:T, KV:KV + ROPE], kr_t[:, 1, 0:T], ident[0:ROPE, 0:ROPE])\
                    .then_inc(on.kv_turned, 1)

            def z_group(f, T, k0, bank):
                for k in range(k0, k0 + 2):
                    w = weights(f, k)
                    for m in range(2):
                        c = 2 * (k - k0) + m
                        last = project(F[bank][:, c * T:(c + 1) * T], w, m * P, P, W[4], T)
                    last.then_inc(on.w_used, 1)

            def conv_in(f, T):
                z_group(f, T, 3, 3)
                z_group(f, T, 5, 4)

            def conv_gate(f, T):
                z_group(f, T, 7, 5)
                if T != P:
                    pe.wait_ge(on.z_kept, f + 1)
                    for c in range(4):
                        nc.tensor.transpose(F[0][0:SB, c * P:(c + 1) * P], z_s[:, c, 2, :], ident[:])
                    for c in range(4):
                        last = nc.tensor.transpose(F[1][0:2, c * P:(c + 1) * P], z_ext[:, c, 0:2], ident[:])
                    last.then_inc(on.z_tail_turned, 1)

            def q_proj(f, T):
                pe.wait_ge(on.cq_normed, f + 1)
                if T != P:
                    pe.wait_ge(on.z_tail_kept, 1)
                for h in range(H):
                    for c in range(3):
                        nc.tensor.matmul(F[0][:, h * T:(h + 1) * T], w_uq[:, c, h, 0:NOPE], W[1][:, c * T:(c + 1) * T],
                                         start=(c == 0), stop=(c == 2))
                for h in range(H):
                    for c in range(3):
                        last = nc.tensor.matmul(F[1][0:ROPE, h * T:(h + 1) * T], w_uq[:, c, h, NOPE:NOPE + ROPE],
                                                W[1][:, c * T:(c + 1) * T], start=(c == 0), stop=(c == 2))
                last.then_inc(on.q_projected, 1)

            def q_latent(f, T):
                pe.wait_ge(on.q_kept, f + 1)
                pe.wait_ge(on.kv_rows_kept, f + 1)
                waited(pe)
                nc.tensor.matmul(F[2][0:ROPE, 0:4 * T], rot[:], W[4][0:ROPE, 512:512 + 4 * T], start=True, stop=True)\
                    .then_inc(on.qr_rotated, 1)
                pe.wait_ge(on.z_kept, f + 1)
                for c in range(2):
                    for h in range(H):
                        last = nc.tensor.matmul(F[3 + c][:, h * T:(h + 1) * T], w_ukT[:, h, c * P:(c + 1) * P],
                                                W[4][:, h * T:(h + 1) * T], start=True, stop=True)
                last.then_inc(on.qlat_projected, 1)

            def head_start(f, h):
                n = f * H + h
                if h == 0:
                    pe.wait_ge(on.qlat_kept, f + 1)
                    pe.wait_ge(on.q_roped, f + 1)
                    pe.wait_ge(on.kv_cols_kept, f + 1)
                else:
                    pe.wait_ge(on.scores_masked, n)
                for half in range(2):
                    ks = slice(half * 512, half * 512 + 512)
                    for c in range(2):
                        nc.tensor.matmul(F[half][:, :], q_lat[:, c, h, :], ckvT[:, c, ks], start=(c == 0), stop=False)
                    last = nc.tensor.matmul(F[half][:, :], q_ro[:, h, :], krT[:, ks], start=False, stop=True)
                last.then_inc(on.scores_made, 1)

            def head_end(f, h):
                n = f * H + h
                pe.wait_ge(on.probs_made, n + 1)
                for j in range(4):
                    last = nc.tensor.transpose(F[2][:, j * P:(j + 1) * P], W[0][:, j * P:(j + 1) * P], ident[:])
                last.then_inc(on.probs_turned_a, 1)
                for j in range(4):
                    last = nc.tensor.transpose(F[3][:, j * P:(j + 1) * P], W[0][:, (4 + j) * P:(5 + j) * P], ident[:])
                last.then_inc(on.probs_turned_b, 1)
                pe.wait_ge(on.probs_kept_a, n + 1)
                pe.wait_ge(on.probs_kept_b, n + 1)
                for c in range(2):
                    for j in range(TILES):
                        last = nc.tensor.matmul(F[4][:, c * P:(c + 1) * P], ckv_rows[:, j, c * P:(c + 1) * P],
                                                W[1][:, j * P:(j + 1) * P], start=(j == 0), stop=(j == TILES - 1))
                last.then_inc(on.pv_made, 1)

            def attn_out(f, T):
                pe.wait_ge(on.olat_kept, (f + 1) * H if T == P else TILES * H + SB)
                pe.wait_ge(on.zb_kept, f + 1)
                for h in range(H):
                    for c in range(2):
                        last = nc.tensor.matmul(F[5][:, h * T:(h + 1) * T], w_uv[:, c, h, :],
                                                o_lat[:, (c * H + h) * T:(c * H + h + 1) * T],
                                                start=(c == 0), stop=(c == 1))
                last.then_inc(on.attn_projected, 1)
                pe.wait_ge(on.mix_squared, f + 1)
                for half in range(2):
                    last = nc.tensor.matmul(F[half][:, 0:4 * T], ones[:], W[0][:, half * 4 * T:(half + 1) * 4 * T],
                                            start=True, stop=True)
                last.then_inc(on.mix_summed, 1)

            def mix_out(f, T):
                pe.wait_ge(on.mix_normed, f + 1)
                for j in range(N_OUT):
                    w = weights(f, N_IN + j)
                    dst = F[2 + j // 2][0:T, (j % 2) * 256:(j % 2) * 256 + 256]
                    for k in range(DC):
                        last = nc.tensor.matmul(dst, W[2][:, k * T:(k + 1) * T], w[:, k, :],
                                                start=(k == 0), stop=(k == DC - 1))
                    last.then_inc(on.w_used, 1)

            def ffn_turn(f, T):
                pe.wait_ge(on.xn2_made, f + 1)
                turn_rows(xn2_next, F[4:6], T).then_inc(on.xn2_turned, 1)

            def query_start(f, T, h):
                n = f * PH + h
                if h == 0:
                    pe.wait_ge(on.xn2_kept, f + 1)
                else:
                    pe.wait_ge(on.pq_kept, n)
                w = weights(f, N_IN + N_OUT + h)
                for c in range(2):
                    last = project(F[0][:, c * T:(c + 1) * T], w, c * P, P, W[4], T)
                last.then_inc(on.w_used, 1)

            def query_end(f, T, h):
                n = f * PH + h
                pe.wait_ge(on.pq_kept, n + 1)
                if h:
                    pe.wait_ge(on.key_scores_kept, n)
                for c in range(2):
                    last = nc.tensor.matmul(F[1][0:T, c * KEYS:(c + 1) * KEYS], W[3][:, c * T:(c + 1) * T],
                                            sub_keysT[:, c, :], start=True, stop=True)
                last.then_inc(on.key_scores_made, 1)

            def page_scores(f, b, part):
                for pg in range(4):
                    n = 4 * part + pg
                    for c in range(2):
                        nc.tensor.transpose(F[c][:, pg * P:(pg + 1) * P], pages[:, n, c * P:(c + 1) * P], ident[:])
                    last = nc.tensor.transpose(F[2][0:ROPE, pg * P:(pg + 1) * P], pages_kr[:, n, :], ident[:])
                last.then_inc(on.page_turned, 1)
                pe.wait_ge(on.page_kept, 2 * (4 * b + part + 1))
                for pg in range(4):
                    n = 4 * part + pg
                    for c in range(2):
                        nc.tensor.matmul(F[3][:, 4 * n:4 * n + 4], pages_T[:, c, pg * P:(pg + 1) * P],
                                         q_lat_s[:, c, :, b], start=(c == 0), stop=False)
                    last = nc.tensor.matmul(F[3][:, 4 * n:4 * n + 4], pages_T[0:ROPE, 2, pg * P:(pg + 1) * P],
                                            q_ro[:, :, b], start=False, stop=True)
                last.then_inc(on.page_scores_made, 1)

            def sample_keys(f, b, part):
                if b == 0 and part == 0:
                    pe.wait_ge(on.qlat_kept, f + 1)
                    pe.wait_ge(on.q_roped, f + 1)
                    for c in range(2):
                        nc.tensor.matmul(F[5][0:SB, 0:4 * SB], ck_t[:, c, 0:SB],
                                         q_lat_s[:, c, :, :], start=(c == 0), stop=False)
                    nc.tensor.matmul(F[5][0:SB, 0:4 * SB], kr_t[:, 1, 0:SB], q_ro[:, :, 0:SB],
                                     start=False, stop=True).then_inc(on.s_new_made, 1)
                    pe.wait_ge(on.s_new_kept, 1)
                if part == 0:
                    pe.wait_ge(pages_loaded, (b + 1) * 2 * NPAGES * 16)
                    if b:
                        pe.wait_ge(on.page_scores_kept, b)
                for q in (2 * part, 2 * part + 1):
                    page_scores(f, b, q)

            def sample_attend(f, b):
                pe.wait_ge(on.page_max_made, 2 * b + 1)
                nc.tensor.transpose(F[4][0:H, 0:P], small_col(C_PM, 4), ident[:]).then_inc(on.page_gmax, 1)
                pe.wait_ge(on.page_max_made, 2 * b + 2)
                nc.tensor.matmul(F[4][:, 128:132], gm_rows[:], ident[0:H, 0:H], start=True, stop=True)\
                    .then_inc(on.page_gmax_spread, 1)
                pe.wait_ge(on.page_sums, b + 1)
                nc.tensor.matmul(F[4][:, 132:136], ones[:], small_col(C_PL, 4), start=True, stop=True)\
                    .then_inc(on.page_lsum, 1)
                pe.wait_ge(on.page_probs, b + 1)
                for c in range(2):
                    for n in range(NPAGES):
                        nc.tensor.matmul(F[5][:, 4 * c:4 * c + 4], pages[:, n, c * P:(c + 1) * P],
                                         page_p[:, 4 * n:4 * n + 4], start=(n == 0), stop=False)
                    last = nc.tensor.matmul(F[5][:, 4 * c:4 * c + 4], kv_rows_t[0:SB, c * P:(c + 1) * P],
                                            page_p[0:SB, 4 * NPAGES:4 * NPAGES + 4], start=False, stop=True)
                last.then_inc(on.page_pv, 1)

            def v_group(it, g):
                for r in range(G):
                    slot = (g % 2) * G + r
                    pe.wait_ge(on.diag_made, it * SLOTS + g * G + r + 1)
                    pe.wait_ge(v_loaded[slot], (it * (GROUPS // 2) + g // 2 + 1) * 16)
                    for half in range(2):
                        last = nc.tensor.matmul(acc[:, half, :], diag[:, slot, :], v_ring[:, slot, half * 512:half * 512 + 512],
                                                start=False, stop=(g == GROUPS - 1 and r == G - 1))
                    last.then_inc(on.v_free, 1)

            def residual(f):
                after(pe, on.acc_free, f)
                pe.wait_ge(on.x1_kept, f + 1)
                for half in range(2):
                    last = nc.tensor.matmul(acc[:, half, :], ident[:], x1_next[:, half * 512:half * 512 + 512],
                                            start=True, stop=False)
                last.then_inc(on.residual_in, 1)

            def piece(f, T, i):
                if i == 0:
                    norm_in(f, T)
                elif i == 1:
                    proj_lat(f, T)
                elif i == 2:
                    kv_rows(f, T)
                elif i == 3:
                    conv_in(f, T)
                elif i == 4:
                    conv_gate(f, T)
                elif i == 5:
                    q_proj(f, T)
                elif i == 6:
                    q_latent(f, T)
                elif T == P and i < 7 + HEAD_PIECES:
                    if i > 7:
                        head_end(f, i - 8)
                    if i < 7 + H:
                        head_start(f, i - 7)
                elif T != P and i < 7 + SAMPLE_PIECES:
                    b, part = divmod(i - 7, 3)
                    if part < 2:
                        sample_keys(f, b, part)
                    else:
                        sample_attend(f, b)
                else:
                    i -= 7 + (HEAD_PIECES if T == P else SAMPLE_PIECES)
                    if i == 0:
                        attn_out(f, T)
                    elif i == 1:
                        mix_out(f, T)
                    elif i == 2:
                        ffn_turn(f, T)
                    elif i < 3 + QUERY_PIECES:
                        if i > 3:
                            query_end(f, T, i - 4)
                        if i < 3 + PH:
                            query_start(f, T, i - 3)

            def tile(it, T):
                for g in range(GROUPS):
                    for i in schedule(g, PIECES_PROMPT if T == P else PIECES_SAMPLE):
                        piece(it + 1, T, i)
                    v_group(it, g)

            pe.wait_ge(on.consts_ready, 6 * 16)
            pe.wait_ge(on.vec_loaded, 6 * 16)
            nc.tensor.transpose(F[0][:, 0:VEC_ROWS], W[0][0:VEC_ROWS, 0:P], ident[0:VEC_ROWS, 0:VEC_ROWS]).then_inc(on.vec_turned, 1)
            pe.wait_ge(on.uk_loaded, 16)
            for h in range(H):
                for c in range(2):
                    last = nc.tensor.transpose(F[1 + h // 2][:, (h % 2) * KV + c * P:(h % 2) * KV + (c + 1) * P],
                                               W[2][:, c * 512 + h * P:c * 512 + (h + 1) * P], ident[:])
            last.then_inc(on.uk_turned, 1)
            pe.wait_ge(on.sub_loaded, 16)
            for c in range(2):
                last = nc.tensor.transpose(F[3][:, c * P:(c + 1) * P], W[3][:, c * P:(c + 1) * P], ident[:])
            last.then_inc(on.sub_turned, 1)
            pe.wait_ge(on.state_loaded, 16)
            for c in range(4):
                last = nc.tensor.transpose(F[4][:, c * 2 * SB:(c + 1) * 2 * SB], W[4][0:2 * SB, c * P:(c + 1) * P],
                                           ident[0:2 * SB, 0:2 * SB])
            last.then_inc(on.state_turned, 1)
            pe.wait_ge(on.uq_loaded, 16)
            pe.wait_ge(on.uv_loaded, 16)
            for i in range(PIECES_PROMPT):
                piece(0, P, i)
            residual(0)
            with pe.Fori(0, TILES - 1) as it:
                tile(it, P)
                residual(it + 1)
            tile(TILES - 1, SB)
            pe.wait_ge(on.picked, TILES + 1)
            nc.tensor.transpose(F[0][:, 0:SB], picked_ab[0:SB, 0, :, :].rearrange("p h k -> p (h k)"), ident[0:SB, 0:SB])
            nc.tensor.transpose(F[0][:, SB:2 * SB], gate_next[0:SB, :], ident[0:SB, 0:SB]).then_inc(on.s_turned, 1)
            pe.wait_ge(on.acc_free, TILES)
            for half in range(2):
                nc.tensor.matmul(acc[0:SB, half, :], ident[0:SB, 0:SB], x1_next[0:SB, half * 512:half * 512 + 512],
                                 start=True, stop=False)
            pe.wait_ge(on.s_weights, 1)
            for t in range(SB):
                pe.wait_ge(v_loaded[t], (TILES * (GROUPS // 2) + 1) * 16)
                for half in range(2):
                    last = nc.tensor.matmul(acc[0:SB, half, :], s_fan[:, t, :], v_ring[:, t, half * 512:half * 512 + 512],
                                            start=False, stop=(t == SB - 1))
            last.then_inc(on.v_free, 1)

        @block.scalar
        def _(act):
            def rsqrt_start(own, dst, ms):
                own(nc.scalar.activation(dst, ms, ACT.Ln))
                return nc.scalar.activation(dst, dst, ACT.Exp, scale=-0.5)

            def piece(own, f, T, i):
                if i == 0:
                    act.wait_ge(on.in_ms, f + 1)
                    rsqrt_start(own, small_col(C_Y, 1, T), small_col(C_MS, 1, T)).then_inc(on.in_rs, 1)
                elif i == 1:
                    act.wait_ge(on.w_used, f * PIECES + 3)
                    nc.scalar.copy(W[1][:, 0:3 * T], F[2][:, 0:3 * T])
                    nc.scalar.copy(W[1][:, 3 * T:5 * T], F[3][:, 0:2 * T])
                    nc.scalar.copy(kr_t[:, 0, 0:T], F[2][0:ROPE, 3 * T:4 * T]).then_inc(on.lat_kept, 1)
                    act.wait_ge(on.lat_ms, f + 1)
                    rsqrt_start(own, W[3][:, 256:256 + 2 * T], W[3][:, 0:2 * T]).then_inc(on.lat_rs, 1)
                elif i == 2:
                    act.wait_ge(on.kv_turned, f + 1)
                    after(act, on.kv_stored, f * 2 * 16)
                    own(nc.scalar.copy(kv_rows_t[0:T, :], F[2][0:T, 0:KV + ROPE]))
                    if T == P:
                        if isinstance(f, int):
                            act.wait_ge(on.zeroed, 3)
                        nc.scalar.copy(ckv_rows[:, bass.ds(f, 1), :].rearrange("p a r -> p (a r)"), F[2][:, 0:KV])\
                            .then_inc(on.kv_rows_kept, 1)
                        nc.scalar.copy(ckvT[:, :, bass.ds(f * P, P)], ck_t[:, :, :])
                        nc.scalar.copy(krT[:, bass.ds(f * P, P)], kr_t[:, 1, :]).then_inc(on.kv_cols_kept, 1)
                        ckv_out, kr_out = out["new_ckv_prompt"][0, 0, bass.ds(f * P, P)], out["new_krope_prompt"][0, 0, bass.ds(f * P, P)]
                    else:
                        nc.scalar.copy(page_s[0:1, 0:1], ones[0:1, 0:1]).then_inc(on.kv_rows_kept, 1)
                        ckv_out = out["new_ckv_sample"].rearrange("l b s r -> (l b s) r")
                        kr_out = out["new_krope_sample"].rearrange("l b s r -> (l b s) r")
                    act.dma_start(ckv_out, kv_rows_t[0:T, 0:KV]).then_inc(on.kv_stored, 16)
                    act.dma_start(kr_out, kv_rows_t[0:T, KV:KV + ROPE]).then_inc(on.kv_stored, 16)
                elif i == 3:
                    act.wait_ge(on.w_used, f * PIECES + 5)
                    nc.scalar.copy(W[0][:, 0:4 * T], F[3][:, 0:4 * T]).then_inc(on.zin_kept, 1)
                elif i == 4:
                    act.wait_ge(on.w_used, f * PIECES + 9)
                    nc.scalar.copy(zb[:, :, 0:T], F[5][:, 0:4 * T].rearrange("p (c t) -> p c t", c=4)).then_inc(on.zb_kept, 1)
                    if T != P:
                        act.wait_ge(on.z_tail_turned, 1)
                        act.wait_ge(on.conv_done, f + 1)
                        own(nc.scalar.copy(W[3][0:SB, 0:CW], F[0][0:SB, :]))
                        nc.scalar.copy(W[3][0:2, CW:2 * CW], F[1][0:2, :]).then_inc(on.z_tail_kept, 1)
                        act.wait_ge(on.z_tail_kept, 1)
                        act.dma_start(out["new_conv_sample"][0, :, 1, :], W[3][0:SB, 0:CW]).then_inc(on.conv_stored, 16)
                        act.dma_start(out["new_conv_prompt"][0, 0], W[3][0:2, CW:2 * CW]).then_inc(on.conv_stored, 16)
                elif i == 5:
                    act.wait_ge(on.q_projected, f + 1)
                    nc.scalar.copy(W[4][:, 0:4 * T], F[0][:, 0:4 * T])
                    nc.scalar.copy(W[4][0:ROPE, 512:512 + 4 * T], F[1][0:ROPE, 0:4 * T]).then_inc(on.q_kept, 1)
                elif i == 6:
                    act.wait_ge(on.qlat_projected, f + 1)
                    for c in range(2):
                        last = nc.scalar.copy((q_lat if T == P else q_lat_s)[:, c, :, :], F[3 + c][:, 0:4 * T].rearrange("p (h t) -> p h t", h=H))
                    last.then_inc(on.qlat_kept, 1)
                elif T == P and i < 7 + HEAD_PIECES:
                    if i > 7:
                        h = i - 8
                        n = f * H + h
                        act.wait_ge(on.probs_turned_b, n + 1)
                        nc.scalar.copy(W[1][:, 512:1024], F[3][:, :]).then_inc(on.probs_kept_b, 1)
                    if i < 7 + H:
                        act.wait_ge(on.max_made, f * H + i - 7 + 1)
                        nc.scalar.activation(W[0], W[0], ACT.Exp, bias=small_col(C_NMAX), scale=SCALE,
                                             accum_out=small_col(C_L)).then_inc(on.exp_made, 1)
                    if i > 7:
                        act.wait_ge(on.pv_made, n + 1)
                        nc.scalar.copy(o_lat.rearrange("p (c h t) -> p c h t", c=2, h=H)[:, :, h, :],
                                       F[4][:, 0:2 * P].rearrange("p (c t) -> p c t", c=2)).then_inc(on.olat_kept, 1)
                elif T != P and i < 7 + SAMPLE_PIECES:
                    b, part = divmod(i - 7, 3)
                    if part < 2:
                        for q in (2 * part, 2 * part + 1):
                            act.wait_ge(on.page_turned, 4 * b + q + 1)
                            nc.scalar.copy(pages_T[:, 0, :], F[0][:, :]).then_inc(on.page_kept, 1)
                    else:
                        act.wait_ge(on.page_shifted, b + 1)
                        nc.scalar.activation(page_p[:], page_s[:], ACT.Exp, scale=SCALE).then_inc(on.page_exp, 1)
                        act.wait_ge(on.page_pv, b + 1)
                        nc.scalar.copy(o_lat[:, 0:2 * H * SB].rearrange("p (c t) -> p c t", t=SB)[:, :, b],
                                       F[5][:, 0:2 * H]).then_inc(on.olat_kept, 1)
                else:
                    i -= 7 + (HEAD_PIECES if T == P else SAMPLE_PIECES)
                    if i == 0:
                        act.wait_ge(on.attn_projected, f + 1)
                        nc.scalar.copy(mix_raw[:, 0:4 * T], F[5][:, 0:4 * T]).then_inc(on.attn_kept, 1)
                        act.wait_ge(on.mix_ms, f + 1)
                        rsqrt_start(own, W[1][:, 0:8 * T], W[0][:, 0:8 * T]).then_inc(on.mix_rs, 1)
                    elif i == 2:
                        act.wait_ge(on.ffn_ms, f + 1)
                        rsqrt_start(own, small_col(C_Y2, 1, T), small_col(C_MS2, 1, T)).then_inc(on.ffn_rs, 1)
                    elif 3 <= i < 3 + QUERY_PIECES:
                        if i > 3:
                            h = i - 4
                            act.wait_ge(on.key_scores_made, f * PH + h + 1)
                            after(act, on.top_keys_done, f * PH + h)
                            nc.scalar.copy(keys_s[0:T].rearrange("p c k -> p (c k)"), F[1][0:T, 0:2 * KEYS])\
                                .then_inc(on.key_scores_kept, 1)
                        if i < 3 + PH:
                            act.wait_ge(on.w_used, f * PIECES + N_IN + N_OUT + i - 3 + 1)
                            nc.scalar.copy(W[3][:, 0:2 * T], F[0][:, 0:2 * T]).then_inc(on.pq_kept, 1)
                    elif i == 3 + QUERY_PIECES:
                        act.wait_ge(on.gate_max_made, f + 1)
                        nc.scalar.activation(gate_next[0:T, :], gate_next[0:T, :], ACT.Exp).then_inc(on.gate_exp_made, 1)

            def gelu_group(it, g):
                act.wait_ge(on.u_free, it * SLOTS + (g + 1) * G + RING)
                nc.scalar.activation(gelu[:, g * G:(g + 1) * G], dots[:, g * G:(g + 1) * G], ACT.Gelu).then_inc(on.gelu_done, 1)

            def diag_group(it, g):
                act.wait_ge(on.w_made, it * GROUPS + g + 1)
                act.wait_ge(on.v_free, it * SLOTS + (g + 1) * G)
                for r in range(G):
                    s = g * G + r
                    nc.scalar.activation(diag[:, s % RING, :], ident[:], ACT.Copy, scale=wgt[:, s:s + 1]).then_inc(on.diag_made, 1)

            def finalize(own, it, T):
                act.wait_ge(on.y_ms, it + 1)
                rsqrt_start(own, small_col(C_Y3, 1, T), small_col(C_MS3, 1, T)).then_inc(on.y_rs, 1)
                act.wait_ge(on.y_made, it + 1)
                dst = out["y_prompt"][0, bass.ds(it * P, P)] if T == P else out["y_sample"].rearrange("b s d -> (b s) d")
                act.dma_start(dst, y_t[0:T, :]).then_inc(on.y_stored, 16)

            def tile(it, T):
                own = Own(act, on.act_front, (it + 1) * ACT_FRONT)
                for g in range(GROUPS):
                    gelu_group(it, g)
                    diag_group(it, g)
                    for i in schedule(g, PIECES_PROMPT if T == P else PIECES_SAMPLE):
                        piece(own, it + 1, T, i)
                if T == P:
                    own.check(ACT_FRONT)
                own2 = Own(act, on.act_peer, it * ACT_PEER)
                finalize(own2, it, P)
                own2.check(ACT_PEER)

            own = Own(act, on.act_front, 0)
            act.wait_ge(on.consts_ready, 6 * 16)
            for i in range(PIECES_PROMPT):
                piece(own, 0, P, i)
            own.check(ACT_FRONT)
            with act.Fori(0, TILES - 1) as it:
                tile(it, P)
            tile(TILES - 1, SB)
            act.wait_ge(on.s_dots, SB)
            nc.scalar.activation(gelu[:, 0:SB], dots[:, 0:SB], ACT.Gelu).then_inc(on.s_gelu, 1)
            finalize(Own(act, on.act_peer, TILES * ACT_PEER), TILES, SB)

        @block.vector
        def _(dve):
            v = nc.vector

            def sharpen(own, ms, y, t):
                own(v.tensor_tensor(t, ms, y, ALU.mult))
                own(v.scalar_tensor_tensor(out=t, in0=t, scalar=-0.5, in1=y, op0=ALU.mult, op1=ALU.mult))
                own(v.scalar_tensor_tensor(out=y, in0=t, scalar=1.5, in1=y, op0=ALU.add, op1=ALU.mult))

            def mean(dst, total, n):
                return v.tensor_scalar(dst, total, 1.0 / n, EPS, ALU.mult, ALU.add)

            def spread_cols(first, n, T):
                return vec_cols[:, first:first + n].unsqueeze(2).to_broadcast([P, n, T])

            def split(ap, c):
                return ap.rearrange("p (c t) -> p c t", c=c)

            def norm_in(own, f, T):
                dve.wait_ge(on.x_loaded, (f + 1) * 16)
                own(v.tensor_tensor_reduce(W[0][0:T, :], x_t[0:T, :], x_t[0:T, :], 1.0, 0.0, ALU.mult, ALU.add, small_col(C_SS, 1, T)))
                mean(small_col(C_MS, 1, T), small_col(C_SS, 1, T), D).then_inc(on.in_ms, 1)
                dve.wait_ge(on.in_rs, f + 1)
                sharpen(own, small_col(C_MS, 1, T), small_col(C_Y, 1, T), small_col(C_T, 1, T))
                v.tensor_scalar(W[0][0:T, :], x_t[0:T, :], small_col(C_Y, 1, T), None, ALU.mult).then_inc(on.x_scaled, 1)
                dve.wait_ge(on.x_turned, f + 1)
                for half in range(2):
                    last = v.tensor_tensor(split(W[4][:, half * 4 * T:(half + 1) * 4 * T], 4), split(F[half][:, 0:4 * T], 4),
                                           spread_cols(ROW_GMIX + 4 * half, 4, T), ALU.mult)
                last.then_inc(on.xn_kept, 1)

            def latents(own, f, T):
                dve.wait_ge(on.lat_kept, f + 1)
                v.tensor_tensor(W[2][:, 0:5 * T], W[1][:, 0:5 * T], W[1][:, 0:5 * T], ALU.mult).then_inc(on.lat_squared, 1)
                dve.wait_ge(on.lat_summed, f + 1)
                after(dve, on.y_stored, f * 16)
                mean(W[3][:, 0:T], F[4][:, 0:T], QR)
                mean(W[3][:, T:2 * T], F[4][:, T:2 * T], KV).then_inc(on.lat_ms, 1)
                dve.wait_ge(on.kr_rotated, f + 1)
                dve.wait_ge(on.rope_loaded, (f + 1) * 2 * 16)
                own(v.tensor_tensor(kr_t[:, 1, 0:T], kr_t[:, 0, 0:T], cos_t[:, 0:T], ALU.mult))
                own(v.tensor_tensor(kr_t[:, 2, 0:T], F[5][0:ROPE, 0:T], sin_t[:, 0:T], ALU.mult))
                v.tensor_tensor(kr_t[:, 1, 0:T], kr_t[:, 1, 0:T], kr_t[:, 2, 0:T], ALU.add).then_inc(on.kr_roped, 1)
                dve.wait_ge(on.lat_ms, f + 1)
                dve.wait_ge(on.lat_rs, f + 1)
                rs = W[3][:, 256:256 + 2 * T]
                sharpen(own, W[3][:, 0:2 * T], rs, W[3][:, 512:512 + 2 * T])
                for c in range(5):
                    dst = W[1][:, c * T:(c + 1) * T] if c < 3 else ck_t[:, c - 3, 0:T]
                    last = v.scalar_tensor_tensor(out=dst, in0=W[1][:, c * T:(c + 1) * T], scalar=vec_cols[:, ROW_GQ + c:ROW_GQ + c + 1],
                                                  in1=rs[:, 0:T] if c < 3 else rs[:, T:2 * T], op0=ALU.mult, op1=ALU.mult)
                    if c == 2:
                        last.then_inc(on.cq_normed, 1)
                last.then_inc(on.kv_normed, 1)

            def conv_in(own, f, T):
                dve.wait_ge(on.zin_kept, f + 1)
                dve.wait_ge(on.w_used, f * PIECES + 7)
                v.tensor_tensor(z_ext[:, :, 2:2 + P] if T == P else z_s[:, :, 2, :], split(F[4][:, 0:4 * T], 4),
                                split(W[0][:, 0:4 * T], 4), ALU.mult).then_inc(on.z_kept, 1)
                dve.wait_ge(on.z_kept, f + 1)

            def conv(own, f, T):
                steps = [z_ext[:, :, k:k + P] for k in range(3)] if T == P else [z_s[:, :, k, :] for k in range(3)]
                y, t = split(W[3][:, 0:4 * T], 4), split(W[2][:, 0:4 * T], 4)
                own(v.tensor_tensor(y, steps[0], spread_cols(ROW_CONV, 4, T), ALU.mult))
                for k in (1, 2):
                    own(v.tensor_tensor(t, steps[k], spread_cols(ROW_CONV + 4 * k, 4, T), ALU.mult))
                    own(v.tensor_tensor(y, y, t, ALU.add))
                dve.wait_ge(on.zb_kept, f + 1)
                v.tensor_tensor(split(mix_raw[:, 4 * T:8 * T], 4), y, zb[:, :, 0:T], ALU.mult).then_inc(on.conv_done, 1)
                dve.wait_ge(on.conv_done, f + 1)
                if T == P:
                    own(v.tensor_copy(z_ext[:, :, 0:2], z_ext[:, :, P:P + 2]))

            def q_rope(own, f, T):
                dve.wait_ge(on.q_kept, f + 1)
                raw = split(W[4][0:ROPE, 512:512 + 4 * T], 4)
                t = split(W[2][0:ROPE, 0:4 * T], 4)
                c4 = cos_t[:, 0:T].unsqueeze(1).to_broadcast([ROPE, H, T])
                s4 = sin_t[:, 0:T].unsqueeze(1).to_broadcast([ROPE, H, T])
                own(v.tensor_tensor(q_ro[:, :, 0:T], raw, c4, ALU.mult))
                dve.wait_ge(on.qr_rotated, f + 1)
                own(v.tensor_tensor(t, split(F[2][0:ROPE, 0:4 * T], 4), s4, ALU.mult))
                v.tensor_tensor(q_ro[:, :, 0:T], q_ro[:, :, 0:T], t, ALU.add).then_inc(on.q_roped, 1)

            def head_start(own, f, h):
                n = f * H + h
                if h == 0:
                    own(v.tensor_copy(small_col(C_LIM), q_limit[:, bass.ds(f, 1)]))
                    own(v.tensor_scalar(small_col(C_LIM + 1), small_col(C_LIM), -512 * BIG, None, ALU.add))
                dve.wait_ge(on.scores_made, n + 1)
                for half in range(2):
                    last = v.scalar_tensor_tensor(out=W[0][:, half * 512:half * 512 + 512], in0=low_keys[:],
                                                  scalar=small_col(C_LIM + half), in1=F[half][:, :], op0=ALU.add, op1=ALU.min)
                last.then_inc(on.scores_masked, 1)
                dve.wait_ge(on.scores_masked, n + 1)
                own(v.tensor_reduce(small_col(C_MAX), W[0], AX.X, ALU.max))
                v.tensor_scalar(small_col(C_NMAX), small_col(C_MAX), -SCALE, None, ALU.mult).then_inc(on.max_made, 1)
                dve.wait_ge(on.exp_made, n + 1)
                own(v.reciprocal(small_col(C_RL), small_col(C_L)))
                v.tensor_scalar(W[0], W[0], small_col(C_RL), None, ALU.mult).then_inc(on.probs_made, 1)

            def head_end(own, f, h):
                n = f * H + h
                dve.wait_ge(on.probs_turned_a, n + 1)
                v.tensor_copy(W[1][:, 0:512], F[2][:, :]).then_inc(on.probs_kept_a, 1)

            def sample_keys(own, b, part):
                if b == 0 and part == 0:
                    dve.wait_ge(on.s_new_made, 1)
                    v.tensor_copy(s_new[:], F[5][0:SB, 0:4 * SB]).then_inc(on.s_new_kept, 1)
                for q in (2 * part, 2 * part + 1):
                    dve.wait_ge(on.page_turned, 4 * b + q + 1)
                    v.tensor_copy(pages_T[:, 1, :], F[1][:, :])
                    v.tensor_copy(pages_T[0:ROPE, 2, :], F[2][0:ROPE, :]).then_inc(on.page_kept, 1)
                if part == 1:
                    dve.wait_ge(on.page_scores_made, 4 * (b + 1))
                    v.tensor_copy(page_s[:, 0:4 * NPAGES], F[3][:, 0:4 * NPAGES]).then_inc(on.page_scores_kept, 1)

            def sample_attend(own, b):
                own(v.memset(page_s[:, 4 * NPAGES:], -BIG))
                own(v.tensor_scalar(page_s[0:SB, 4 * NPAGES:], s_new[:, b:4 * SB:SB], own_row[:, b:b + 1], None, ALU.add))
                dve.wait_ge(on.page_scores_kept, b + 1)
                v.tensor_reduce(small_col(C_PM, 4), page_s[:].rearrange("p (n h) -> p h n", h=H), AX.X, ALU.max)\
                    .then_inc(on.page_max_made, 1)
                dve.wait_ge(on.page_gmax, b + 1)
                own(v.tensor_reduce(small_col(C_GM, 1, H), F[4][0:H, 0:P], AX.X, ALU.max))
                v.tensor_scalar(gm_rows[:], ones[0:H, :], small_col(C_GM, 1, H), None, ALU.mult).then_inc(on.page_max_made, 1)
                dve.wait_ge(on.page_gmax_spread, b + 1)
                s3 = page_s[:].rearrange("p (n h) -> p n h", h=H)
                v.tensor_tensor(s3, s3, F[4][:, 128:132].unsqueeze(1).to_broadcast([P, NPAGES + 1, H]), ALU.subtract)\
                    .then_inc(on.page_shifted, 1)
                dve.wait_ge(on.page_exp, b + 1)
                v.tensor_reduce(small_col(C_PL, 4), page_p[:].rearrange("p (n h) -> p h n", h=H), AX.X, ALU.add)\
                    .then_inc(on.page_sums, 1)
                dve.wait_ge(on.page_lsum, b + 1)
                own(v.reciprocal(small_col(C_PLS, 4), F[4][:, 132:136]))
                p3 = page_p[:].rearrange("p (n h) -> p n h", h=H)
                v.tensor_tensor(p3, p3, small_col(C_PLS, 4).unsqueeze(1).to_broadcast([P, NPAGES + 1, H]), ALU.mult)\
                    .then_inc(on.page_probs, 1)

            def attn_out(own, f, T):
                dve.wait_ge(on.attn_kept, f + 1)
                v.tensor_tensor(W[0][:, 0:8 * T], mix_raw[:, 0:8 * T], mix_raw[:, 0:8 * T], ALU.mult).then_inc(on.mix_squared, 1)
                dve.wait_ge(on.mix_summed, f + 1)
                for half in range(2):
                    last = mean(W[0][:, half * 4 * T:(half + 1) * 4 * T], F[half][:, 0:4 * T], P)
                last.then_inc(on.mix_ms, 1)
                dve.wait_ge(on.mix_ms, f + 1)
                dve.wait_ge(on.mix_rs, f + 1)
                sharpen(own, W[0][:, 0:8 * T], W[1][:, 0:8 * T], W[2][:, 0:8 * T])
                own(v.tensor_tensor(W[2][:, 0:8 * T], mix_raw[:, 0:8 * T], W[1][:, 0:8 * T], ALU.mult))
                v.tensor_tensor(split(W[2][:, 0:8 * T], 8), split(W[2][:, 0:8 * T], 8), spread_cols(ROW_GOUT, 8, T), ALU.mult)\
                    .then_inc(on.mix_normed, 1)

            def mix_out(own, f, T):
                dve.wait_ge(on.w_used, f * PIECES + N_IN + N_OUT)
                after(dve, on.residual_in, f)
                for half in range(2):
                    cols = slice(half * 512, half * 512 + 512)
                    last = v.tensor_tensor(x1_next[0:T, cols], F[2 + half][0:T, :], x_t[0:T, cols], ALU.add)
                last.then_inc(on.x1_kept, 1)
                dve.wait_ge(on.x1_kept, f + 1)

            def ffn_norm(own, f, T):
                x1, xn = x1_next[0:T, :], xn2_next[0:T, :]
                own(v.tensor_tensor_reduce(W[0][0:T, :], x1, x1, 1.0, 0.0, ALU.mult, ALU.add, small_col(C_SS2, 1, T)))
                mean(small_col(C_MS2, 1, T), small_col(C_SS2, 1, T), D).then_inc(on.ffn_ms, 1)
                dve.wait_ge(on.ffn_rs, f + 1)
                sharpen(own, small_col(C_MS2, 1, T), small_col(C_Y2, 1, T), small_col(C_T2, 1, T))
                v.scalar_tensor_tensor(out=xn, in0=x1, scalar=small_col(C_Y2, 1, T), in1=g_ffn[0:T, :], op0=ALU.mult,
                                       op1=ALU.mult).then_inc(on.xn2_made, 1)
                dve.wait_ge(on.xn2_turned, f + 1)
                for half in range(2):
                    last = v.tensor_copy(W[4][:, half * 4 * T:(half + 1) * 4 * T], F[4 + half][:, 0:4 * T])
                last.then_inc(on.xn2_kept, 1)

            def top16(own, values, scores, index):
                for r in range(2):
                    best = values[:, 8 * r:8 * r + 8]
                    own(v.max(best, scores), held=True)
                    last = v.max_index(index[:, 8 * r:8 * r + 8], best, scores)
                    if r == 0:
                        own(v.match_replace(scores, best, scores, LOW), held=True)
                return last

            def query(own, f, T, h):
                dve.wait_ge(on.key_scores_kept, f * PH + h + 1)
                waited(dve)
                for c in range(2):
                    last = top16(own, sv[0:T, h, c, :], keys_s[0:T, c, :], si_u[0:T, h, c, :])
                last.then_inc(on.top_keys_done, 1)
                dve.wait_ge(on.top_keys_done, f * PH + h + 1)

            def select(own, f, T):
                grid = [T, PH, TOPK, TOPK]
                pairs = cand[0:T, :].rearrange("p (h a b) -> p h a b", h=PH, a=TOPK)
                own(v.tensor_copy(si[0:T], si_u[0:T]))
                own(v.tensor_tensor(pairs, sv[0:T, :, 0, :].unsqueeze(3).to_broadcast(grid),
                                    sv[0:T, :, 1, :].unsqueeze(2).to_broadcast(grid), ALU.add), held=True)
                for h in range(PH):
                    own(held=True, ins=top16(own, top_s[0:T, h, :], cand[0:T, h * 256:(h + 1) * 256], pos_u[0:T, h, :]))
                gates = gate_next[0:T, :].rearrange("p (h k) -> p h k", h=PH)
                v.tensor_tensor(gates, top_s[0:T], top_s[0:T, :, 0:1].to_broadcast([T, PH, TOPK]), ALU.subtract)\
                    .then_inc(on.gate_max_made, 1)
                own(v.tensor_scalar(pos_ab[0:T, 0], pos_u[0:T], 4, None, ALU.logical_shift_right))
                own(v.tensor_scalar(pos_ab[0:T, 1], pos_u[0:T], TOPK - 1, None, ALU.bitwise_and))
                own(v.tensor_copy(pos_f[0:T], pos_ab[0:T]))
                hit = work[0:T, 0:2 * D].rearrange("p (h k a) -> p h k a", h=PH, k=TOPK)
                for c in range(2):
                    own(v.tensor_tensor(hit, pos_f[0:T, c].unsqueeze(3).to_broadcast(grid),
                                        iota16[0:T].unsqueeze(1).unsqueeze(1).to_broadcast(grid), ALU.is_equal))
                    own(v.tensor_tensor(hit, hit, si[0:T, :, c, :].unsqueeze(2).to_broadcast(grid), ALU.mult))
                    own(v.tensor_reduce(picked_ab[0:T, c], hit, AX.X, ALU.add))
                dve.wait_ge(on.gate_exp_made, f + 1)
                total = small_col(C_GS, PH, T)
                own(v.tensor_reduce(total, gates, AX.X, ALU.add))
                own(v.reciprocal(small_col(C_GR, PH, T), total))
                own(v.tensor_tensor(gates, gates, small_col(C_GR, PH, T).unsqueeze(2).to_broadcast([T, PH, TOPK]), ALU.mult))
                dst = pick_next[0:T, :].rearrange("p (h k) -> p h k", h=PH) if T == P else picked_ab[0:T, 0]
                v.scalar_tensor_tensor(out=dst, in0=picked_ab[0:T, 0], scalar=float(KEYS), in1=picked_ab[0:T, 1],
                                       op0=ALU.mult, op1=ALU.add).then_inc(on.picked, 1)
                dve.wait_ge(on.picked, f + 1)

            def piece(own, f, T, i):
                if i == 0:
                    norm_in(own, f, T)
                elif i == 1:
                    latents(own, f, T)
                elif i == 3:
                    conv_in(own, f, T)
                elif i == 4:
                    conv(own, f, T)
                elif i == 6:
                    q_rope(own, f, T)
                elif T == P and 7 <= i < 7 + HEAD_PIECES:
                    if i > 7:
                        head_end(own, f, i - 8)
                    if i < 7 + H:
                        head_start(own, f, i - 7)
                elif T != P and 7 <= i < 7 + SAMPLE_PIECES:
                    b, part = divmod(i - 7, 3)
                    if part < 2:
                        sample_keys(own, b, part)
                    else:
                        sample_attend(own, b)
                elif i >= 7:
                    i -= 7 + (HEAD_PIECES if T == P else SAMPLE_PIECES)
                    if i == 0:
                        attn_out(own, f, T)
                    elif i == 1:
                        mix_out(own, f, T)
                    elif i == 2:
                        ffn_norm(own, f, T)
                    elif i < 3 + QUERY_PIECES:
                        if i > 3:
                            query(own, f, T, i - 4)
                    else:
                        select(own, f, T)

            def dot_group(it, g):
                for r in range(G):
                    slot = (g % 2) * G + r
                    dve.wait_ge(u_loaded[slot], (it * (GROUPS // 2) + g // 2 + 1) * 16)
                    v.tensor_tensor_reduce(u_ring[:, slot, :], u_ring[:, slot, :], xn2_cur[:], 1.0, 0.0, ALU.mult, ALU.add,
                                           dots[:, g * G + r:g * G + r + 1]).then_inc(on.u_free, 1)

            def weigh_group(it, g):
                dve.wait_ge(on.gelu_done, it * GROUPS + g + 1)
                s = slice(g * G, (g + 1) * G)
                v.tensor_tensor(wgt[:, s], gelu[:, s], gate_cur[:, s], ALU.mult).then_inc(on.w_made, 1)

            def move_on(own, f):
                after(dve, on.v_free, f * SLOTS + RING if not isinstance(f, int) or f else 0)
                v.tensor_copy(pick_cur[:], pick_next[:]).then_inc(on.picked_moved, 1)
                v.tensor_copy(gate_cur[:], gate_next[:])
                own(v.tensor_copy(xn2_cur[:], xn2_next))

            def finalize(own, it, T):
                total = acc[0:T].rearrange("p a n -> p (a n)")
                dve.wait_ge(on.y_stored, (it + 1) * 16)
                own(v.tensor_copy(y_t[0:T, :], total))
                v.tensor_tensor_reduce(total, total, y_t[0:T, :], 1.0, 0.0, ALU.mult, ALU.add, small_col(C_SS3, 1, T))\
                    .then_inc(on.acc_free, 1)
                dve.wait_ge(on.acc_free, it + 1)
                mean(small_col(C_MS3, 1, T), small_col(C_SS3, 1, T), D).then_inc(on.y_ms, 1)
                dve.wait_ge(on.y_ms, it + 1)
                dve.wait_ge(on.y_rs, it + 1)
                sharpen(own, small_col(C_MS3, 1, T), small_col(C_Y3, 1, T), small_col(C_T3, 1, T))
                v.scalar_tensor_tensor(out=y_t[0:T, :], in0=y_t[0:T, :], scalar=small_col(C_Y3, 1, T), in1=g_fin[0:T, :],
                                       op0=ALU.mult, op1=ALU.mult).then_inc(on.y_made, 1)

            def tile(it, T):
                own = Own(dve, on.dve_front, (it + 1) * DVE_FRONT)
                for g in range(GROUPS):
                    dot_group(it, g)
                    weigh_group(it, g)
                    for i in schedule(g, PIECES_PROMPT if T == P else PIECES_SAMPLE):
                        piece(own, it + 1, T, i)
                if T == P:
                    own.check(DVE_FRONT)
                own2 = Own(dve, on.dve_peer, it * DVE_PEER + 1)
                if T == P:
                    move_on(own2, it + 1)
                else:
                    dve.wait_ge(on.v_free, TILES * SLOTS + RING)
                finalize(own2, it, P)
                if T == P:
                    own2.check(DVE_PEER)

            own = Own(dve, on.dve_setup, 0)
            own(v.memset(z_ext[:, :, 0:2], 0.0))
            v.memset(s_fan[:], 0.0).then_inc(on.u_free, RING)
            v.memset(gelu[:], 0.0).then_inc(on.v_free, RING)
            v.memset(dots[:], 0.0).then_inc(on.y_stored, 16)
            dve.wait_ge(on.consts_ready, 6 * 16)
            dve.wait_ge(on.vec_turned, 1)
            own(v.tensor_copy(vec_cols[:], F[0][:, 0:VEC_ROWS]))
            dve.wait_ge(on.uk_turned, 1)
            for h in range(H):
                own(v.tensor_copy(w_ukT[:, h, :], F[1 + h // 2][:, (h % 2) * KV:(h % 2 + 1) * KV]))
            dve.wait_ge(on.sub_turned, 1)
            own(v.tensor_copy(sub_keysT[:].rearrange("p c k -> p (c k)"), F[3][:, 0:2 * KEYS]))
            dve.wait_ge(on.state_turned, 1)
            for k in range(2):
                own(v.tensor_copy(z_s[:, :, k, :], F[4][:, 0:8 * SB].rearrange("p (c b k) -> p c b k", c=4, k=2)[:, :, :, k]))
            dve.wait_ge(on.gains_loaded, 3 * 16)
            own = Own(dve, on.dve_front, 0)
            for i in range(PIECES_PROMPT):
                piece(own, 0, P, i)
            own.check(DVE_FRONT)
            move_on(Own(dve, on.dve_peer, 0), 0)
            with dve.Fori(0, TILES - 1) as it:
                tile(it, P)
            tile(TILES - 1, SB)
            own = Own(dve, on.dve_tail, 0)
            dve.wait_ge(on.s_turned, 1)
            v.tensor_copy(s_pick[:], F[0][:, 0:SB]).then_inc(on.s_slots, 1)
            own(v.tensor_copy(wgt[:, 0:SB], F[0][:, SB:2 * SB]))
            dve.wait_ge(on.srow_loaded, SB * 16)
            for t in range(SB):
                dve.wait_ge(u_loaded[t], (TILES * (GROUPS // 2) + 1) * 16)
                v.tensor_tensor_reduce(u_ring[:, t, :], u_ring[:, t, :], SPREAD[t], 1.0, 0.0, ALU.mult, ALU.add,
                                       dots[:, t:t + 1]).then_inc(on.s_dots, 1)
            dve.wait_ge(on.s_gelu, 1)
            v.tensor_tensor(s_fan[:].rearrange("p a b -> p (a b)")[:, 0:SB * SB:SB + 1], gelu[:, 0:SB], wgt[:, 0:SB], ALU.mult)\
                .then_inc(on.s_weights, 1)
            dve.wait_ge(on.v_free, TILES * SLOTS + RING + 1)
            finalize(own, TILES, SB)

        @block.gpsimd
        def _(pool):
            pool.memset(ckv_rows[:], 0.0).then_inc(on.zeroed, 1)
            pool.memset(ckvT[:], 0.0).then_inc(on.zeroed, 1)
            pool.memset(krT[:], 0.0).then_inc(on.zeroed, 1)

            def gather(table, ring, slot, loaded, pick):
                pool.indirect_dma_start(ring[:, slot, :], None, a[table][0],
                                        bass.IndirectOffsetOnAxis(ap=pick, axis=0)).then_inc(loaded[slot], 16)

            with pool.Fori(0, TILES) as it:
                pool.wait_ge(on.picked_moved, it + 1)
                for g in range(GROUPS):
                    pool.wait_ge(on.u_free, it * SLOTS + (g + 1) * G)
                    waited(pool)
                    for r in range(G):
                        s = g * G + r
                        gather("expert_u", u_ring, s % RING, u_loaded, pick_cur[:, s:s + 1])
                    pool.wait_ge(on.v_free, it * SLOTS + (g + 1) * G)
                    waited(pool)
                    for r in range(G):
                        s = g * G + r
                        gather("expert_v", v_ring, s % RING, v_loaded, pick_cur[:, s:s + 1])
            pool.wait_ge(on.s_slots, 1)
            pool.wait_ge(on.u_free, TILES * SLOTS + RING)
            pool.wait_ge(on.v_free, TILES * SLOTS + RING)
            for t in range(SB):
                gather("expert_u", u_ring, t, u_loaded, s_pick[:, t:t + 1])
            for t in range(SB):
                gather("expert_v", v_ring, t, v_loaded, s_pick[:, t:t + 1])


IN_NAMES = ["x_prompt", "x_sample", "cache_ckv", "cache_krope", "state_conv", "page_table", "g_mix_norm", "w_in", "g_q",
            "w_uq", "g_kv", "w_uk", "w_uv", "conv_w", "g_attn_out", "g_conv_out", "w_o", "g_ffn_norm", "w_query",
            "sub_keys", "expert_u", "expert_v", "g_final"]
OUT_SHAPES = {"y_prompt": (1, SEQ, D), "y_sample": (SB, 1, D), "new_ckv_prompt": (1, 1, SEQ, KV),
              "new_krope_prompt": (1, 1, SEQ, ROPE), "new_conv_prompt": (1, 1, 2, CW), "new_ckv_sample": (1, SB, 1, KV),
              "new_krope_sample": (1, SB, 1, ROPE), "new_conv_sample": (1, SB, 2, CW)}


def constants():
    import numpy as np

    f32 = np.float32
    rot = np.zeros((ROPE, ROPE), f32)
    for p in range(ROPE // 2):
        rot[p + ROPE // 2, p] = -1.0
        rot[p, p + ROPE // 2] = 1.0
    inv = (f32(10000.0) ** (-np.arange(0, ROPE, 2, dtype=f32) / f32(ROPE))).astype(f32)
    pos = np.concatenate([np.arange(SEQ), np.full(SB, PAST)]).astype(f32)
    ang = (pos[:, None] * inv[None, :]).astype(f32)
    table = np.stack([np.concatenate([t, t], axis=1).T for t in (np.cos(ang), np.sin(ang))])
    own = np.full((SB, SB), -BIG, f32)
    np.fill_diagonal(own, 0.0)
    return {
        "c_ident": np.eye(P, dtype=f32), "c_ones": np.ones((P, P), f32), "c_rot": rot,
        "c_limit": ((np.arange(TILES)[None, :] * P + np.arange(P)[:, None] + 0.5) * BIG).astype(f32),
        "c_iota16": np.tile(np.arange(TOPK, dtype=f32), (P, 1)), "c_own": own,
        "c_rope": np.ascontiguousarray(table.astype(f32)), "c_low": (-np.arange(512) * BIG).astype(f32),
    }


def kernel(**inputs):
    import numpy as np
    import concourse.bacc as bacc
    from concourse.bass_utils import run_bass_kernel_spmd

    nc = bacc.Bacc("TRN2", target_bir_lowering=False, num_devices=1)
    arrays = {n: np.ascontiguousarray(inputs[n]) for n in IN_NAMES}
    arrays.update(constants())
    a = {n: nc.dram_tensor(f"in_{n}", x.shape, mybir.dt.from_np(x.dtype), kind="ExternalInput").ap() for n, x in arrays.items()}
    a["scratch"] = nc.dram_tensor("scratch", (SB, D), F32, kind="Internal").ap()
    out = {n: nc.dram_tensor(f"out_{n}", s, F32, kind="ExternalOutput").ap() for n, s in OUT_SHAPES.items()}
    build(nc, a, out)
    r = run_bass_kernel_spmd(nc, [{f"in_{n}": x for n, x in arrays.items()}], core_ids=[0])
    return tuple(r.results[0][f"out_{n}"] for n in OUT_SHAPES)
```

```python
from collections import namedtuple
from contextlib import ExitStack

import concourse.bass as bass
from concourse import mybir

F32 = mybir.dt.float32
U32 = mybir.dt.uint32
I32 = mybir.dt.int32
ALU = mybir.AluOpType
ACT = mybir.ActivationFunctionType
AX = mybir.AxisListType

P = 128
D = 1024
DC = D // P
SEQ = 1024
TILES = SEQ // P
SB = 8
PAGE = 128
NPAGES = 16
PAST = NPAGES * PAGE
H = 4
NOPE = 128
ROPE = 64
QR = 384
KV = 256
CW = 512
D_IN = QR + KV + ROPE + 3 * CW
PH = 8
KEYS = 128
TOPK = 16
SLOTS = PH * TOPK
EPS = 1e-6
SCALE = float(NOPE + ROPE) ** -0.5
BIG = 1e30
LOW = -3.0e38

PW = 256
IN_COLS = [(0, 256), (256, 256), (512, 192)] + [(704 + 256 * k, 256) for k in range(6)]
OUT_COLS = [(256 * k, 256) for k in range(4)]
QUERY_COLS = [(256 * k, 256) for k in range(PH)]
WR = 3
N_IN, N_OUT, N_QUERY = len(IN_COLS), len(OUT_COLS), len(QUERY_COLS)
PIECES = N_IN + N_OUT + N_QUERY
assert PIECES % WR == 0

G = 4
GROUPS = SLOTS // G
RING = 2 * G

QUARTERS = 4
QP = NPAGES // QUARTERS
_FIRST = ["norm", "turn", "latent", "latent_norm", "kv_rows", "z_in", "z_gate", "conv", "q_proj", "q_latent"]
_LAST = (["attn", "mix_norm", "mix_out", "ffn_norm", "ffn_turn"] + [("query", h) for h in range(PH + 1)]
         + [("select", c) for c in range(2)])
STAGES_PROMPT = _FIRST + [("head", h) for h in range(H + 1)] + _LAST
STAGES_SAMPLE = _FIRST + [("pages", n) for n in range(SB * QUARTERS + 3)] + _LAST


def stages_of(T):
    return [s if isinstance(s, tuple) else (s, 0) for s in (STAGES_PROMPT if T == P else STAGES_SAMPLE)]


def beside(g, T):
    stages = stages_of(T)
    span = GROUPS - 2 if T == P else GROUPS - 1
    return [s for i, s in enumerate(stages) if i * span // len(stages) == g]


DVE_FRONT, DVE_PEER, ACT_FRONT, ACT_PEER = 136, 5, 5, 1

ROW_GMIX, ROW_GQ, ROW_GKV, ROW_GOUT, ROW_CONV, VEC_ROWS = 0, 8, 11, 13, 21, 33

EVENTS = """
vec_loaded consts_ready uk_loaded sub_loaded uq_loaded uv_loaded gains_loaded pages_table_loaded vec_turned
uk_turned sub_turned zeroed state_loaded state_turned x_loaded rope_loaded w_used in_ms in_rs x_scaled
x_turned xn_kept lat_kept lat_squared lat_summed lat_ms lat_rs cq_normed kv_normed kr_rotated kr_roped
kv_turned kv_rows_kept kv_cols_kept kv_stored zin_kept z_kept zb_kept conv_done q_projected q_kept qr_rotated
q_roped qlat_projected qlat_kept scores_made scores_masked max_made exp_made probs_made probs_turned_a
probs_turned_b probs_kept_a probs_kept_b pv_made olat_kept attn_projected attn_kept mix_squared mix_summed
mix_ms mix_rs mix_normed x1_kept ffn_ms ffn_rs xn2_made xn2_turned xn2_kept pq_kept key_scores_made
key_scores_kept top_keys_done gate_max_made gate_exp_made picked picked_moved picks_moved u_free v_free
gelu_done w_made diag_made residual_in y_ms y_rs y_made y_stored acc_free z_tail_turned z_tail_kept
conv_stored s_new_made s_new_kept page_turned page_kept page_scores_made page_scores_kept page_max_made
page_gmax page_gmax_spread page_shifted page_exp page_pv srow_stored srow_loaded s_turned s_slots s_dots
s_gelu s_weights dve_front dve_peer act_front act_peer dve_setup dve_tail
""".split()


def build(nc, a, out):
    with ExitStack() as ctx:
        def sb(name, shape, dt=F32):
            return ctx.enter_context(nc.sbuf_tensor(name, shape, dt))

        on = namedtuple("Events", EVENTS)(*[ctx.enter_context(nc.semaphore(n)) for n in EVENTS])
        w_loaded = [ctx.enter_context(nc.semaphore(f"w_loaded{r}")) for r in range(WR)]
        u_loaded = [ctx.enter_context(nc.semaphore(f"u_loaded{r}")) for r in range(RING)]
        v_loaded = [ctx.enter_context(nc.semaphore(f"v_loaded{r}")) for r in range(RING)]
        pages_loaded = [[ctx.enter_context(nc.semaphore(f"pages_loaded{i}{q}")) for q in range(QUARTERS)] for i in range(2)]

        acc = ctx.enter_context(nc.psum_tensor("acc", [P, 2, 512], F32))
        F = [ctx.enter_context(nc.psum_tensor(f"front{i}", [P, 512], F32)) for i in range(6)]

        ident = sb("ident", [P, P])
        ones = sb("ones", [P, P])
        rot = sb("rot", [ROPE, ROPE])
        low_keys = sb("low_keys", [P, 512])
        q_limit = sb("q_limit", [P, TILES])
        iota16 = sb("iota16", [P, TOPK])
        own_row = sb("own_row", [SB, SB])
        vec_cols = sb("vec_cols", [P, VEC_ROWS])
        g_ffn = sb("g_ffn", [P, D])
        g_fin = sb("g_fin", [P, D])
        w_uq = sb("w_uq", [P, QR // P, H, NOPE + ROPE])
        w_ukT = sb("w_ukT", [P, H, KV])
        w_uv = sb("w_uv", [P, KV // P, H, P])
        sub_keysT = sb("sub_keysT", [P, 2, KEYS])
        w_ring = sb("w_ring", [P, WR, DC, PW])
        ckv_rows = sb("ckv_rows", [P, TILES, KV])
        ckvT = sb("ckvT", [P, 2, SEQ])
        krT = sb("krT", [ROPE, SEQ])
        u_ring = sb("u_ring", [P, RING, D])
        v_ring = sb("v_ring", [P, RING, D])
        diag = sb("diag", [P, RING, P])
        pick_cur = sb("pick_cur", [P, SLOTS], U32)
        pick_next = sb("pick_next", [P, SLOTS], U32)
        gate_cur = sb("gate_cur", [P, SLOTS])
        gate_next = sb("gate_next", [P, SLOTS])
        dots = sb("dots", [P, SLOTS])
        gelu = sb("gelu", [P, SLOTS])
        wgt = sb("wgt", [P, SLOTS])
        xn2_cur = sb("xn2_cur", [P, D])
        rows_next = sb("rows_next", [P, 2, D])
        mo = sb("mo", [P, 2, D])
        x_t = sb("x_t", [P, D])
        work = sb("work", [P, 5 * D])
        cos_t = sb("cos_t", [ROPE, P])
        sin_t = sb("sin_t", [ROPE, P])
        z_ext = sb("z_ext", [P, 4, P + 2])
        z_s = sb("z_s", [P, 4, 3, SB])
        q_ro = sb("q_ro", [ROPE, H, P])
        kr_t = sb("kr_t", [ROPE, 3, P])
        ck_t = sb("ck_t", [P, 2, P])
        kv_rows_t = sb("kv_rows_t", [P, KV + ROPE])
        small = sb("small", [P, 96])
        sv = sb("sv", [P, PH, 2, TOPK])
        si_u = sb("si_u", [P, PH, 2, TOPK], U32)
        si = sb("si", [P, PH, 2, TOPK])
        s_new = sb("s_new", [SB, H * SB])
        page_s = sb("page_s", [P, 4 * (NPAGES + 1)])
        page_p = sb("page_p", [P, 4 * (NPAGES + 1)])
        gm_rows = sb("gm_rows", [H, P])
        s_pick = sb("s_pick", [P, SB], U32)
        s_fan = sb("s_fan", [P, SB, SB])
        page_table_sb = sb("page_table_sb", [1, SB * NPAGES], I32)
        picked_ab = sb("picked_ab", [P, 2, PH, TOPK])

        W = [work[:, k * D:(k + 1) * D] for k in range(5)]
        y_t = W[3]
        zb = W[0][:, 512:1024].rearrange("p (c t) -> p c t", c=4)
        keys_s = W[2][:, 0:2 * KEYS].rearrange("p (c k) -> p c k", c=2)
        pos_f = W[4][:, 0:2 * SLOTS].rearrange("p (c h k) -> p c h k", c=2, h=PH)
        pos_ab = W[4][:, 2 * SLOTS:4 * SLOTS].bitcast(U32).rearrange("p (c h k) -> p c h k", c=2, h=PH)
        top_s = W[3][:, 2 * SLOTS:3 * SLOTS].rearrange("p (h k) -> p h k", h=PH)
        pos_u = W[3][:, 3 * SLOTS:4 * SLOTS].bitcast(U32).rearrange("p (h k) -> p h k", h=PH)
        x1_next, xn2_next = rows_next[:, 0, :], rows_next[:, 1, :]
        mix_raw, o_lat = mo[:, 0, :], mo[:, 1, :]
        cand = mo[:, :, :].rearrange("p a b -> p (a b)")
        prompt_keys = [ckv_rows[:, :, :], ckvT[:, :, :].rearrange("p c (n r) -> p (c n) r", r=KV)]
        pages_kr = [w_ukT[:, :, :].rearrange("p h (n r) -> p (h n) r", r=ROPE),
                    work[:, NPAGES * KV:NPAGES * (KV + ROPE)].rearrange("p (n r) -> p n r", r=ROPE)]

        def page_rows(b, n):
            if b % 2:
                return work[:, n * KV:(n + 1) * KV]
            return prompt_keys[n // TILES][:, n % TILES, :]

        pages_T = rows_next[:, :, :].rearrange("p a b -> p (a b)")[:, 0:3 * 512].rearrange("p (c k) -> p c k", c=3)

        SPREAD = [W[0], W[1], W[2], xn2_cur[:, :], W[4], mix_raw, o_lat, x_t[:, :]]

        all_rows = rows_next[:, :, :].rearrange("p a b -> p (a b)")
        q_lat = all_rows[:, D:2 * D].rearrange("p (c h t) -> p c h t", c=2, h=H)
        q_lat_s = all_rows[:, 3 * 512:3 * 512 + 2 * H * SB].rearrange("p (c h t) -> p c h t", c=2, h=H)

        def small_col(n, w=1, rows=P):
            return small[0:rows, n:n + w]

        (C_SS, C_MS, C_Y, C_T, C_SS2, C_MS2, C_Y2, C_T2, C_SS3, C_MS3, C_Y3, C_T3, C_MAX, C_NMAX,
         C_L, C_RL) = range(16)
        C_PM, C_GM, C_PL, C_PLS, C_LIM = 16, 20, 24, 28, 32
        C_GS, C_GR = 40, 48

        def b3(ap, shape):
            return ap.to_broadcast(shape)

        def after(eng, sem, value):
            if isinstance(value, int) and value <= 0:
                return
            eng.wait_ge(sem, value)


        def waited(eng):
            eng.nop(nofuse=True)

        class Own:

            def __init__(self, eng, sem, base):
                self.eng, self.sem, self.base, self.n = eng, sem, base, 0

            def __call__(self, ins, held=False):
                self.n += 1
                ins.then_inc(self.sem, 1)
                self.eng.wait_ge(self.sem, self.base + self.n)
                if held:
                    waited(self.eng)

            def check(self, count):
                assert self.n == count, (self.sem, self.n, count)

        block = ctx.enter_context(nc.Block())

        @block.sync
        def _(sp):
            for dst, src in ((ident, a["c_ident"]), (ones, a["c_ones"]), (rot, a["c_rot"]), (q_limit, a["c_limit"]),
                             (iota16, a["c_iota16"]), (own_row, a["c_own"])):
                sp.dma_start(dst[:], src).then_inc(on.consts_ready, 16)
            r = 0
            for name in ("g_mix_norm", "g_q", "g_kv", "g_attn_out", "g_conv_out"):
                n = a[name].shape[1] // P
                sp.dma_start(W[0][r:r + n, 0:P], a[name].rearrange("l (c p) -> (l c) p", p=P)).then_inc(on.vec_loaded, 16)
                r += n
            sp.dma_start(W[0][r:r + 12, 0:P], a["conv_w"].rearrange("l k (c p) -> (l k c) p", p=P)).then_inc(on.vec_loaded, 16)
            assert r + 12 == VEC_ROWS

            def load_x(f, T, row=0):
                after(sp, on.x1_kept, f)
                waited(sp)
                src = a["x_prompt"][0, bass.ds(row, P), :] if T == P else a["x_sample"].rearrange("b s d -> (b s) d")
                sp.dma_start(x_t[0:T, :], src).then_inc(on.x_loaded, 16)

            def load_rope(f, T, row=0):
                after(sp, on.q_roped, f)
                waited(sp)
                sp.dma_start(cos_t[:, 0:T], a["c_rope"][0, :, bass.ds(row, T)]).then_inc(on.rope_loaded, 16)
                sp.dma_start(sin_t[:, 0:T], a["c_rope"][1, :, bass.ds(row, T)]).then_inc(on.rope_loaded, 16)

            w_src = ([(a["w_in"], c) for c in IN_COLS] + [(a["w_o"], c) for c in OUT_COLS]
                     + [(a["w_query"], c) for c in QUERY_COLS])

            def load_w(f, k):
                after(sp, on.w_used, f * PIECES + k - WR + 1)
                src, (c0, n) = w_src[k]
                sp.dma_start(w_ring[:, k % WR, :, 0:n],
                             src[0].rearrange("(c p) n -> p c n", p=P)[:, :, c0:c0 + n]).then_inc(w_loaded[k % WR], 16)

            def load_tile(f, T):
                row = sp.snap(f * P)
                load_x(f, T, row)
                for k in range(PIECES):
                    load_w(f, k)
                    if k == 2:
                        load_rope(f, T, row)

            load_x(0, P)
            for k in range(WR):
                load_w(0, k)
            sp.dma_start(page_table_sb[:], a["page_table"].rearrange("b n -> (b n)").unsqueeze(0)).then_inc(on.pages_table_loaded, 16)
            sp.dma_start(work[0:2 * SB, 4 * D:4 * D + CW], a["state_conv"].rearrange("l b k c -> (l b k) c"))\
                .then_inc(on.state_loaded, 16)
            sp.dma_start(out["new_conv_sample"][0, :, 0, :], a["state_conv"][0, :, 1, :]).then_inc(on.conv_stored, 16)
            load_rope(0, P)
            sp.dma_start(w_uq[:], a["w_uq"][0].rearrange("(c p) h n -> p c h n", p=P)).then_inc(on.uq_loaded, 16)
            sp.dma_start(work[:, 2 * D:3 * D].rearrange("p (c n) -> p c n", c=2),
                         a["w_uk"][0].rearrange("(c p) h n -> p c (h n)", p=P)).then_inc(on.uk_loaded, 16)
            sp.dma_start(w_uv[:], a["w_uv"][0].rearrange("(c p) h n -> p c h n", p=P)).then_inc(on.uv_loaded, 16)
            sp.dma_start(work[:, 3 * D:3 * D + 256].rearrange("p (c n) -> p c n", c=2),
                         a["sub_keys"][0].rearrange("c k d -> k c d")).then_inc(on.sub_loaded, 16)
            sp.dma_start(low_keys[:], a["c_low"].partition_broadcast(P)).then_inc(on.gains_loaded, 16)
            sp.dma_start(g_ffn[:], a["g_ffn_norm"][0].partition_broadcast(P)).then_inc(on.gains_loaded, 16)
            sp.dma_start(g_fin[:], a["g_final"].partition_broadcast(P)).then_inc(on.gains_loaded, 16)
            for k in range(WR, PIECES):
                load_w(0, k)
            with sp.Fori(1, TILES) as f:
                load_tile(f, P)
            def load_page(b, n, what):
                page = sp.value_load(page_table_sb[0:1, b * NPAGES + n:b * NPAGES + n + 1], min_val=0,
                                     max_val=a["cache_ckv"].shape[1] - 1)
                for dst, src in what:
                    sp.dma_start(dst, a[src][0, bass.ds(page, 1)].rearrange("a k r -> k (a r)"))\
                        .then_inc(pages_loaded[b % 2][n // QP], 16)

            load_x(TILES, SB)
            for k in range(3):
                load_w(TILES, k)
            load_rope(TILES, SB, SEQ)
            sp.wait_ge(on.olat_kept, TILES * H)
            sp.wait_ge(on.pages_table_loaded, 16)
            for n in range(NPAGES):
                load_page(0, n, [(page_rows(0, n), "cache_ckv")])
            for k in range(3, N_IN + WR):
                load_w(TILES, k)
            for event in (on.qlat_kept, on.q_roped, on.conv_done):
                sp.wait_ge(event, TILES + 1)
            sp.wait_ge(on.conv_stored, 3 * 16)
            for n in range(NPAGES):
                load_page(0, n, [(pages_kr[0][:, n, :], "cache_krope")])
            for b in range(1, SB):
                if b >= 2:
                    sp.wait_ge(on.page_pv, b - 1)
                for n in range(NPAGES):
                    load_page(b, n, [(page_rows(b, n), "cache_ckv"), (pages_kr[b % 2][:, n, :], "cache_krope")])
            for k in range(N_IN + WR, PIECES):
                load_w(TILES, k)
            sp.wait_ge(on.picked, TILES + 1)
            sp.dma_start(a["scratch"], xn2_next[0:SB, :]).then_inc(on.srow_stored, 16)
            sp.wait_ge(on.srow_stored, 16)
            sp.wait_ge(on.u_free, TILES * SLOTS + RING)
            for t in range(SB):
                sp.dma_start(SPREAD[t], a["scratch"][t].partition_broadcast(P)).then_inc(on.srow_loaded, 16)
            sp.wait_ge(on.kv_stored, (TILES + 1) * 2 * 16)
            sp.wait_ge(on.conv_stored, 3 * 16)
            sp.wait_ge(on.y_stored, (TILES + 2) * 16)

        @block.tensor
        def _(pe):
            def weights(f, k):
                pe.wait_ge(w_loaded[k % WR], (f * (PIECES // WR) + k // WR + 1) * 16)
                return w_ring[:, k % WR]

            def project(dst, w, c0, m, xT, T):
                for k in range(DC):
                    last = nc.tensor.matmul(dst, w[:, k, c0:c0 + m], xT[:, k * T:(k + 1) * T],
                                            start=(k == 0), stop=(k == DC - 1))
                return last

            def turn_rows(src, banks, T):
                for c in range(DC):
                    last = nc.tensor.transpose(banks[c // 4][:, (c % 4) * T:(c % 4 + 1) * T],
                                               src[0:T, c * P:(c + 1) * P], ident[0:T, 0:T])
                return last

            def turn_in(f, T):
                pe.wait_ge(on.x_scaled, f + 1)
                turn_rows(W[0], F[0:2], T).then_inc(on.x_turned, 1)

            def proj_lat(f, T):
                xT = W[4]
                pe.wait_ge(on.xn_kept, f + 1)
                for k in range(3):
                    w = weights(f, k)
                    for m in range(2 * k, min(2 * k + 2, 5)):
                        dst = F[2][:, m * T:(m + 1) * T] if m < 3 else F[3][:, (m - 3) * T:(m - 2) * T]
                        last = project(dst, w, (m % 2) * P, P, xT, T)
                    if k < 2:
                        last.then_inc(on.w_used, 1)
                project(F[2][0:ROPE, 3 * T:4 * T], w, P, ROPE, xT, T).then_inc(on.w_used, 1)

            def latent_norm(f, T):
                pe.wait_ge(on.lat_squared, f + 1)
                for c in range(3):
                    nc.tensor.matmul(F[4][:, 0:T], ones[:], W[2][:, c * T:(c + 1) * T], start=(c == 0), stop=(c == 2))
                for c in range(2):
                    last = nc.tensor.matmul(F[4][:, T:2 * T], ones[:], W[2][:, (3 + c) * T:(4 + c) * T],
                                            start=(c == 0), stop=(c == 1))
                last.then_inc(on.lat_summed, 1)
                nc.tensor.matmul(F[5][0:ROPE, 0:T], rot[:], kr_t[:, 0, 0:T], start=True, stop=True)\
                    .then_inc(on.kr_rotated, 1)

            def kv_rows(f, T):
                pe.wait_ge(on.kv_normed, f + 1)
                pe.wait_ge(on.kr_roped, f + 1)
                for c in range(2):
                    nc.tensor.transpose(F[2][0:T, c * P:(c + 1) * P], ck_t[:, c, 0:T], ident[:])
                nc.tensor.transpose(F[2][0:T, KV:KV + ROPE], kr_t[:, 1, 0:T], ident[0:ROPE, 0:ROPE])\
                    .then_inc(on.kv_turned, 1)

            def z_group(f, T, k0, bank):
                for k in range(k0, k0 + 2):
                    w = weights(f, k)
                    for m in range(2):
                        c = 2 * (k - k0) + m
                        last = project(F[bank][:, c * T:(c + 1) * T], w, m * P, P, W[4], T)
                    last.then_inc(on.w_used, 1)

            def conv_gate(f, T):
                z_group(f, T, 7, 5)
                if T != P:
                    pe.wait_ge(on.z_kept, f + 1)
                    for c in range(4):
                        nc.tensor.transpose(F[0][0:SB, c * P:(c + 1) * P], z_s[:, c, 2, :], ident[:])
                    for c in range(4):
                        last = nc.tensor.transpose(F[1][0:2, c * P:(c + 1) * P], z_ext[:, c, 0:2], ident[:])
                    last.then_inc(on.z_tail_turned, 1)

            def q_proj(f, T):
                pe.wait_ge(on.cq_normed, f + 1)
                if T != P:
                    pe.wait_ge(on.z_tail_kept, 1)
                for h in range(H):
                    for c in range(3):
                        nc.tensor.matmul(F[0][:, h * T:(h + 1) * T], w_uq[:, c, h, 0:NOPE], W[1][:, c * T:(c + 1) * T],
                                         start=(c == 0), stop=(c == 2))
                for h in range(H):
                    for c in range(3):
                        last = nc.tensor.matmul(F[1][0:ROPE, h * T:(h + 1) * T], w_uq[:, c, h, NOPE:NOPE + ROPE],
                                                W[1][:, c * T:(c + 1) * T], start=(c == 0), stop=(c == 2))
                last.then_inc(on.q_projected, 1)

            def q_latent(f, T):
                pe.wait_ge(on.q_kept, f + 1)
                pe.wait_ge(on.kv_rows_kept, f + 1)
                waited(pe)
                nc.tensor.matmul(F[2][0:ROPE, 0:4 * T], rot[:], W[4][0:ROPE, 512:512 + 4 * T], start=True, stop=True)\
                    .then_inc(on.qr_rotated, 1)
                pe.wait_ge(on.z_kept, f + 1)
                for c in range(2):
                    for h in range(H):
                        last = nc.tensor.matmul(F[3 + c][:, h * T:(h + 1) * T], w_ukT[:, h, c * P:(c + 1) * P],
                                                W[4][:, h * T:(h + 1) * T], start=True, stop=True)
                last.then_inc(on.qlat_projected, 1)

            def head_start(f, h):
                n = f * H + h
                if h == 0:
                    pe.wait_ge(on.qlat_kept, f + 1)
                    pe.wait_ge(on.q_roped, f + 1)
                    pe.wait_ge(on.kv_cols_kept, f + 1)
                else:
                    pe.wait_ge(on.scores_masked, n)
                for half in range(2):
                    ks = slice(half * 512, half * 512 + 512)
                    for c in range(2):
                        nc.tensor.matmul(F[half][:, :], q_lat[:, c, h, :], ckvT[:, c, ks], start=(c == 0), stop=False)
                    last = nc.tensor.matmul(F[half][:, :], q_ro[:, h, :], krT[:, ks], start=False, stop=True)
                last.then_inc(on.scores_made, 1)

            def head_end(f, h):
                n = f * H + h
                pe.wait_ge(on.probs_made, n + 1)
                for j in range(4):
                    last = nc.tensor.transpose(F[2][:, j * P:(j + 1) * P], W[0][:, j * P:(j + 1) * P], ident[:])
                last.then_inc(on.probs_turned_a, 1)
                for j in range(4):
                    last = nc.tensor.transpose(F[3][:, j * P:(j + 1) * P], W[0][:, (4 + j) * P:(5 + j) * P], ident[:])
                last.then_inc(on.probs_turned_b, 1)

            def head_values(f, h):
                n = f * H + h
                pe.wait_ge(on.probs_kept_a, n + 1)
                pe.wait_ge(on.probs_kept_b, n + 1)
                for c in range(2):
                    for j in range(TILES):
                        last = nc.tensor.matmul(F[4][:, c * P:(c + 1) * P], ckv_rows[:, j, c * P:(c + 1) * P],
                                                W[1][:, j * P:(j + 1) * P], start=(j == 0), stop=(j == TILES - 1))
                last.then_inc(on.pv_made, 1)

            def attn_out(f, T):
                pe.wait_ge(on.olat_kept, (f + 1) * H if T == P else TILES * H + SB)
                pe.wait_ge(on.zb_kept, f + 1)
                for h in range(H):
                    for c in range(2):
                        last = nc.tensor.matmul(F[5][:, h * T:(h + 1) * T], w_uv[:, c, h, :],
                                                o_lat[:, (c * H + h) * T:(c * H + h + 1) * T],
                                                start=(c == 0), stop=(c == 1))
                last.then_inc(on.attn_projected, 1)

            def mix_norm(f, T):
                pe.wait_ge(on.mix_squared, f + 1)
                for half in range(2):
                    last = nc.tensor.matmul(F[half][:, 0:4 * T], ones[:], W[0][:, half * 4 * T:(half + 1) * 4 * T],
                                            start=True, stop=True)
                last.then_inc(on.mix_summed, 1)

            def mix_out(f, T):
                pe.wait_ge(on.mix_normed, f + 1)
                for j in range(N_OUT):
                    w = weights(f, N_IN + j)
                    dst = F[2 + j // 2][0:T, (j % 2) * 256:(j % 2) * 256 + 256]
                    for k in range(DC):
                        last = nc.tensor.matmul(dst, W[2][:, k * T:(k + 1) * T], w[:, k, :],
                                                start=(k == 0), stop=(k == DC - 1))
                    last.then_inc(on.w_used, 1)

            def ffn_turn(f, T):
                pe.wait_ge(on.xn2_made, f + 1)
                turn_rows(xn2_next, F[4:6], T).then_inc(on.xn2_turned, 1)

            def query_start(f, T, h):
                n = f * PH + h
                if h == 0:
                    pe.wait_ge(on.xn2_kept, f + 1)
                else:
                    pe.wait_ge(on.pq_kept, n)
                w = weights(f, N_IN + N_OUT + h)
                for c in range(2):
                    last = project(F[0][:, c * T:(c + 1) * T], w, c * P, P, W[4], T)
                last.then_inc(on.w_used, 1)

            def query_end(f, T, h):
                n = f * PH + h
                pe.wait_ge(on.pq_kept, n + 1)
                if h:
                    pe.wait_ge(on.key_scores_kept, n)
                for c in range(2):
                    last = nc.tensor.matmul(F[1][0:T, c * KEYS:(c + 1) * KEYS], W[3][:, c * T:(c + 1) * T],
                                            sub_keysT[:, c, :], start=True, stop=True)
                last.then_inc(on.key_scores_made, 1)

            def page_scores(n):
                b, q = divmod(n, QUARTERS)
                pe.wait_ge(on.page_kept, 2 * (n + 1))
                if q == 0 and b:
                    pe.wait_ge(on.page_scores_kept, b)
                for pg in range(QP):
                    col = 4 * (q * QP + pg)
                    for c in range(2):
                        nc.tensor.matmul(F[3][:, col:col + 4], pages_T[:, c, pg * P:(pg + 1) * P],
                                         q_lat_s[:, c, :, b], start=(c == 0), stop=False)
                    last = nc.tensor.matmul(F[3][:, col:col + 4], pages_T[0:ROPE, 2, pg * P:(pg + 1) * P],
                                            q_ro[:, :, b], start=False, stop=True)
                last.then_inc(on.page_scores_made, 1)

            def page_turn(n):
                b, q = divmod(n, QUARTERS)
                pe.wait_ge(pages_loaded[b % 2][q], (b // 2 + 1) * 2 * QP * 16)
                for pg in range(QP):
                    for c in range(2):
                        nc.tensor.transpose(F[c][:, pg * P:(pg + 1) * P], page_rows(b, q * QP + pg)[:, c * P:(c + 1) * P], ident[:])
                    last = nc.tensor.transpose(F[2][0:ROPE, pg * P:(pg + 1) * P], pages_kr[b % 2][:, q * QP + pg, :], ident[:])
                last.then_inc(on.page_turned, 1)

            def own_key_scores(f):
                pe.wait_ge(on.qlat_kept, f + 1)
                pe.wait_ge(on.q_roped, f + 1)
                for c in range(2):
                    nc.tensor.matmul(F[5][0:SB, 0:4 * SB], ck_t[:, c, 0:SB],
                                     q_lat_s[:, c, :, :], start=(c == 0), stop=False)
                nc.tensor.matmul(F[5][0:SB, 0:4 * SB], kr_t[:, 1, 0:SB], q_ro[:, :, 0:SB],
                                 start=False, stop=True).then_inc(on.s_new_made, 1)

            def page_values(b):
                pe.wait_ge(on.page_exp, b + 1)
                if b == 0:
                    pe.wait_ge(on.s_new_kept, 1)
                nc.tensor.matmul(F[4][:, 256:256 + 4 * (NPAGES + 1)], ones[:], page_p[:], start=True, stop=True)
                for c in range(2):
                    for n in range(NPAGES):
                        nc.tensor.matmul(F[5][:, 4 * c:4 * c + 4], page_rows(b, n)[:, c * P:(c + 1) * P],
                                         page_p[:, 4 * n:4 * n + 4], start=(n == 0), stop=False)
                    last = nc.tensor.matmul(F[5][:, 4 * c:4 * c + 4], kv_rows_t[0:SB, c * P:(c + 1) * P],
                                            page_p[0:SB, 4 * NPAGES:4 * NPAGES + 4], start=False, stop=True)
                last.then_inc(on.page_pv, 1)

            def pages_stage(f, n):
                b, q = divmod(n, QUARTERS)
                if n == 0:
                    own_key_scores(f)
                if q == 1 and b:
                    pe.wait_ge(on.page_max_made, 2 * b)
                    nc.tensor.matmul(F[4][:, 128:132], gm_rows[:], ident[0:H, 0:H], start=True, stop=True)\
                        .then_inc(on.page_gmax_spread, 1)
                if 0 < n <= SB * QUARTERS:
                    page_scores(n - 1)
                if n < SB * QUARTERS:
                    page_turn(n)
                if q == 0 and b:
                    pe.wait_ge(on.page_max_made, 2 * b - 1)
                    nc.tensor.transpose(F[4][0:H, 0:P], small_col(C_PM, 4), ident[:]).then_inc(on.page_gmax, 1)
                if q == 2 and b:
                    page_values(b - 1)

            def v_group(it, g):
                for r in range(G):
                    slot = (g % 2) * G + r
                    pe.wait_ge(on.diag_made, it * SLOTS + g * G + r + 1)
                    pe.wait_ge(v_loaded[slot], (it * (GROUPS // 2) + g // 2 + 1) * 16)
                    for half in range(2):
                        last = nc.tensor.matmul(acc[:, half, :], diag[:, slot, :], v_ring[:, slot, half * 512:half * 512 + 512],
                                                start=False, stop=(g == GROUPS - 1 and r == G - 1))
                    last.then_inc(on.v_free, 1)

            def residual(f):
                after(pe, on.acc_free, f)
                pe.wait_ge(on.x1_kept, f + 1)
                for half in range(2):
                    last = nc.tensor.matmul(acc[:, half, :], ident[:], x1_next[:, half * 512:half * 512 + 512],
                                            start=True, stop=False)
                last.then_inc(on.residual_in, 1)

            def stage(f, T, name, n):
                if name == "turn":
                    turn_in(f, T)
                elif name == "latent":
                    proj_lat(f, T)
                elif name == "latent_norm":
                    latent_norm(f, T)
                elif name == "kv_rows":
                    kv_rows(f, T)
                elif name == "z_in":
                    z_group(f, T, 3, 3)
                elif name == "z_gate":
                    z_group(f, T, 5, 4)
                elif name == "conv":
                    conv_gate(f, T)
                elif name == "q_proj":
                    q_proj(f, T)
                elif name == "q_latent":
                    q_latent(f, T)
                elif name == "head":
                    if n > 0:
                        head_end(f, n - 1)
                    if n < H:
                        head_start(f, n)
                    if n > 0:
                        head_values(f, n - 1)
                elif name == "pages":
                    pages_stage(f, n)
                elif name == "attn":
                    attn_out(f, T)
                elif name == "mix_norm":
                    mix_norm(f, T)
                elif name == "mix_out":
                    mix_out(f, T)
                elif name == "ffn_turn":
                    ffn_turn(f, T)
                elif name == "query":
                    if n > 0:
                        query_end(f, T, n - 1)
                    if n < PH:
                        query_start(f, T, n)

            def tile(it, T):
                for g in range(GROUPS):
                    for name, n in beside(g, T):
                        stage(it + 1, T, name, n)
                    v_group(it, g)

            pe.wait_ge(on.consts_ready, 6 * 16)
            pe.wait_ge(on.vec_loaded, 6 * 16)
            nc.tensor.transpose(F[0][:, 0:VEC_ROWS], W[0][0:VEC_ROWS, 0:P], ident[0:VEC_ROWS, 0:VEC_ROWS]).then_inc(on.vec_turned, 1)
            pe.wait_ge(on.uk_loaded, 16)
            for h in range(H):
                for c in range(2):
                    last = nc.tensor.transpose(F[1 + h // 2][:, (h % 2) * KV + c * P:(h % 2) * KV + (c + 1) * P],
                                               W[2][:, c * 512 + h * P:c * 512 + (h + 1) * P], ident[:])
            last.then_inc(on.uk_turned, 1)
            pe.wait_ge(on.sub_loaded, 16)
            for c in range(2):
                last = nc.tensor.transpose(F[3][:, c * P:(c + 1) * P], W[3][:, c * P:(c + 1) * P], ident[:])
            last.then_inc(on.sub_turned, 1)
            pe.wait_ge(on.state_loaded, 16)
            for c in range(4):
                last = nc.tensor.transpose(F[4][:, c * 2 * SB:(c + 1) * 2 * SB], W[4][0:2 * SB, c * P:(c + 1) * P],
                                           ident[0:2 * SB, 0:2 * SB])
            last.then_inc(on.state_turned, 1)
            pe.wait_ge(on.uq_loaded, 16)
            pe.wait_ge(on.uv_loaded, 16)
            for name, n in stages_of(P):
                stage(0, P, name, n)
            residual(0)
            with pe.Fori(0, TILES - 1) as it:
                tile(it, P)
                residual(it + 1)
            tile(TILES - 1, SB)
            pe.wait_ge(on.picked, TILES + 1)
            nc.tensor.transpose(F[0][:, 0:SB], picked_ab[0:SB, 0, :, :].rearrange("p h k -> p (h k)"), ident[0:SB, 0:SB])
            nc.tensor.transpose(F[0][:, SB:2 * SB], gate_next[0:SB, :], ident[0:SB, 0:SB]).then_inc(on.s_turned, 1)
            pe.wait_ge(on.acc_free, TILES)
            for half in range(2):
                nc.tensor.matmul(acc[0:SB, half, :], ident[0:SB, 0:SB], x1_next[0:SB, half * 512:half * 512 + 512],
                                 start=True, stop=False)
            pe.wait_ge(on.s_weights, 1)
            for t in range(SB):
                pe.wait_ge(v_loaded[t], (TILES * (GROUPS // 2) + 1) * 16)
                for half in range(2):
                    last = nc.tensor.matmul(acc[0:SB, half, :], s_fan[:, t, :], v_ring[:, t, half * 512:half * 512 + 512],
                                            start=False, stop=(t == SB - 1))
            last.then_inc(on.v_free, 1)

        @block.scalar
        def _(act):
            def rsqrt_start(own, dst, ms):
                own(nc.scalar.activation(dst, ms, ACT.Ln))
                return nc.scalar.activation(dst, dst, ACT.Exp, scale=-0.5)

            def stage(own, f, T, name, n):
                if name == "norm":
                    act.wait_ge(on.in_ms, f + 1)
                    rsqrt_start(own, small_col(C_Y, 1, T), small_col(C_MS, 1, T)).then_inc(on.in_rs, 1)
                elif name == "latent":
                    act.wait_ge(on.w_used, f * PIECES + 3)
                    nc.scalar.copy(W[1][:, 0:3 * T], F[2][:, 0:3 * T])
                    nc.scalar.copy(W[1][:, 3 * T:5 * T], F[3][:, 0:2 * T])
                    nc.scalar.copy(kr_t[:, 0, 0:T], F[2][0:ROPE, 3 * T:4 * T]).then_inc(on.lat_kept, 1)
                elif name == "latent_norm":
                    act.wait_ge(on.lat_ms, f + 1)
                    rsqrt_start(own, W[3][:, 256:256 + 2 * T], W[3][:, 0:2 * T]).then_inc(on.lat_rs, 1)
                elif name == "kv_rows":
                    act.wait_ge(on.kv_turned, f + 1)
                    after(act, on.kv_stored, f * 2 * 16)
                    own(nc.scalar.copy(kv_rows_t[0:T, :], F[2][0:T, 0:KV + ROPE]))
                    if T == P:
                        if isinstance(f, int):
                            act.wait_ge(on.zeroed, 3)
                        nc.scalar.copy(ckv_rows[:, bass.ds(f, 1), :].rearrange("p a r -> p (a r)"), F[2][:, 0:KV])\
                            .then_inc(on.kv_rows_kept, 1)
                        nc.scalar.copy(ckvT[:, :, bass.ds(f * P, P)], ck_t[:, :, :])
                        nc.scalar.copy(krT[:, bass.ds(f * P, P)], kr_t[:, 1, :]).then_inc(on.kv_cols_kept, 1)
                        ckv_out, kr_out = out["new_ckv_prompt"][0, 0, bass.ds(f * P, P)], out["new_krope_prompt"][0, 0, bass.ds(f * P, P)]
                    else:
                        nc.scalar.copy(page_s[0:1, 0:1], ones[0:1, 0:1]).then_inc(on.kv_rows_kept, 1)
                        ckv_out = out["new_ckv_sample"].rearrange("l b s r -> (l b s) r")
                        kr_out = out["new_krope_sample"].rearrange("l b s r -> (l b s) r")
                    act.dma_start(ckv_out, kv_rows_t[0:T, 0:KV]).then_inc(on.kv_stored, 16)
                    act.dma_start(kr_out, kv_rows_t[0:T, KV:KV + ROPE]).then_inc(on.kv_stored, 16)
                elif name == "z_in":
                    act.wait_ge(on.w_used, f * PIECES + 5)
                    nc.scalar.copy(W[0][:, 0:4 * T], F[3][:, 0:4 * T]).then_inc(on.zin_kept, 1)
                elif name == "conv":
                    act.wait_ge(on.w_used, f * PIECES + 9)
                    nc.scalar.copy(zb[:, :, 0:T], F[5][:, 0:4 * T].rearrange("p (c t) -> p c t", c=4)).then_inc(on.zb_kept, 1)
                    if T != P:
                        act.wait_ge(on.z_tail_turned, 1)
                        act.wait_ge(on.conv_done, f + 1)
                        own(nc.scalar.copy(W[3][0:SB, 0:CW], F[0][0:SB, :]))
                        nc.scalar.copy(W[3][0:2, CW:2 * CW], F[1][0:2, :]).then_inc(on.z_tail_kept, 1)
                        act.wait_ge(on.z_tail_kept, 1)
                        act.dma_start(out["new_conv_sample"][0, :, 1, :], W[3][0:SB, 0:CW]).then_inc(on.conv_stored, 16)
                        act.dma_start(out["new_conv_prompt"][0, 0], W[3][0:2, CW:2 * CW]).then_inc(on.conv_stored, 16)
                elif name == "q_proj":
                    act.wait_ge(on.q_projected, f + 1)
                    nc.scalar.copy(W[4][:, 0:4 * T], F[0][:, 0:4 * T])
                    nc.scalar.copy(W[4][0:ROPE, 512:512 + 4 * T], F[1][0:ROPE, 0:4 * T]).then_inc(on.q_kept, 1)
                elif name == "q_latent":
                    act.wait_ge(on.qlat_projected, f + 1)
                    for c in range(2):
                        last = nc.scalar.copy((q_lat if T == P else q_lat_s)[:, c, :, :], F[3 + c][:, 0:4 * T].rearrange("p (h t) -> p h t", h=H))
                    last.then_inc(on.qlat_kept, 1)
                elif name == "head":
                    if n > 0:
                        act.wait_ge(on.probs_turned_b, f * H + n)
                        nc.scalar.copy(W[1][:, 512:1024], F[3][:, :]).then_inc(on.probs_kept_b, 1)
                    if n < H:
                        act.wait_ge(on.max_made, f * H + n + 1)
                        nc.scalar.activation(W[0], W[0], ACT.Exp, bias=small_col(C_NMAX), scale=SCALE,
                                             accum_out=small_col(C_L)).then_inc(on.exp_made, 1)
                    if n > 0:
                        act.wait_ge(on.pv_made, f * H + n)
                        nc.scalar.copy(o_lat.rearrange("p (c h t) -> p c h t", c=2, h=H)[:, :, n - 1, :],
                                       F[4][:, 0:2 * P].rearrange("p (c t) -> p c t", c=2)).then_inc(on.olat_kept, 1)
                elif name == "pages":
                    b, q = divmod(n, QUARTERS)
                    if q == 1 and b:
                        act.wait_ge(on.page_shifted, b)
                        nc.scalar.activation(page_p[:], page_s[:], ACT.Exp, scale=SCALE).then_inc(on.page_exp, 1)
                    if n < SB * QUARTERS:
                        act.wait_ge(on.page_turned, n + 1)
                        nc.scalar.copy(pages_T[:, 0, :], F[0][:, :]).then_inc(on.page_kept, 1)
                elif name == "attn":
                    act.wait_ge(on.attn_projected, f + 1)
                    nc.scalar.copy(mix_raw[:, 0:4 * T], F[5][:, 0:4 * T]).then_inc(on.attn_kept, 1)
                elif name == "mix_norm":
                    act.wait_ge(on.mix_ms, f + 1)
                    rsqrt_start(own, W[1][:, 0:8 * T], W[0][:, 0:8 * T]).then_inc(on.mix_rs, 1)
                elif name == "ffn_norm":
                    act.wait_ge(on.ffn_ms, f + 1)
                    rsqrt_start(own, small_col(C_Y2, 1, T), small_col(C_MS2, 1, T)).then_inc(on.ffn_rs, 1)
                elif name == "query":
                    if n > 0:
                        act.wait_ge(on.key_scores_made, f * PH + n)
                        after(act, on.top_keys_done, f * PH + n - 1)
                        nc.scalar.copy(keys_s[0:T].rearrange("p c k -> p (c k)"), F[1][0:T, 0:2 * KEYS])\
                            .then_inc(on.key_scores_kept, 1)
                    if n < PH:
                        act.wait_ge(on.w_used, f * PIECES + N_IN + N_OUT + n + 1)
                        nc.scalar.copy(W[3][:, 0:2 * T], F[0][:, 0:2 * T]).then_inc(on.pq_kept, 1)
                elif name == "select" and n == 0:
                    act.wait_ge(on.gate_max_made, f + 1)
                    nc.scalar.activation(gate_next[0:T, :], gate_next[0:T, :], ACT.Exp).then_inc(on.gate_exp_made, 1)

            def gelu_group(it, g):
                act.wait_ge(on.u_free, it * SLOTS + (g + 1) * G + RING)
                nc.scalar.activation(gelu[:, g * G:(g + 1) * G], dots[:, g * G:(g + 1) * G], ACT.Gelu).then_inc(on.gelu_done, 1)

            def diag_group(it, g):
                act.wait_ge(on.w_made, it * GROUPS + g + 1)
                act.wait_ge(on.v_free, it * SLOTS + (g + 1) * G)
                for r in range(G):
                    s = g * G + r
                    nc.scalar.activation(diag[:, s % RING, :], ident[:], ACT.Copy, scale=wgt[:, s:s + 1]).then_inc(on.diag_made, 1)

            def finalize(own, it, T):
                act.wait_ge(on.y_ms, it + 1)
                rsqrt_start(own, small_col(C_Y3, 1, T), small_col(C_MS3, 1, T)).then_inc(on.y_rs, 1)
                act.wait_ge(on.y_made, it + 1)
                dst = out["y_prompt"][0, bass.ds(it * P, P)] if T == P else out["y_sample"].rearrange("b s d -> (b s) d")
                act.dma_start(dst, y_t[0:T, :]).then_inc(on.y_stored, 16)

            def tile(it, T):
                own = Own(act, on.act_front, (it + 1) * ACT_FRONT)
                gelu_group(it, 0)
                for g in range(GROUPS):
                    if g + 1 < GROUPS:
                        gelu_group(it, g + 1)
                    diag_group(it, g)
                    for name, n in beside(g, T):
                        stage(own, it + 1, T, name, n)
                if T == P:
                    own.check(ACT_FRONT)
                own2 = Own(act, on.act_peer, it * ACT_PEER)
                finalize(own2, it, P)
                own2.check(ACT_PEER)

            own = Own(act, on.act_front, 0)
            act.wait_ge(on.consts_ready, 6 * 16)
            for name, n in stages_of(P):
                stage(own, 0, P, name, n)
            own.check(ACT_FRONT)
            with act.Fori(0, TILES - 1) as it:
                tile(it, P)
            tile(TILES - 1, SB)
            act.wait_ge(on.s_dots, SB)
            nc.scalar.activation(gelu[:, 0:SB], dots[:, 0:SB], ACT.Gelu).then_inc(on.s_gelu, 1)
            finalize(Own(act, on.act_peer, TILES * ACT_PEER), TILES, SB)

        @block.vector
        def _(dve):
            v = nc.vector

            def sharpen(own, ms, y, t):
                own(v.tensor_tensor(t, ms, y, ALU.mult))
                own(v.scalar_tensor_tensor(out=t, in0=t, scalar=-0.5, in1=y, op0=ALU.mult, op1=ALU.mult))
                own(v.scalar_tensor_tensor(out=y, in0=t, scalar=1.5, in1=y, op0=ALU.add, op1=ALU.mult))

            def mean(dst, total, n):
                return v.tensor_scalar(dst, total, 1.0 / n, EPS, ALU.mult, ALU.add)

            def spread_cols(first, n, T):
                return vec_cols[:, first:first + n].unsqueeze(2).to_broadcast([P, n, T])

            def split(ap, c):
                return ap.rearrange("p (c t) -> p c t", c=c)

            def norm_in(own, f, T):
                dve.wait_ge(on.x_loaded, (f + 1) * 16)
                own(v.tensor_tensor_reduce(W[0][0:T, :], x_t[0:T, :], x_t[0:T, :], 1.0, 0.0, ALU.mult, ALU.add, small_col(C_SS, 1, T)))
                mean(small_col(C_MS, 1, T), small_col(C_SS, 1, T), D).then_inc(on.in_ms, 1)
                dve.wait_ge(on.in_rs, f + 1)
                sharpen(own, small_col(C_MS, 1, T), small_col(C_Y, 1, T), small_col(C_T, 1, T))
                v.tensor_scalar(W[0][0:T, :], x_t[0:T, :], small_col(C_Y, 1, T), None, ALU.mult).then_inc(on.x_scaled, 1)

            def keep_turned(f, T):
                dve.wait_ge(on.x_turned, f + 1)
                for half in range(2):
                    last = v.tensor_tensor(split(W[4][:, half * 4 * T:(half + 1) * 4 * T], 4), split(F[half][:, 0:4 * T], 4),
                                           spread_cols(ROW_GMIX + 4 * half, 4, T), ALU.mult)
                last.then_inc(on.xn_kept, 1)

            def square_latents(f, T):
                dve.wait_ge(on.lat_kept, f + 1)
                v.tensor_tensor(W[2][:, 0:5 * T], W[1][:, 0:5 * T], W[1][:, 0:5 * T], ALU.mult).then_inc(on.lat_squared, 1)

            def latents(own, f, T):
                dve.wait_ge(on.lat_summed, f + 1)
                after(dve, on.y_stored, f * 16)
                mean(W[3][:, 0:T], F[4][:, 0:T], QR)
                mean(W[3][:, T:2 * T], F[4][:, T:2 * T], KV).then_inc(on.lat_ms, 1)
                dve.wait_ge(on.kr_rotated, f + 1)
                dve.wait_ge(on.rope_loaded, (f + 1) * 2 * 16)
                own(v.tensor_tensor(kr_t[:, 1, 0:T], kr_t[:, 0, 0:T], cos_t[:, 0:T], ALU.mult))
                own(v.tensor_tensor(kr_t[:, 2, 0:T], F[5][0:ROPE, 0:T], sin_t[:, 0:T], ALU.mult))
                v.tensor_tensor(kr_t[:, 1, 0:T], kr_t[:, 1, 0:T], kr_t[:, 2, 0:T], ALU.add).then_inc(on.kr_roped, 1)
                dve.wait_ge(on.lat_ms, f + 1)
                dve.wait_ge(on.lat_rs, f + 1)
                rs = W[3][:, 256:256 + 2 * T]
                sharpen(own, W[3][:, 0:2 * T], rs, W[3][:, 512:512 + 2 * T])
                for c in range(5):
                    dst = W[1][:, c * T:(c + 1) * T] if c < 3 else ck_t[:, c - 3, 0:T]
                    last = v.scalar_tensor_tensor(out=dst, in0=W[1][:, c * T:(c + 1) * T], scalar=vec_cols[:, ROW_GQ + c:ROW_GQ + c + 1],
                                                  in1=rs[:, 0:T] if c < 3 else rs[:, T:2 * T], op0=ALU.mult, op1=ALU.mult)
                    if c == 2:
                        last.then_inc(on.cq_normed, 1)
                last.then_inc(on.kv_normed, 1)

            def conv_in(own, f, T):
                dve.wait_ge(on.zin_kept, f + 1)
                dve.wait_ge(on.w_used, f * PIECES + 7)
                v.tensor_tensor(z_ext[:, :, 2:2 + P] if T == P else z_s[:, :, 2, :], split(F[4][:, 0:4 * T], 4),
                                split(W[0][:, 0:4 * T], 4), ALU.mult).then_inc(on.z_kept, 1)
                dve.wait_ge(on.z_kept, f + 1)

            def conv(own, f, T):
                steps = [z_ext[:, :, k:k + P] for k in range(3)] if T == P else [z_s[:, :, k, :] for k in range(3)]
                y, t = split(W[3][:, 0:4 * T], 4), split(W[2][:, 0:4 * T], 4)
                own(v.tensor_tensor(y, steps[0], spread_cols(ROW_CONV, 4, T), ALU.mult))
                for k in (1, 2):
                    own(v.tensor_tensor(t, steps[k], spread_cols(ROW_CONV + 4 * k, 4, T), ALU.mult))
                    own(v.tensor_tensor(y, y, t, ALU.add))
                dve.wait_ge(on.zb_kept, f + 1)
                v.tensor_tensor(split(mix_raw[:, 4 * T:8 * T], 4), y, zb[:, :, 0:T], ALU.mult).then_inc(on.conv_done, 1)
                dve.wait_ge(on.conv_done, f + 1)
                if T == P:
                    own(v.tensor_copy(z_ext[:, :, 0:2], z_ext[:, :, P:P + 2]))

            def q_rope(own, f, T):
                dve.wait_ge(on.q_kept, f + 1)
                raw = split(W[4][0:ROPE, 512:512 + 4 * T], 4)
                t = split(W[2][0:ROPE, 0:4 * T], 4)
                c4 = cos_t[:, 0:T].unsqueeze(1).to_broadcast([ROPE, H, T])
                s4 = sin_t[:, 0:T].unsqueeze(1).to_broadcast([ROPE, H, T])
                own(v.tensor_tensor(q_ro[:, :, 0:T], raw, c4, ALU.mult))
                dve.wait_ge(on.qr_rotated, f + 1)
                own(v.tensor_tensor(t, split(F[2][0:ROPE, 0:4 * T], 4), s4, ALU.mult))
                v.tensor_tensor(q_ro[:, :, 0:T], q_ro[:, :, 0:T], t, ALU.add).then_inc(on.q_roped, 1)

            def head_start(own, f, h):
                n = f * H + h
                if h == 0:
                    own(v.tensor_copy(small_col(C_LIM), q_limit[:, bass.ds(f, 1)]))
                    own(v.tensor_scalar(small_col(C_LIM + 1), small_col(C_LIM), -512 * BIG, None, ALU.add))
                dve.wait_ge(on.scores_made, n + 1)
                for half in range(2):
                    last = v.scalar_tensor_tensor(out=W[0][:, half * 512:half * 512 + 512], in0=low_keys[:],
                                                  scalar=small_col(C_LIM + half), in1=F[half][:, :], op0=ALU.add, op1=ALU.min)
                last.then_inc(on.scores_masked, 1)
                dve.wait_ge(on.scores_masked, n + 1)
                own(v.tensor_reduce(small_col(C_MAX), W[0], AX.X, ALU.max))
                v.tensor_scalar(small_col(C_NMAX), small_col(C_MAX), -SCALE, None, ALU.mult).then_inc(on.max_made, 1)
                dve.wait_ge(on.exp_made, n + 1)
                own(v.reciprocal(small_col(C_RL), small_col(C_L)))
                v.tensor_scalar(W[0], W[0], small_col(C_RL), None, ALU.mult).then_inc(on.probs_made, 1)

            def head_end(own, f, h):
                n = f * H + h
                dve.wait_ge(on.probs_turned_a, n + 1)
                v.tensor_copy(W[1][:, 0:512], F[2][:, :]).then_inc(on.probs_kept_a, 1)

            def pages_stage(own, n):
                b, q = divmod(n, QUARTERS)
                if n == 0:
                    dve.wait_ge(on.s_new_made, 1)
                    v.tensor_copy(s_new[:], F[5][0:SB, 0:4 * SB]).then_inc(on.s_new_kept, 1)
                    dve.wait_ge(on.s_new_kept, 1)
                if q == 0 and b:
                    dve.wait_ge(on.page_scores_made, QUARTERS * b)
                    v.tensor_copy(page_s[:, 0:4 * NPAGES], F[3][:, 0:4 * NPAGES]).then_inc(on.page_scores_kept, 1)
                    own(v.memset(page_s[:, 4 * NPAGES:], -BIG))
                    own(v.tensor_scalar(page_s[0:SB, 4 * NPAGES:], s_new[:, b - 1:4 * SB:SB], own_row[:, b - 1:b], None, ALU.add))
                    v.tensor_reduce(small_col(C_PM, 4), page_s[:].rearrange("p (n h) -> p h n", h=H), AX.X, ALU.max)\
                        .then_inc(on.page_max_made, 1)
                if q == 1 and b:
                    dve.wait_ge(on.page_gmax_spread, b)
                    s3 = page_s[:].rearrange("p (n h) -> p n h", h=H)
                    v.tensor_tensor(s3, s3, F[4][:, 128:132].unsqueeze(1).to_broadcast([P, NPAGES + 1, H]), ALU.subtract)\
                        .then_inc(on.page_shifted, 1)
                if n < SB * QUARTERS:
                    dve.wait_ge(on.page_turned, n + 1)
                    v.tensor_copy(pages_T[:, 1, :], F[1][:, :])
                    v.tensor_copy(pages_T[0:ROPE, 2, :], F[2][0:ROPE, :]).then_inc(on.page_kept, 1)
                if q == 0 and b:
                    dve.wait_ge(on.page_gmax, b)
                    own(v.tensor_reduce(small_col(C_GM, 1, H), F[4][0:H, 0:P], AX.X, ALU.max))
                    v.tensor_scalar(gm_rows[:], ones[0:H, :], small_col(C_GM, 1, H), None, ALU.mult).then_inc(on.page_max_made, 1)
                if q == 2 and b:
                    dve.wait_ge(on.page_pv, b)
                    own(v.tensor_reduce(small_col(C_PL, 4), F[4][:, 256:256 + 4 * (NPAGES + 1)].rearrange("p (n h) -> p h n", h=H),
                                        AX.X, ALU.add))
                    own(v.reciprocal(small_col(C_PLS, 4), small_col(C_PL, 4)))
                    v.tensor_tensor(o_lat[:, 0:2 * H * SB].rearrange("p (c h t) -> p c h t", c=2, h=H)[:, :, :, b - 1],
                                    F[5][:, 0:2 * H].rearrange("p (c h) -> p c h", c=2),
                                    small_col(C_PLS, 4).unsqueeze(1).to_broadcast([P, 2, H]), ALU.mult).then_inc(on.olat_kept, 1)

            def square_mix(f, T):
                dve.wait_ge(on.attn_kept, f + 1)
                v.tensor_tensor(W[0][:, 0:8 * T], mix_raw[:, 0:8 * T], mix_raw[:, 0:8 * T], ALU.mult).then_inc(on.mix_squared, 1)

            def mix_norm(own, f, T):
                dve.wait_ge(on.mix_summed, f + 1)
                for half in range(2):
                    last = mean(W[0][:, half * 4 * T:(half + 1) * 4 * T], F[half][:, 0:4 * T], P)
                last.then_inc(on.mix_ms, 1)
                dve.wait_ge(on.mix_ms, f + 1)
                dve.wait_ge(on.mix_rs, f + 1)
                sharpen(own, W[0][:, 0:8 * T], W[1][:, 0:8 * T], W[2][:, 0:8 * T])
                own(v.tensor_tensor(W[2][:, 0:8 * T], mix_raw[:, 0:8 * T], W[1][:, 0:8 * T], ALU.mult))
                v.tensor_tensor(split(W[2][:, 0:8 * T], 8), split(W[2][:, 0:8 * T], 8), spread_cols(ROW_GOUT, 8, T), ALU.mult)\
                    .then_inc(on.mix_normed, 1)

            def mix_out(own, f, T):
                dve.wait_ge(on.w_used, f * PIECES + N_IN + N_OUT)
                after(dve, on.residual_in, f)
                for half in range(2):
                    cols = slice(half * 512, half * 512 + 512)
                    last = v.tensor_tensor(x1_next[0:T, cols], F[2 + half][0:T, :], x_t[0:T, cols], ALU.add)
                last.then_inc(on.x1_kept, 1)
                dve.wait_ge(on.x1_kept, f + 1)

            def ffn_norm(own, f, T):
                x1, xn = x1_next[0:T, :], xn2_next[0:T, :]
                own(v.tensor_tensor_reduce(W[0][0:T, :], x1, x1, 1.0, 0.0, ALU.mult, ALU.add, small_col(C_SS2, 1, T)))
                mean(small_col(C_MS2, 1, T), small_col(C_SS2, 1, T), D).then_inc(on.ffn_ms, 1)
                dve.wait_ge(on.ffn_rs, f + 1)
                sharpen(own, small_col(C_MS2, 1, T), small_col(C_Y2, 1, T), small_col(C_T2, 1, T))
                v.scalar_tensor_tensor(out=xn, in0=x1, scalar=small_col(C_Y2, 1, T), in1=g_ffn[0:T, :], op0=ALU.mult,
                                       op1=ALU.mult).then_inc(on.xn2_made, 1)

            def keep_ffn_turned(f, T):
                dve.wait_ge(on.xn2_turned, f + 1)
                for half in range(2):
                    last = v.tensor_copy(W[4][:, half * 4 * T:(half + 1) * 4 * T], F[4 + half][:, 0:4 * T])
                last.then_inc(on.xn2_kept, 1)

            def top16(own, values, scores, index):
                for r in range(2):
                    best = values[:, 8 * r:8 * r + 8]
                    own(v.max(best, scores), held=True)
                    last = v.max_index(index[:, 8 * r:8 * r + 8], best, scores)
                    if r == 0:
                        own(v.match_replace(scores, best, scores, LOW), held=True)
                return last

            def query(own, f, T, h):
                dve.wait_ge(on.key_scores_kept, f * PH + h + 1)
                waited(dve)
                for c in range(2):
                    last = top16(own, sv[0:T, h, c, :], keys_s[0:T, c, :], si_u[0:T, h, c, :])
                last.then_inc(on.top_keys_done, 1)
                dve.wait_ge(on.top_keys_done, f * PH + h + 1)
                grid = [T, TOPK, TOPK]
                scores = cand[0:T, h * 256:(h + 1) * 256]
                own(v.tensor_tensor(scores.rearrange("p (a b) -> p a b", a=TOPK), sv[0:T, h, 0, :].unsqueeze(2).to_broadcast(grid),
                                    sv[0:T, h, 1, :].unsqueeze(1).to_broadcast(grid), ALU.add), held=True)
                own(top16(own, top_s[0:T, h, :], scores, pos_u[0:T, h, :]))

            def select(own, f, T, c):
                grid = [T, PH, TOPK, TOPK]
                gates = gate_next[0:T, :].rearrange("p (h k) -> p h k", h=PH)
                if c == 0:
                    v.tensor_tensor(gates, top_s[0:T], top_s[0:T, :, 0:1].to_broadcast([T, PH, TOPK]), ALU.subtract)\
                        .then_inc(on.gate_max_made, 1)
                    own(v.tensor_copy(si[0:T], si_u[0:T]))
                    own(v.tensor_scalar(pos_ab[0:T, 0], pos_u[0:T], 4, None, ALU.logical_shift_right))
                    own(v.tensor_scalar(pos_ab[0:T, 1], pos_u[0:T], TOPK - 1, None, ALU.bitwise_and))
                    own(v.tensor_copy(pos_f[0:T], pos_ab[0:T]))
                hit = work[0:T, 0:2 * D].rearrange("p (h k a) -> p h k a", h=PH, k=TOPK)
                own(v.tensor_tensor(hit, pos_f[0:T, c].unsqueeze(3).to_broadcast(grid),
                                    iota16[0:T].unsqueeze(1).unsqueeze(1).to_broadcast(grid), ALU.is_equal))
                own(v.tensor_tensor(hit, hit, si[0:T, :, c, :].unsqueeze(2).to_broadcast(grid), ALU.mult))
                own(v.tensor_reduce(picked_ab[0:T, c], hit, AX.X, ALU.add))
                if c == 0:
                    return
                dve.wait_ge(on.gate_exp_made, f + 1)
                total = small_col(C_GS, PH, T)
                own(v.tensor_reduce(total, gates, AX.X, ALU.add))
                own(v.reciprocal(small_col(C_GR, PH, T), total))
                own(v.tensor_tensor(gates, gates, small_col(C_GR, PH, T).unsqueeze(2).to_broadcast([T, PH, TOPK]), ALU.mult))
                dst = pick_next[0:T, :].rearrange("p (h k) -> p h k", h=PH) if T == P else picked_ab[0:T, 0]
                v.scalar_tensor_tensor(out=dst, in0=picked_ab[0:T, 0], scalar=float(KEYS), in1=picked_ab[0:T, 1],
                                       op0=ALU.mult, op1=ALU.add).then_inc(on.picked, 1)
                dve.wait_ge(on.picked, f + 1)
                if T == P:
                    if not isinstance(f, int):
                        dve.wait_ge(on.v_free, f * SLOTS - SLOTS // 2 + RING)
                    v.tensor_copy(pick_cur[:, 0:SLOTS // 2], pick_next[:, 0:SLOTS // 2]).then_inc(on.picked_moved, 1)

            def stage(own, f, T, name, n):
                if name == "norm":
                    norm_in(own, f, T)
                elif name == "turn":
                    keep_turned(f, T)
                elif name == "latent":
                    square_latents(f, T)
                elif name == "latent_norm":
                    latents(own, f, T)
                elif name == "z_gate":
                    conv_in(own, f, T)
                elif name == "conv":
                    conv(own, f, T)
                elif name == "q_latent":
                    q_rope(own, f, T)
                elif name == "head":
                    if n > 0:
                        head_end(own, f, n - 1)
                    if n < H:
                        head_start(own, f, n)
                elif name == "pages":
                    pages_stage(own, n)
                elif name == "attn":
                    square_mix(f, T)
                elif name == "mix_norm":
                    mix_norm(own, f, T)
                elif name == "mix_out":
                    mix_out(own, f, T)
                elif name == "ffn_norm":
                    ffn_norm(own, f, T)
                elif name == "ffn_turn":
                    keep_ffn_turned(f, T)
                elif name == "query":
                    if n > 0:
                        query(own, f, T, n - 1)
                elif name == "select":
                    select(own, f, T, n)

            def dot_group(it, g):
                for r in range(G):
                    slot = (g % 2) * G + r
                    dve.wait_ge(u_loaded[slot], (it * (GROUPS // 2) + g // 2 + 1) * 16)
                    v.tensor_tensor_reduce(u_ring[:, slot, :], u_ring[:, slot, :], xn2_cur[:], 1.0, 0.0, ALU.mult, ALU.add,
                                           dots[:, g * G + r:g * G + r + 1]).then_inc(on.u_free, 1)

            def weigh_group(it, g):
                dve.wait_ge(on.gelu_done, it * GROUPS + g + 1)
                s = slice(g * G, (g + 1) * G)
                v.tensor_tensor(wgt[:, s], gelu[:, s], gate_cur[:, s], ALU.mult).then_inc(on.w_made, 1)

            def move_on(own, f):
                if not isinstance(f, int):
                    dve.wait_ge(on.w_made, f * GROUPS)
                    dve.wait_ge(on.u_free, f * SLOTS + RING)
                v.tensor_copy(gate_cur[:], gate_next[:])
                own(v.tensor_copy(xn2_cur[:], xn2_next))
                if not isinstance(f, int):
                    dve.wait_ge(on.v_free, f * SLOTS + RING)
                v.tensor_copy(pick_cur[:, SLOTS // 2:], pick_next[:, SLOTS // 2:]).then_inc(on.picks_moved, 1)

            def finalize(own, it, T):
                total = acc[0:T].rearrange("p a n -> p (a n)")
                dve.wait_ge(on.y_stored, (it + 1) * 16)
                own(v.tensor_copy(y_t[0:T, :], total))
                v.tensor_tensor_reduce(total, total, y_t[0:T, :], 1.0, 0.0, ALU.mult, ALU.add, small_col(C_SS3, 1, T))\
                    .then_inc(on.acc_free, 1)
                dve.wait_ge(on.acc_free, it + 1)
                mean(small_col(C_MS3, 1, T), small_col(C_SS3, 1, T), D).then_inc(on.y_ms, 1)
                dve.wait_ge(on.y_ms, it + 1)
                dve.wait_ge(on.y_rs, it + 1)
                sharpen(own, small_col(C_MS3, 1, T), small_col(C_Y3, 1, T), small_col(C_T3, 1, T))
                v.scalar_tensor_tensor(out=y_t[0:T, :], in0=y_t[0:T, :], scalar=small_col(C_Y3, 1, T), in1=g_fin[0:T, :],
                                       op0=ALU.mult, op1=ALU.mult).then_inc(on.y_made, 1)

            def tile(it, T):
                own = Own(dve, on.dve_front, (it + 1) * DVE_FRONT)
                dot_group(it, 0)
                for g in range(GROUPS):
                    if g + 1 < GROUPS:
                        dot_group(it, g + 1)
                    weigh_group(it, g)
                    for name, n in beside(g, T):
                        stage(own, it + 1, T, name, n)
                if T == P:
                    own.check(DVE_FRONT)
                own2 = Own(dve, on.dve_peer, it * DVE_PEER + 1)
                if T == P:
                    move_on(own2, it + 1)
                else:
                    dve.wait_ge(on.v_free, TILES * SLOTS + RING)
                finalize(own2, it, P)
                if T == P:
                    own2.check(DVE_PEER)

            own = Own(dve, on.dve_setup, 0)
            own(v.memset(z_ext[:, :, 0:2], 0.0))
            v.memset(s_fan[:], 0.0).then_inc(on.u_free, RING)
            v.memset(gelu[:], 0.0).then_inc(on.v_free, RING)
            v.memset(dots[:], 0.0).then_inc(on.y_stored, 16)
            dve.wait_ge(on.consts_ready, 6 * 16)
            dve.wait_ge(on.vec_turned, 1)
            own(v.tensor_copy(vec_cols[:], F[0][:, 0:VEC_ROWS]))
            dve.wait_ge(on.uk_turned, 1)
            for h in range(H):
                own(v.tensor_copy(w_ukT[:, h, :], F[1 + h // 2][:, (h % 2) * KV:(h % 2 + 1) * KV]))
            dve.wait_ge(on.sub_turned, 1)
            own(v.tensor_copy(sub_keysT[:].rearrange("p c k -> p (c k)"), F[3][:, 0:2 * KEYS]))
            dve.wait_ge(on.state_turned, 1)
            for k in range(2):
                own(v.tensor_copy(z_s[:, :, k, :], F[4][:, 0:8 * SB].rearrange("p (c b k) -> p c b k", c=4, k=2)[:, :, :, k]))
            dve.wait_ge(on.gains_loaded, 3 * 16)
            own = Own(dve, on.dve_front, 0)
            for name, n in stages_of(P):
                stage(own, 0, P, name, n)
            own.check(DVE_FRONT)
            move_on(Own(dve, on.dve_peer, 0), 0)
            with dve.Fori(0, TILES - 1) as it:
                tile(it, P)
            tile(TILES - 1, SB)
            own = Own(dve, on.dve_tail, 0)
            dve.wait_ge(on.s_turned, 1)
            v.tensor_copy(s_pick[:], F[0][:, 0:SB]).then_inc(on.s_slots, 1)
            own(v.tensor_copy(wgt[:, 0:SB], F[0][:, SB:2 * SB]))
            dve.wait_ge(on.srow_loaded, SB * 16)
            for t in range(SB):
                dve.wait_ge(u_loaded[t], (TILES * (GROUPS // 2) + 1) * 16)
                v.tensor_tensor_reduce(u_ring[:, t, :], u_ring[:, t, :], SPREAD[t], 1.0, 0.0, ALU.mult, ALU.add,
                                       dots[:, t:t + 1]).then_inc(on.s_dots, 1)
            dve.wait_ge(on.s_gelu, 1)
            v.tensor_tensor(s_fan[:].rearrange("p a b -> p (a b)")[:, 0:SB * SB:SB + 1], gelu[:, 0:SB], wgt[:, 0:SB], ALU.mult)\
                .then_inc(on.s_weights, 1)
            dve.wait_ge(on.v_free, TILES * SLOTS + RING + 1)
            finalize(own, TILES, SB)

        @block.gpsimd
        def _(pool):
            pool.memset(ckv_rows[:], 0.0).then_inc(on.zeroed, 1)
            pool.memset(ckvT[:], 0.0).then_inc(on.zeroed, 1)
            pool.memset(krT[:], 0.0).then_inc(on.zeroed, 1)

            def gather(table, ring, slot, loaded, pick):
                pool.indirect_dma_start(ring[:, slot, :], None, a[table][0],
                                        bass.IndirectOffsetOnAxis(ap=pick, axis=0)).then_inc(loaded[slot], 16)

            def gather_group(it, g, table, ring, loaded, free):
                if g * G == SLOTS // 2:
                    pool.wait_ge(on.picks_moved, it + 1)
                for s in range(g * G, (g + 1) * G):
                    pool.wait_ge(free, it * SLOTS + s + 1)
                    waited(pool)
                    gather(table, ring, s % RING, loaded, pick_cur[:, s:s + 1])

            with pool.Fori(0, TILES) as it:
                pool.wait_ge(on.picked_moved, it + 1)
                gather_group(it, 0, "expert_u", u_ring, u_loaded, on.u_free)
                for g in range(GROUPS):
                    if g + 1 < GROUPS:
                        gather_group(it, g + 1, "expert_u", u_ring, u_loaded, on.u_free)
                    gather_group(it, g, "expert_v", v_ring, v_loaded, on.v_free)
            pool.wait_ge(on.s_slots, 1)
            pool.wait_ge(on.u_free, TILES * SLOTS + RING)
            pool.wait_ge(on.v_free, TILES * SLOTS + RING)
            for t in range(SB):
                gather("expert_u", u_ring, t, u_loaded, s_pick[:, t:t + 1])
            for t in range(SB):
                gather("expert_v", v_ring, t, v_loaded, s_pick[:, t:t + 1])


IN_NAMES = ["x_prompt", "x_sample", "cache_ckv", "cache_krope", "state_conv", "page_table", "g_mix_norm", "w_in", "g_q",
            "w_uq", "g_kv", "w_uk", "w_uv", "conv_w", "g_attn_out", "g_conv_out", "w_o", "g_ffn_norm", "w_query",
            "sub_keys", "expert_u", "expert_v", "g_final"]
OUT_SHAPES = {"y_prompt": (1, SEQ, D), "y_sample": (SB, 1, D), "new_ckv_prompt": (1, 1, SEQ, KV),
              "new_krope_prompt": (1, 1, SEQ, ROPE), "new_conv_prompt": (1, 1, 2, CW), "new_ckv_sample": (1, SB, 1, KV),
              "new_krope_sample": (1, SB, 1, ROPE), "new_conv_sample": (1, SB, 2, CW)}


def constants():
    import numpy as np

    f32 = np.float32
    rot = np.zeros((ROPE, ROPE), f32)
    for p in range(ROPE // 2):
        rot[p + ROPE // 2, p] = -1.0
        rot[p, p + ROPE // 2] = 1.0
    inv = (f32(10000.0) ** (-np.arange(0, ROPE, 2, dtype=f32) / f32(ROPE))).astype(f32)
    pos = np.concatenate([np.arange(SEQ), np.full(SB, PAST)]).astype(f32)
    ang = (pos[:, None] * inv[None, :]).astype(f32)
    table = np.stack([np.concatenate([t, t], axis=1).T for t in (np.cos(ang), np.sin(ang))])
    own = np.full((SB, SB), -BIG, f32)
    np.fill_diagonal(own, 0.0)
    return {
        "c_ident": np.eye(P, dtype=f32), "c_ones": np.ones((P, P), f32), "c_rot": rot,
        "c_limit": ((np.arange(TILES)[None, :] * P + np.arange(P)[:, None] + 0.5) * BIG).astype(f32),
        "c_iota16": np.tile(np.arange(TOPK, dtype=f32), (P, 1)), "c_own": own,
        "c_rope": np.ascontiguousarray(table.astype(f32)), "c_low": (-np.arange(512) * BIG).astype(f32),
    }


def kernel(**inputs):
    import numpy as np
    import concourse.bacc as bacc
    from concourse.bass_utils import run_bass_kernel_spmd

    nc = bacc.Bacc("TRN2", target_bir_lowering=False, num_devices=1)
    arrays = {n: np.ascontiguousarray(inputs[n]) for n in IN_NAMES}
    arrays.update(constants())
    a = {n: nc.dram_tensor(f"in_{n}", x.shape, mybir.dt.from_np(x.dtype), kind="ExternalInput").ap() for n, x in arrays.items()}
    a["scratch"] = nc.dram_tensor("scratch", (SB, D), F32, kind="Internal").ap()
    out = {n: nc.dram_tensor(f"out_{n}", s, F32, kind="ExternalOutput").ap() for n, s in OUT_SHAPES.items()}
    build(nc, a, out)
    r = run_bass_kernel_spmd(nc, [{f"in_{n}": x for n, x in arrays.items()}], core_ids=[0])
    return tuple(r.results[0][f"out_{n}"] for n in OUT_SHAPES)
```

```python
from collections import namedtuple
from contextlib import ExitStack

import concourse.bass as bass
from concourse import mybir

F32 = mybir.dt.float32
U32 = mybir.dt.uint32
I32 = mybir.dt.int32
ALU = mybir.AluOpType
ACT = mybir.ActivationFunctionType
AX = mybir.AxisListType

P = 128
D = 1024
DC = D // P
SEQ = 1024
TILES = SEQ // P
SB = 8
PAGE = 128
NPAGES = 16
PAST = NPAGES * PAGE
H = 4
NOPE = 128
ROPE = 64
QR = 384
KV = 256
CW = 512
D_IN = QR + KV + ROPE + 3 * CW
PH = 8
KEYS = 128
TOPK = 16
SLOTS = PH * TOPK
EPS = 1e-6
SCALE = float(NOPE + ROPE) ** -0.5
BIG = 1e30
LOW = -3.0e38

PW = 256
IN_COLS = [(0, 256), (256, 256), (512, 192)] + [(704 + 256 * k, 256) for k in range(6)]
OUT_COLS = [(256 * k, 256) for k in range(4)]
QUERY_COLS = [(256 * k, 256) for k in range(PH)]
WR = 3
N_IN, N_OUT, N_QUERY = len(IN_COLS), len(OUT_COLS), len(QUERY_COLS)
PIECES = N_IN + N_OUT + N_QUERY
assert PIECES % WR == 0

G = 4
GROUPS = SLOTS // G
RING = 2 * G

QUARTERS = 4
QP = NPAGES // QUARTERS
_FIRST = ["norm", "turn", "latent", "latent_norm", "kv_rows", "z_in", "z_gate", "conv", "q_proj", "q_latent"]
_LAST = (["attn", "mix_norm", "mix_out", "ffn_norm", "ffn_turn"] + [("query", h) for h in range(PH // 2 + 1)] + [("select", 0)]
         + [("query", h) for h in range(PH // 2 + 1, PH + 1)] + [("select", 1)])
STAGES_PROMPT = _FIRST + [("head", h) for h in range(H + 1)] + _LAST
STAGES_SAMPLE = _FIRST + [("pages", n) for n in range(SB * QUARTERS + QUARTERS)] + _LAST


def stages_of(T):
    return [s if isinstance(s, tuple) else (s, 0) for s in (STAGES_PROMPT if T == P else STAGES_SAMPLE)]


def beside(g, T):
    stages = stages_of(T)
    span = GROUPS - 2 if T == P else GROUPS - 1
    return [s for i, s in enumerate(stages) if i * span // len(stages) == g]


LAST = TILES - 1
FIRST_SHARED = 1 + max(g for g in range(GROUPS) if ("q_latent", 0) in beside(g, SB))


def has_pages(stages):
    return any(name == "pages" for name, n in stages)


def by_vector(it, s):
    return isinstance(it, int) and it == LAST and s // G >= FIRST_SHARED and s % G >= G // 2


def tensor_slots(it, s):
    return it * SLOTS + s + 1 - vector_slots(it, s)


def vector_slots(it, s):
    return sum(by_vector(it, x) for x in range(s + 1))


DVE_FRONT, DVE_PEER, ACT_FRONT, ACT_PEER = 146, 5, 5, 1

ROW_GMIX, ROW_GQ, ROW_GKV, ROW_GOUT, ROW_CONV, VEC_ROWS = 0, 8, 11, 13, 21, 33

EVENTS = """
value_rows_kept values_turned vec_kept uk_kept state_kept vec_loaded consts_ready uk_loaded sub_loaded
uq_loaded uv_loaded gains_loaded pages_table_loaded vec_turned uk_turned sub_turned zeroed state_loaded
state_turned x_loaded rope_loaded w_used in_ms in_rs x_scaled x_turned xn_kept lat_kept lat_squared lat_summed
lat_ms lat_rs cq_normed kv_normed kr_rotated kr_roped kv_turned kv_rows_kept kv_cols_kept kv_stored zin_kept
z_kept zb_kept conv_done q_projected q_kept qr_rotated q_roped qlat_projected qlat_kept scores_made
scores_masked max_made exp_made probs_made probs_turned_a probs_turned_b probs_kept_a probs_kept_b pv_made
olat_kept attn_projected attn_kept mix_squared mix_summed mix_ms mix_rs mix_normed x1_kept ffn_ms ffn_rs
xn2_made xn2_turned xn2_kept pq_kept key_scores_made key_scores_kept top_keys_done gate_max_made gate_exp_made
picked picked_moved picks_moved u_free v_free gelu_done w_made diag_made residual_in y_ms y_rs y_made y_stored
acc_free score_rows_made score_rows_kept v_free_vector z_tail_turned z_tail_kept conv_stored s_new_made
s_new_kept page_turned page_kept page_scores_made page_scores_kept page_max_made page_gmax page_gmax_spread
page_shifted page_exp page_pv srow_stored srow_loaded s_turned s_slots s_dots s_gelu s_weights dve_front
dve_peer act_front act_peer dve_setup dve_tail
""".split()


def build(nc, a, out):
    with ExitStack() as ctx:
        def sb(name, shape, dt=F32):
            return ctx.enter_context(nc.sbuf_tensor(name, shape, dt))

        on = namedtuple("Events", EVENTS)(*[ctx.enter_context(nc.semaphore(n)) for n in EVENTS])
        w_loaded = [ctx.enter_context(nc.semaphore(f"w_loaded{r}")) for r in range(WR)]
        u_loaded = [ctx.enter_context(nc.semaphore(f"u_loaded{r}")) for r in range(RING)]
        v_loaded = [ctx.enter_context(nc.semaphore(f"v_loaded{r}")) for r in range(RING)]
        pages_loaded = [[ctx.enter_context(nc.semaphore(f"pages_loaded{i}{q}")) for q in range(QUARTERS)] for i in range(2)]

        acc = ctx.enter_context(nc.psum_tensor("acc", [P, 2, 512], F32))
        F = [ctx.enter_context(nc.psum_tensor(f"front{i}", [P, 512], F32)) for i in range(6)]

        ident = sb("ident", [P, P])
        ones = sb("ones", [P, P])
        rot = sb("rot", [ROPE, ROPE])
        low_keys = sb("low_keys", [P, 512])
        q_limit = sb("q_limit", [P, TILES])
        iota16 = sb("iota16", [P, TOPK])
        own_row = sb("own_row", [SB, SB])
        vec_cols = sb("vec_cols", [P, VEC_ROWS])
        g_ffn = sb("g_ffn", [P, D])
        g_fin = sb("g_fin", [P, D])
        w_uq = sb("w_uq", [P, QR // P, H, NOPE + ROPE])
        w_ukT = sb("w_ukT", [P, H, KV])
        w_uv = sb("w_uv", [P, KV // P, H, P])
        sub_keysT = sb("sub_keysT", [P, 2, KEYS])
        w_ring = sb("w_ring", [P, WR, DC, PW])
        ckv_rows = sb("ckv_rows", [P, TILES, KV])
        ckvT = sb("ckvT", [P, 2, SEQ])
        krT = sb("krT", [ROPE, SEQ])
        u_ring = sb("u_ring", [P, RING, D])
        v_ring = sb("v_ring", [P, RING, D])
        diag = sb("diag", [P, RING, P])
        pick_cur = sb("pick_cur", [P, SLOTS], U32)
        pick_next = sb("pick_next", [P, SLOTS], U32)
        gate_cur = sb("gate_cur", [P, SLOTS])
        gate_next = sb("gate_next", [P, SLOTS])
        dots = sb("dots", [P, SLOTS])
        gelu = sb("gelu", [P, SLOTS])
        wgt = sb("wgt", [P, SLOTS])
        xn2_cur = sb("xn2_cur", [P, D])
        rows_next = sb("rows_next", [P, 2, D])
        mo = sb("mo", [P, 2, D])
        x_t = sb("x_t", [P, D])
        work = sb("work", [P, 5 * D])
        cos_t = sb("cos_t", [ROPE, P])
        sin_t = sb("sin_t", [ROPE, P])
        z_ext = sb("z_ext", [P, 4, P + 2])
        z_s = sb("z_s", [P, 4, 3, SB])
        q_ro = sb("q_ro", [ROPE, H, P])
        kr_t = sb("kr_t", [ROPE, 3, P])
        ck_t = sb("ck_t", [P, 2, P])
        kv_rows_t = sb("kv_rows_t", [P, KV + ROPE])
        small = sb("small", [P, 96])
        sv = sb("sv", [P, PH, 2, TOPK])
        si_u = sb("si_u", [P, PH, 2, TOPK], U32)
        si = sb("si", [P, PH, 2, TOPK])
        s_new = sb("s_new", [SB, H * SB])
        page_s = sb("page_s", [P, 4 * (NPAGES + 1)])
        page_p = sb("page_p", [P, 4 * (NPAGES + 1)])
        gm_rows = sb("gm_rows", [H, P])
        s_pick = sb("s_pick", [P, SB], U32)
        s_fan = sb("s_fan", [P, SB, SB])
        page_table_sb = sb("page_table_sb", [1, SB * NPAGES], I32)
        picked_ab = sb("picked_ab", [P, 2, PH, TOPK])

        W = [work[:, k * D:(k + 1) * D] for k in range(5)]
        y_t = W[3]
        zb = W[0][:, 512:1024].rearrange("p (c t) -> p c t", c=4)
        keys_s = W[2][:, 0:2 * KEYS].rearrange("p (c k) -> p c k", c=2)
        pos_f = W[3][:, 4 * SLOTS:6 * SLOTS].rearrange("p (c h k) -> p c h k", c=2, h=PH)
        pos_ab = W[3][:, 6 * SLOTS:8 * SLOTS].bitcast(U32).rearrange("p (c h k) -> p c h k", c=2, h=PH)
        hit = W[0].rearrange("p (h k a) -> p h k a", h=PH // 2, k=TOPK)
        top_s = W[3][:, 2 * SLOTS:3 * SLOTS].rearrange("p (h k) -> p h k", h=PH)
        pos_u = W[3][:, 3 * SLOTS:4 * SLOTS].bitcast(U32).rearrange("p (h k) -> p h k", h=PH)
        x1_next, xn2_next = rows_next[:, 0, :], rows_next[:, 1, :]
        mix_raw, o_lat = mo[:, 0, :], mo[:, 1, :]
        cand = mo[:, :, :].rearrange("p a b -> p (a b)")
        prompt_keys = [ckv_rows[:, :, :], ckvT[:, :, :].rearrange("p c (n r) -> p (c n) r", r=KV)]
        pages_kr = [w_ukT[:, :, :].rearrange("p h (n r) -> p (h n) r", r=ROPE),
                    work[:, NPAGES * KV:NPAGES * (KV + ROPE)].rearrange("p (n r) -> p n r", r=ROPE)]

        def page_rows(b, n):
            if b % 2:
                return work[:, n * KV:(n + 1) * KV]
            return prompt_keys[n // TILES][:, n % TILES, :]

        pages_T = rows_next[:, :, :].rearrange("p a b -> p (a b)")[:, 0:3 * 512].rearrange("p (c k) -> p c k", c=3)

        XN2_PLACE = 3
        SPREAD = [W[0], W[1], W[2], xn2_cur[:, :], W[4], mix_raw, o_lat, x_t[:, :]]

        score_rows = low_keys[0:H, :]
        COLS_SCORES, COLS_SUMS, COLS_VALUES = 256, 256, 384
        value_rows = z_ext[0:H, :, :].rearrange("p c t -> p (c t)")[:, 0:KV]

        stage_uk, stage_sub = u_ring[:, 0, :], u_ring[:, 1, 0:2 * KEYS]
        stage_vec, stage_state = u_ring[0:VEC_ROWS, 2, 0:P], u_ring[0:2 * SB, 3, 0:CW]

        vector_acc = w_uq[:, :, :, :].rearrange("p c h n -> p (c h n)")[:, 0:D]

        all_rows = rows_next[:, :, :].rearrange("p a b -> p (a b)")
        q_lat = all_rows[:, D:2 * D].rearrange("p (c h t) -> p c h t", c=2, h=H)
        q_lat_s = all_rows[:, 3 * 512:3 * 512 + 2 * H * SB].rearrange("p (c h t) -> p c h t", c=2, h=H)

        def small_col(n, w=1, rows=P):
            return small[0:rows, n:n + w]

        (C_SS, C_MS, C_Y, C_T, C_SS2, C_MS2, C_Y2, C_T2, C_SS3, C_MS3, C_Y3, C_T3, C_MAX, C_NMAX,
         C_L, C_RL) = range(16)
        C_PM, C_GM, C_PL, C_PLS, C_LIM = 16, 20, 24, 28, 32
        C_GS, C_GR = 40, 48

        def after(eng, sem, value):
            if isinstance(value, int) and value <= 0:
                return
            eng.wait_ge(sem, value)

        def waited(eng):
            eng.nop(nofuse=True)

        class Own:

            def __init__(self, eng, sem, base):
                self.eng, self.sem, self.base, self.n = eng, sem, base, 0

            def __call__(self, ins, held=False):
                self.n += 1
                ins.then_inc(self.sem, 1)
                self.eng.wait_ge(self.sem, self.base + self.n)
                if held:
                    waited(self.eng)

            def check(self, count):
                assert self.n == count, (self.sem, self.n, count)

        block = ctx.enter_context(nc.Block())

        @block.sync
        def _(sp):
            def load_x(f, T, row=0):
                after(sp, on.x1_kept, f)
                waited(sp)
                src = a["x_prompt"][0, bass.ds(row, P), :] if T == P else a["x_sample"].rearrange("b s d -> (b s) d")
                sp.dma_start(x_t[0:T, :], src).then_inc(on.x_loaded, 16)

            load_x(0, P)
            for dst, src in ((ident, a["c_ident"]), (ones, a["c_ones"]), (rot, a["c_rot"]), (q_limit, a["c_limit"]),
                             (iota16, a["c_iota16"]), (own_row, a["c_own"])):
                sp.dma_start(dst[:], src).then_inc(on.consts_ready, 16)
            r = 0
            for name in ("g_mix_norm", "g_q", "g_kv", "g_attn_out", "g_conv_out"):
                n = a[name].shape[1] // P
                sp.dma_start(stage_vec[r:r + n, :], a[name].rearrange("l (c p) -> (l c) p", p=P)).then_inc(on.vec_loaded, 16)
                r += n
            sp.dma_start(stage_vec[r:r + 12, :], a["conv_w"].rearrange("l k (c p) -> (l k c) p", p=P)).then_inc(on.vec_loaded, 16)
            assert r + 12 == VEC_ROWS

            def load_rope(f, T, row=0):
                after(sp, on.q_roped, f)
                waited(sp)
                sp.dma_start(cos_t[:, 0:T], a["c_rope"][0, :, bass.ds(row, T)]).then_inc(on.rope_loaded, 16)
                sp.dma_start(sin_t[:, 0:T], a["c_rope"][1, :, bass.ds(row, T)]).then_inc(on.rope_loaded, 16)

            w_src = ([(a["w_in"], c) for c in IN_COLS] + [(a["w_o"], c) for c in OUT_COLS]
                     + [(a["w_query"], c) for c in QUERY_COLS])

            def load_w(f, k):
                after(sp, on.w_used, f * PIECES + k - WR + 1)
                src, (c0, n) = w_src[k]
                sp.dma_start(w_ring[:, k % WR, :, 0:n],
                             src[0].rearrange("(c p) n -> p c n", p=P)[:, :, c0:c0 + n]).then_inc(w_loaded[k % WR], 16)

            def load_tile(f, T):
                row = sp.snap(f * P)
                load_x(f, T, row)
                for k in range(PIECES):
                    load_w(f, k)
                    if k == 2:
                        load_rope(f, T, row)

            for k in range(WR):
                load_w(0, k)
            sp.dma_start(page_table_sb[:], a["page_table"].rearrange("b n -> (b n)").unsqueeze(0)).then_inc(on.pages_table_loaded, 16)
            sp.dma_start(stage_state, a["state_conv"].rearrange("l b k c -> (l b k) c"))\
                .then_inc(on.state_loaded, 16)
            sp.dma_start(out["new_conv_sample"][0, :, 0, :], a["state_conv"][0, :, 1, :]).then_inc(on.conv_stored, 16)
            load_rope(0, P)
            sp.dma_start(w_uq[:], a["w_uq"][0].rearrange("(c p) h n -> p c h n", p=P)).then_inc(on.uq_loaded, 16)
            sp.dma_start(stage_uk.rearrange("p (c n) -> p c n", c=2),
                         a["w_uk"][0].rearrange("(c p) h n -> p c (h n)", p=P)).then_inc(on.uk_loaded, 16)
            sp.dma_start(w_uv[:], a["w_uv"][0].rearrange("(c p) h n -> p c h n", p=P)).then_inc(on.uv_loaded, 16)
            sp.dma_start(stage_sub.rearrange("p (c n) -> p c n", c=2),
                         a["sub_keys"][0].rearrange("c k d -> k c d")).then_inc(on.sub_loaded, 16)
            sp.dma_start(low_keys[:], a["c_low"].partition_broadcast(P)).then_inc(on.gains_loaded, 16)
            sp.dma_start(g_ffn[:], a["g_ffn_norm"][0].partition_broadcast(P)).then_inc(on.gains_loaded, 16)
            sp.dma_start(g_fin[:], a["g_final"].partition_broadcast(P)).then_inc(on.gains_loaded, 16)
            for k in range(WR, PIECES):
                load_w(0, k)
            with sp.Fori(1, TILES) as f:
                load_tile(f, P)
            def load_page(b, n, what):
                page = sp.value_load(page_table_sb[0:1, b * NPAGES + n:b * NPAGES + n + 1], min_val=0,
                                     max_val=a["cache_ckv"].shape[1] - 1)
                for dst, src in what:
                    sp.dma_start(dst, a[src][0, bass.ds(page, 1)].rearrange("a k r -> k (a r)"))\
                        .then_inc(pages_loaded[b % 2][n // QP], 16)

            load_x(TILES, SB)
            for k in range(3):
                load_w(TILES, k)
            load_rope(TILES, SB, SEQ)
            sp.wait_ge(on.olat_kept, TILES * H)
            sp.wait_ge(on.pages_table_loaded, 16)
            for n in range(NPAGES):
                load_page(0, n, [(page_rows(0, n), "cache_ckv")])
            for k in range(3, N_IN + WR):
                load_w(TILES, k)
            for event in (on.qlat_kept, on.q_roped, on.conv_done):
                sp.wait_ge(event, TILES + 1)
            sp.wait_ge(on.conv_stored, 3 * 16)
            for n in range(NPAGES):
                load_page(0, n, [(pages_kr[0][:, n, :], "cache_krope")])
            for b in range(1, SB):
                if b >= 2:
                    sp.wait_ge(on.page_pv, b - 1)
                for n in range(NPAGES):
                    load_page(b, n, [(page_rows(b, n), "cache_ckv"), (pages_kr[b % 2][:, n, :], "cache_krope")])
            for k in range(N_IN + WR, PIECES):
                load_w(TILES, k)
            sp.wait_ge(on.picked, TILES + 1)
            sp.dma_start(a["scratch"], xn2_next[0:SB, :]).then_inc(on.srow_stored, 16)
            sp.wait_ge(on.srow_stored, 16)
            for t in sorted(range(SB), key=lambda t: t == XN2_PLACE):
                if t == XN2_PLACE:
                    sp.wait_ge(on.u_free, TILES * SLOTS + RING)
                sp.dma_start(SPREAD[t], a["scratch"][t].partition_broadcast(P)).then_inc(on.srow_loaded, 16)
            sp.wait_ge(on.kv_stored, (TILES + 1) * 2 * 16)
            sp.wait_ge(on.conv_stored, 3 * 16)
            sp.wait_ge(on.y_stored, (TILES + 2) * 16)

        @block.tensor
        def _(pe):
            def weights(f, k):
                pe.wait_ge(w_loaded[k % WR], (f * (PIECES // WR) + k // WR + 1) * 16)
                return w_ring[:, k % WR]

            def project(dst, w, c0, m, xT, T):
                for k in range(DC):
                    last = nc.tensor.matmul(dst, w[:, k, c0:c0 + m], xT[:, k * T:(k + 1) * T],
                                            start=(k == 0), stop=(k == DC - 1))
                return last

            def turn_rows(src, banks, T):
                for c in range(DC):
                    last = nc.tensor.transpose(banks[c // 4][:, (c % 4) * T:(c % 4 + 1) * T],
                                               src[0:T, c * P:(c + 1) * P], ident[0:T, 0:T])
                return last

            def turn_in(f, T):
                pe.wait_ge(on.x_scaled, f + 1)
                turn_rows(W[0], F[0:2], T).then_inc(on.x_turned, 1)

            def proj_lat(f, T):
                xT = W[4]
                pe.wait_ge(on.xn_kept, f + 1)
                for k in range(3):
                    w = weights(f, k)
                    for m in range(2 * k, min(2 * k + 2, 5)):
                        dst = F[2][:, m * T:(m + 1) * T] if m < 3 else F[3][:, (m - 3) * T:(m - 2) * T]
                        last = project(dst, w, (m % 2) * P, P, xT, T)
                    if k < 2:
                        last.then_inc(on.w_used, 1)
                project(F[2][0:ROPE, 3 * T:4 * T], w, P, ROPE, xT, T).then_inc(on.w_used, 1)

            def latent_norm(f, T):
                pe.wait_ge(on.lat_squared, f + 1)
                for c in range(3):
                    nc.tensor.matmul(F[4][:, 0:T], ones[:], W[2][:, c * T:(c + 1) * T], start=(c == 0), stop=(c == 2))
                for c in range(2):
                    last = nc.tensor.matmul(F[4][:, T:2 * T], ones[:], W[2][:, (3 + c) * T:(4 + c) * T],
                                            start=(c == 0), stop=(c == 1))
                last.then_inc(on.lat_summed, 1)
                nc.tensor.matmul(F[5][0:ROPE, 0:T], rot[:], kr_t[:, 0, 0:T], start=True, stop=True)\
                    .then_inc(on.kr_rotated, 1)

            def kv_rows(f, T):
                pe.wait_ge(on.kv_normed, f + 1)
                pe.wait_ge(on.kr_roped, f + 1)
                for c in range(2):
                    nc.tensor.transpose(F[2][0:T, c * P:(c + 1) * P], ck_t[:, c, 0:T], ident[:])
                nc.tensor.transpose(F[2][0:T, KV:KV + ROPE], kr_t[:, 1, 0:T], ident[0:ROPE, 0:ROPE])\
                    .then_inc(on.kv_turned, 1)

            def z_group(f, T, k0, bank):
                for k in range(k0, k0 + 2):
                    w = weights(f, k)
                    for m in range(2):
                        c = 2 * (k - k0) + m
                        last = project(F[bank][:, c * T:(c + 1) * T], w, m * P, P, W[4], T)
                    last.then_inc(on.w_used, 1)

            def conv_gate(f, T):
                z_group(f, T, 7, 5)
                if T != P:
                    pe.wait_ge(on.z_kept, f + 1)
                    for c in range(4):
                        nc.tensor.transpose(F[0][0:SB, c * P:(c + 1) * P], z_s[:, c, 2, :], ident[:])
                    for c in range(4):
                        last = nc.tensor.transpose(F[1][0:2, c * P:(c + 1) * P], z_ext[:, c, 0:2], ident[:])
                    last.then_inc(on.z_tail_turned, 1)

            def q_proj(f, T):
                pe.wait_ge(on.cq_normed, f + 1)
                if T != P:
                    pe.wait_ge(on.z_tail_kept, 1)
                for h in range(H):
                    for c in range(3):
                        nc.tensor.matmul(F[0][:, h * T:(h + 1) * T], w_uq[:, c, h, 0:NOPE], W[1][:, c * T:(c + 1) * T],
                                         start=(c == 0), stop=(c == 2))
                for h in range(H):
                    for c in range(3):
                        last = nc.tensor.matmul(F[1][0:ROPE, h * T:(h + 1) * T], w_uq[:, c, h, NOPE:NOPE + ROPE],
                                                W[1][:, c * T:(c + 1) * T], start=(c == 0), stop=(c == 2))
                last.then_inc(on.q_projected, 1)

            def q_latent(f, T):
                pe.wait_ge(on.q_kept, f + 1)
                pe.wait_ge(on.kv_rows_kept, f + 1)
                waited(pe)
                nc.tensor.matmul(F[2][0:ROPE, 0:4 * T], rot[:], W[4][0:ROPE, 512:512 + 4 * T], start=True, stop=True)\
                    .then_inc(on.qr_rotated, 1)
                pe.wait_ge(on.z_kept, f + 1)
                for c in range(2):
                    for h in range(H):
                        last = nc.tensor.matmul(F[3 + c][:, h * T:(h + 1) * T], w_ukT[:, h, c * P:(c + 1) * P],
                                                W[4][:, h * T:(h + 1) * T], start=True, stop=True)
                last.then_inc(on.qlat_projected, 1)

            def head_start(f, h):
                n = f * H + h
                if h == 0:
                    pe.wait_ge(on.qlat_kept, f + 1)
                    pe.wait_ge(on.q_roped, f + 1)
                    pe.wait_ge(on.kv_cols_kept, f + 1)
                else:
                    pe.wait_ge(on.scores_masked, n)
                for half in range(2):
                    ks = slice(half * 512, half * 512 + 512)
                    for c in range(2):
                        nc.tensor.matmul(F[half][:, :], q_lat[:, c, h, :], ckvT[:, c, ks], start=(c == 0), stop=False)
                    last = nc.tensor.matmul(F[half][:, :], q_ro[:, h, :], krT[:, ks], start=False, stop=True)
                last.then_inc(on.scores_made, 1)

            def head_end(f, h):
                n = f * H + h
                pe.wait_ge(on.probs_made, n + 1)
                for j in range(4):
                    last = nc.tensor.transpose(F[2][:, j * P:(j + 1) * P], W[0][:, j * P:(j + 1) * P], ident[:])
                last.then_inc(on.probs_turned_a, 1)
                for j in range(4):
                    last = nc.tensor.transpose(F[3][:, j * P:(j + 1) * P], W[0][:, (4 + j) * P:(5 + j) * P], ident[:])
                last.then_inc(on.probs_turned_b, 1)

            def head_values(f, h):
                n = f * H + h
                pe.wait_ge(on.probs_kept_a, n + 1)
                pe.wait_ge(on.probs_kept_b, n + 1)
                for c in range(2):
                    for j in range(TILES):
                        last = nc.tensor.matmul(F[4][:, c * P:(c + 1) * P], ckv_rows[:, j, c * P:(c + 1) * P],
                                                W[1][:, j * P:(j + 1) * P], start=(j == 0), stop=(j == TILES - 1))
                last.then_inc(on.pv_made, 1)

            def attn_out(f, T):
                pe.wait_ge(on.olat_kept, (f + 1) * H if T == P else TILES * H + SB)
                pe.wait_ge(on.zb_kept, f + 1)
                for h in range(H):
                    for c in range(2):
                        last = nc.tensor.matmul(F[5][:, h * T:(h + 1) * T], w_uv[:, c, h, :],
                                                o_lat[:, (c * H + h) * T:(c * H + h + 1) * T],
                                                start=(c == 0), stop=(c == 1))
                last.then_inc(on.attn_projected, 1)

            def mix_norm(f, T):
                pe.wait_ge(on.mix_squared, f + 1)
                for half in range(2):
                    last = nc.tensor.matmul(F[half][:, 0:4 * T], ones[:], W[0][:, half * 4 * T:(half + 1) * 4 * T],
                                            start=True, stop=True)
                last.then_inc(on.mix_summed, 1)

            def mix_out(f, T):
                pe.wait_ge(on.mix_normed, f + 1)
                for j in range(N_OUT):
                    w = weights(f, N_IN + j)
                    dst = F[2 + j // 2][0:T, (j % 2) * 256:(j % 2) * 256 + 256]
                    for k in range(DC):
                        last = nc.tensor.matmul(dst, W[2][:, k * T:(k + 1) * T], w[:, k, :],
                                                start=(k == 0), stop=(k == DC - 1))
                    last.then_inc(on.w_used, 1)

            def ffn_turn(f, T):
                pe.wait_ge(on.xn2_made, f + 1)
                turn_rows(xn2_next, F[4:6], T).then_inc(on.xn2_turned, 1)

            def query_start(f, T, h):
                n = f * PH + h
                if h == 0:
                    pe.wait_ge(on.xn2_kept, f + 1)
                else:
                    pe.wait_ge(on.pq_kept, n)
                w = weights(f, N_IN + N_OUT + h)
                for c in range(2):
                    last = project(F[0][:, c * T:(c + 1) * T], w, c * P, P, W[4], T)
                last.then_inc(on.w_used, 1)

            def query_end(f, T, h):
                n = f * PH + h
                pe.wait_ge(on.pq_kept, n + 1)
                if h:
                    pe.wait_ge(on.key_scores_kept, n)
                for c in range(2):
                    last = nc.tensor.matmul(F[1][0:T, c * KEYS:(c + 1) * KEYS], W[3][:, c * T:(c + 1) * T],
                                            sub_keysT[:, c, :], start=True, stop=True)
                last.then_inc(on.key_scores_made, 1)

            def page_scores(n):
                b, q = divmod(n, QUARTERS)
                pe.wait_ge(on.page_kept, 2 * (n + 1))
                for c in range(2):
                    nc.tensor.matmul(F[3][0:H, :], q_lat_s[:, c, :, b], pages_T[:, c, :], start=(c == 0), stop=False)
                nc.tensor.matmul(F[3][0:H, :], q_ro[:, :, b], pages_T[0:ROPE, 2, :], start=False, stop=True)\
                    .then_inc(on.score_rows_made, 1)

            def page_scores_turn(n):
                b, q = divmod(n, QUARTERS)
                pe.wait_ge(on.score_rows_kept, n + 1)
                if q == 0 and b:
                    pe.wait_ge(on.page_scores_kept, b)
                for pg in range(QP):
                    col = COLS_SCORES + 4 * (q * QP + pg)
                    last = nc.tensor.transpose(F[4][:, col:col + 4], score_rows[:, pg * P:(pg + 1) * P], ident[0:H, 0:H])
                last.then_inc(on.page_scores_made, 1)

            def page_turn(n):
                b, q = divmod(n, QUARTERS)
                pe.wait_ge(pages_loaded[b % 2][q], (b // 2 + 1) * 2 * QP * 16)
                for pg in range(QP):
                    for c in range(2):
                        nc.tensor.transpose(F[c][:, pg * P:(pg + 1) * P], page_rows(b, q * QP + pg)[:, c * P:(c + 1) * P], ident[:])
                    last = nc.tensor.transpose(F[2][0:ROPE, pg * P:(pg + 1) * P], pages_kr[b % 2][:, q * QP + pg, :], ident[:])
                last.then_inc(on.page_turned, 1)

            def own_key_scores(f):
                pe.wait_ge(on.qlat_kept, f + 1)
                pe.wait_ge(on.q_roped, f + 1)
                for c in range(2):
                    nc.tensor.matmul(F[5][0:SB, 0:4 * SB], ck_t[:, c, 0:SB],
                                     q_lat_s[:, c, :, :], start=(c == 0), stop=False)
                nc.tensor.matmul(F[5][0:SB, 0:4 * SB], kr_t[:, 1, 0:SB], q_ro[:, :, 0:SB],
                                 start=False, stop=True).then_inc(on.s_new_made, 1)

            def page_values(b):
                pe.wait_ge(on.page_exp, b + 1)
                nc.tensor.matmul(F[5][:, COLS_SUMS:COLS_SUMS + 4 * (NPAGES + 1)], ones[:], page_p[:], start=True, stop=True)
                for n in range(NPAGES):
                    nc.tensor.matmul(F[5][0:H, 0:KV], page_p[:, 4 * n:4 * n + 4], page_rows(b, n), start=(n == 0), stop=False)
                last = nc.tensor.matmul(F[5][0:H, 0:KV], page_p[0:SB, 4 * NPAGES:4 * NPAGES + 4], kv_rows_t[0:SB, 0:KV],
                                        start=False, stop=True)
                last.then_inc(on.page_pv, 1)

            def pages_stage(f, n):
                b, q = divmod(n, QUARTERS)
                if n == 0:
                    own_key_scores(f)
                if q == 1 and b:
                    pe.wait_ge(on.page_max_made, 2 * b - 1)
                    nc.tensor.transpose(F[5][0:H, 0:P], small_col(C_PM, 4), ident[:]).then_inc(on.page_gmax, 1)
                if 0 < n <= SB * QUARTERS:
                    page_scores(n - 1)
                if n < SB * QUARTERS:
                    page_turn(n)
                if q == 1 and b:
                    pe.wait_ge(on.page_max_made, 2 * b)
                    nc.tensor.matmul(F[5][:, 128:132], gm_rows[:], ident[0:H, 0:H], start=True, stop=True)\
                        .then_inc(on.page_gmax_spread, 1)
                if 0 < n <= SB * QUARTERS:
                    page_scores_turn(n - 1)
                if q == 2 and b:
                    page_values(b - 1)
                if q == 3 and b:
                    pe.wait_ge(on.value_rows_kept, b)
                    for c in range(2):
                        last = nc.tensor.transpose(F[5][:, COLS_VALUES + 4 * c:COLS_VALUES + 4 * c + 4],
                                                   value_rows[:, c * P:(c + 1) * P], ident[0:H, 0:H])
                    last.then_inc(on.values_turned, 1)

            def v_group(it, g):
                for r in range(G):
                    slot = (g % 2) * G + r
                    if by_vector(it, g * G + r):
                        continue
                    pe.wait_ge(on.diag_made, tensor_slots(it, g * G + r))
                    pe.wait_ge(v_loaded[slot], (it * (GROUPS // 2) + g // 2 + 1) * 16)
                    for half in range(2):
                        last = nc.tensor.matmul(acc[:, half, :], diag[:, slot, :], v_ring[:, slot, half * 512:half * 512 + 512],
                                                start=False, stop=(g == GROUPS - 1 and (r == G - 1 or by_vector(it, g * G + r + 1))))
                    last.then_inc(on.v_free, 1)

            def residual(f):
                after(pe, on.acc_free, f)
                pe.wait_ge(on.x1_kept, f + 1)
                for half in range(2):
                    last = nc.tensor.matmul(acc[:, half, :], ident[:], x1_next[:, half * 512:half * 512 + 512],
                                            start=True, stop=False)
                last.then_inc(on.residual_in, 1)

            def stage(f, T, name, n):
                if name == "turn":
                    turn_in(f, T)
                elif name == "latent":
                    proj_lat(f, T)
                elif name == "latent_norm":
                    latent_norm(f, T)
                elif name == "kv_rows":
                    kv_rows(f, T)
                elif name == "z_in":
                    z_group(f, T, 3, 3)
                elif name == "z_gate":
                    z_group(f, T, 5, 4)
                elif name == "conv":
                    conv_gate(f, T)
                elif name == "q_proj":
                    q_proj(f, T)
                elif name == "q_latent":
                    q_latent(f, T)
                elif name == "head":
                    if n > 0:
                        head_end(f, n - 1)
                    if n < H:
                        head_start(f, n)
                    if n > 0:
                        head_values(f, n - 1)
                elif name == "pages":
                    pages_stage(f, n)
                elif name == "attn":
                    attn_out(f, T)
                elif name == "mix_norm":
                    mix_norm(f, T)
                elif name == "mix_out":
                    mix_out(f, T)
                elif name == "ffn_turn":
                    ffn_turn(f, T)
                elif name == "query":
                    if n > 0:
                        query_end(f, T, n - 1)
                    if n < PH:
                        query_start(f, T, n)

            def turn_picks():
                pe.wait_ge(on.picked, TILES + 1)
                nc.tensor.transpose(F[0][:, 0:SB], picked_ab[0:SB, 0, :, :].rearrange("p h k -> p (h k)"), ident[0:SB, 0:SB])
                nc.tensor.transpose(F[0][:, SB:2 * SB], gate_next[0:SB, :], ident[0:SB, 0:SB]).then_inc(on.s_turned, 1)

            def tile(it, T):
                for g in range(GROUPS):
                    stages = beside(g, T)
                    before = 1 if has_pages(stages) else len(stages)
                    for name, n in stages[:before]:
                        stage(it + 1, T, name, n)
                    if T != P and g == GROUPS - 1:
                        turn_picks()
                    v_group(it, g)
                    for name, n in stages[before:]:
                        stage(it + 1, T, name, n)

            def turn_weights():
                pe.wait_ge(on.uk_loaded, 16)
                pe.wait_ge(on.vec_kept, 1)
                for h in range(H):
                    for c in range(2):
                        last = nc.tensor.transpose(acc[:, h // 2, (h % 2) * KV + c * P:(h % 2) * KV + (c + 1) * P],
                                                   stage_uk[:, c * 512 + h * P:c * 512 + (h + 1) * P], ident[:])
                last.then_inc(on.uk_turned, 1)

            def turn_keys():
                pe.wait_ge(on.uk_kept, 1)
                pe.wait_ge(on.sub_loaded, 16)
                for c in range(2):
                    last = nc.tensor.transpose(acc[:, 0, c * P:(c + 1) * P], stage_sub[:, c * P:(c + 1) * P], ident[:])
                last.then_inc(on.sub_turned, 1)
                pe.wait_ge(on.state_loaded, 16)
                for c in range(4):
                    last = nc.tensor.transpose(acc[:, 1, c * 2 * SB:(c + 1) * 2 * SB], stage_state[:, c * P:(c + 1) * P],
                                               ident[0:2 * SB, 0:2 * SB])
                last.then_inc(on.state_turned, 1)
                pe.wait_ge(on.uq_loaded, 16)
                pe.wait_ge(on.uv_loaded, 16)

            pe.wait_ge(on.consts_ready, 6 * 16)
            pe.wait_ge(on.vec_loaded, 6 * 16)
            nc.tensor.transpose(acc[:, 0, 0:VEC_ROWS], stage_vec, ident[0:VEC_ROWS, 0:VEC_ROWS]).then_inc(on.vec_turned, 1)
            for name, n in stages_of(P):
                stage(0, P, name, n)
                if name == "latent":
                    turn_weights()
                elif name == "kv_rows":
                    turn_keys()
            pe.wait_ge(on.state_kept, 1)
            residual(0)
            with pe.Fori(0, TILES - 1) as it:
                tile(it, P)
                residual(it + 1)
            tile(TILES - 1, SB)
            pe.wait_ge(on.acc_free, TILES)
            for half in range(2):
                nc.tensor.matmul(acc[0:SB, half, :], ident[0:SB, 0:SB], x1_next[0:SB, half * 512:half * 512 + 512],
                                 start=True, stop=False)
            pe.wait_ge(on.s_weights, 1)
            for t in range(SB):
                pe.wait_ge(v_loaded[t], (TILES * (GROUPS // 2) + 1) * 16)
                for half in range(2):
                    last = nc.tensor.matmul(acc[0:SB, half, :], s_fan[:, t, :], v_ring[:, t, half * 512:half * 512 + 512],
                                            start=False, stop=(t == SB - 1))
            last.then_inc(on.v_free, 1)

        @block.scalar
        def _(act):
            def rsqrt_start(own, dst, ms):
                own(nc.scalar.activation(dst, ms, ACT.Ln))
                return nc.scalar.activation(dst, dst, ACT.Exp, scale=-0.5)

            def stage(own, f, T, name, n):
                if name == "norm":
                    act.wait_ge(on.in_ms, f + 1)
                    rsqrt_start(own, small_col(C_Y, 1, T), small_col(C_MS, 1, T)).then_inc(on.in_rs, 1)
                elif name == "latent":
                    act.wait_ge(on.w_used, f * PIECES + 3)
                    nc.scalar.copy(W[1][:, 0:3 * T], F[2][:, 0:3 * T])
                    nc.scalar.copy(W[1][:, 3 * T:5 * T], F[3][:, 0:2 * T])
                    nc.scalar.copy(kr_t[:, 0, 0:T], F[2][0:ROPE, 3 * T:4 * T]).then_inc(on.lat_kept, 1)
                elif name == "latent_norm":
                    act.wait_ge(on.lat_ms, f + 1)
                    rsqrt_start(own, W[3][:, 256:256 + 2 * T], W[3][:, 0:2 * T]).then_inc(on.lat_rs, 1)
                elif name == "kv_rows":
                    act.wait_ge(on.kv_turned, f + 1)
                    after(act, on.kv_stored, f * 2 * 16)
                    own(nc.scalar.copy(kv_rows_t[0:T, :], F[2][0:T, 0:KV + ROPE]))
                    if T == P:
                        if isinstance(f, int):
                            act.wait_ge(on.zeroed, 3)
                        nc.scalar.copy(ckv_rows[:, bass.ds(f, 1), :].rearrange("p a r -> p (a r)"), F[2][:, 0:KV])\
                            .then_inc(on.kv_rows_kept, 1)
                        nc.scalar.copy(ckvT[:, :, bass.ds(f * P, P)], ck_t[:, :, :])
                        nc.scalar.copy(krT[:, bass.ds(f * P, P)], kr_t[:, 1, :]).then_inc(on.kv_cols_kept, 1)
                        ckv_out, kr_out = out["new_ckv_prompt"][0, 0, bass.ds(f * P, P)], out["new_krope_prompt"][0, 0, bass.ds(f * P, P)]
                    else:
                        nc.scalar.copy(page_s[0:1, 0:1], ones[0:1, 0:1]).then_inc(on.kv_rows_kept, 1)
                        ckv_out = out["new_ckv_sample"].rearrange("l b s r -> (l b s) r")
                        kr_out = out["new_krope_sample"].rearrange("l b s r -> (l b s) r")
                    act.dma_start(ckv_out, kv_rows_t[0:T, 0:KV]).then_inc(on.kv_stored, 16)
                    act.dma_start(kr_out, kv_rows_t[0:T, KV:KV + ROPE]).then_inc(on.kv_stored, 16)
                elif name == "z_in":
                    act.wait_ge(on.w_used, f * PIECES + 5)
                    nc.scalar.copy(W[0][:, 0:4 * T], F[3][:, 0:4 * T]).then_inc(on.zin_kept, 1)
                elif name == "conv":
                    act.wait_ge(on.w_used, f * PIECES + 9)
                    nc.scalar.copy(zb[:, :, 0:T], F[5][:, 0:4 * T].rearrange("p (c t) -> p c t", c=4)).then_inc(on.zb_kept, 1)
                    if T != P:
                        act.wait_ge(on.z_tail_turned, 1)
                        act.wait_ge(on.conv_done, f + 1)
                        own(nc.scalar.copy(W[3][0:SB, 0:CW], F[0][0:SB, :]))
                        nc.scalar.copy(W[3][0:2, CW:2 * CW], F[1][0:2, :]).then_inc(on.z_tail_kept, 1)
                        act.wait_ge(on.z_tail_kept, 1)
                        act.dma_start(out["new_conv_sample"][0, :, 1, :], W[3][0:SB, 0:CW]).then_inc(on.conv_stored, 16)
                        act.dma_start(out["new_conv_prompt"][0, 0], W[3][0:2, CW:2 * CW]).then_inc(on.conv_stored, 16)
                elif name == "q_proj":
                    act.wait_ge(on.q_projected, f + 1)
                    nc.scalar.copy(W[4][:, 0:4 * T], F[0][:, 0:4 * T])
                    nc.scalar.copy(W[4][0:ROPE, 512:512 + 4 * T], F[1][0:ROPE, 0:4 * T]).then_inc(on.q_kept, 1)
                elif name == "q_latent":
                    act.wait_ge(on.qlat_projected, f + 1)
                    for c in range(2):
                        last = nc.scalar.copy((q_lat if T == P else q_lat_s)[:, c, :, :], F[3 + c][:, 0:4 * T].rearrange("p (h t) -> p h t", h=H))
                    last.then_inc(on.qlat_kept, 1)
                elif name == "head":
                    if n > 0:
                        act.wait_ge(on.probs_turned_b, f * H + n)
                        nc.scalar.copy(W[1][:, 512:1024], F[3][:, :]).then_inc(on.probs_kept_b, 1)
                    if n < H:
                        act.wait_ge(on.max_made, f * H + n + 1)
                        nc.scalar.activation(W[0], W[0], ACT.Exp, bias=small_col(C_NMAX), scale=SCALE,
                                             accum_out=small_col(C_L)).then_inc(on.exp_made, 1)
                    if n > 0:
                        act.wait_ge(on.pv_made, f * H + n)
                        nc.scalar.copy(o_lat.rearrange("p (c h t) -> p c h t", c=2, h=H)[:, :, n - 1, :],
                                       F[4][:, 0:2 * P].rearrange("p (c t) -> p c t", c=2)).then_inc(on.olat_kept, 1)
                elif name == "pages":
                    b, q = divmod(n, QUARTERS)
                    if 0 < n <= SB * QUARTERS:
                        act.wait_ge(on.score_rows_made, n)
                        nc.scalar.copy(score_rows, F[3][0:H, :]).then_inc(on.score_rows_kept, 1)
                    if n < SB * QUARTERS:
                        act.wait_ge(on.page_turned, n + 1)
                        nc.scalar.copy(pages_T[:, 0, :], F[0][:, :]).then_inc(on.page_kept, 1)
                    if q == 1 and b:
                        act.wait_ge(on.page_shifted, b)
                        nc.scalar.activation(page_p[:], page_s[:], ACT.Exp, scale=SCALE).then_inc(on.page_exp, 1)
                    if q == 2 and b:
                        act.wait_ge(on.page_pv, b)
                        nc.scalar.copy(value_rows, F[5][0:H, 0:KV]).then_inc(on.value_rows_kept, 1)
                elif name == "attn":
                    act.wait_ge(on.attn_projected, f + 1)
                    nc.scalar.copy(mix_raw[:, 0:4 * T], F[5][:, 0:4 * T]).then_inc(on.attn_kept, 1)
                elif name == "mix_norm":
                    act.wait_ge(on.mix_ms, f + 1)
                    rsqrt_start(own, W[1][:, 0:8 * T], W[0][:, 0:8 * T]).then_inc(on.mix_rs, 1)
                elif name == "ffn_norm":
                    act.wait_ge(on.ffn_ms, f + 1)
                    rsqrt_start(own, small_col(C_Y2, 1, T), small_col(C_MS2, 1, T)).then_inc(on.ffn_rs, 1)
                elif name == "query":
                    if n > 0:
                        act.wait_ge(on.key_scores_made, f * PH + n)
                        after(act, on.top_keys_done, f * PH + n - 1)
                        nc.scalar.copy(keys_s[0:T].rearrange("p c k -> p (c k)"), F[1][0:T, 0:2 * KEYS])\
                            .then_inc(on.key_scores_kept, 1)
                    if n < PH:
                        act.wait_ge(on.w_used, f * PIECES + N_IN + N_OUT + n + 1)
                        nc.scalar.copy(W[3][:, 0:2 * T], F[0][:, 0:2 * T]).then_inc(on.pq_kept, 1)
                elif name == "select" and n == 1:
                    act.wait_ge(on.gate_max_made, f + 1)
                    nc.scalar.activation(gate_next[0:T, :], gate_next[0:T, :], ACT.Exp).then_inc(on.gate_exp_made, 1)

            def gelu_group(it, g):
                act.wait_ge(on.u_free, it * SLOTS + (g + 1) * G + RING)
                nc.scalar.activation(gelu[:, g * G:(g + 1) * G], dots[:, g * G:(g + 1) * G], ACT.Gelu).then_inc(on.gelu_done, 1)

            def diag_group(it, g):
                act.wait_ge(on.w_made, it * GROUPS + g + 1)
                act.wait_ge(on.v_free, RING + tensor_slots(it, (g - 1) * G - 1))
                for s in range(g * G, (g + 1) * G):
                    if by_vector(it, s):
                        continue
                    nc.scalar.activation(diag[:, s % RING, :], ident[:], ACT.Copy, scale=wgt[:, s:s + 1]).then_inc(on.diag_made, 1)

            def finalize(own, it, T):
                act.wait_ge(on.y_ms, it + 1)
                rsqrt_start(own, small_col(C_Y3, 1, T), small_col(C_MS3, 1, T)).then_inc(on.y_rs, 1)
                act.wait_ge(on.y_made, it + 1)
                dst = out["y_prompt"][0, bass.ds(it * P, P)] if T == P else out["y_sample"].rearrange("b s d -> (b s) d")
                act.dma_start(dst, y_t[0:T, :]).then_inc(on.y_stored, 16)

            def tile(it, T):
                own = Own(act, on.act_front, (it + 1) * ACT_FRONT)
                gelu_group(it, 0)
                for g in range(GROUPS):
                    if T == P and g + 1 < GROUPS:
                        gelu_group(it, g + 1)
                    diag_group(it, g)
                    for name, n in beside(g, T):
                        stage(own, it + 1, T, name, n)
                    if T != P and g + 1 < GROUPS:
                        gelu_group(it, g + 1)
                if T == P:
                    own.check(ACT_FRONT)
                own2 = Own(act, on.act_peer, it * ACT_PEER)
                finalize(own2, it, P)
                own2.check(ACT_PEER)

            own = Own(act, on.act_front, 0)
            act.wait_ge(on.consts_ready, 6 * 16)
            for name, n in stages_of(P):
                stage(own, 0, P, name, n)
            own.check(ACT_FRONT)
            with act.Fori(0, TILES - 1) as it:
                tile(it, P)
            tile(TILES - 1, SB)
            act.wait_ge(on.s_dots, SB)
            nc.scalar.activation(gelu[:, 0:SB], dots[:, 0:SB], ACT.Gelu).then_inc(on.s_gelu, 1)
            finalize(Own(act, on.act_peer, TILES * ACT_PEER), TILES, SB)

        @block.vector
        def _(dve):
            v = nc.vector

            def sharpen(own, ms, y, t):
                own(v.tensor_tensor(t, ms, y, ALU.mult))
                own(v.scalar_tensor_tensor(out=t, in0=t, scalar=-0.5, in1=y, op0=ALU.mult, op1=ALU.mult))
                own(v.scalar_tensor_tensor(out=y, in0=t, scalar=1.5, in1=y, op0=ALU.add, op1=ALU.mult))

            def mean(dst, total, n):
                return v.tensor_scalar(dst, total, 1.0 / n, EPS, ALU.mult, ALU.add)

            def spread_cols(first, n, T):
                return vec_cols[:, first:first + n].unsqueeze(2).to_broadcast([P, n, T])

            def split(ap, c):
                return ap.rearrange("p (c t) -> p c t", c=c)

            def norm_in(own, f, T):
                dve.wait_ge(on.x_loaded, (f + 1) * 16)
                own(v.tensor_tensor_reduce(W[0][0:T, :], x_t[0:T, :], x_t[0:T, :], 1.0, 0.0, ALU.mult, ALU.add, small_col(C_SS, 1, T)))
                mean(small_col(C_MS, 1, T), small_col(C_SS, 1, T), D).then_inc(on.in_ms, 1)
                dve.wait_ge(on.in_rs, f + 1)
                sharpen(own, small_col(C_MS, 1, T), small_col(C_Y, 1, T), small_col(C_T, 1, T))
                v.tensor_scalar(W[0][0:T, :], x_t[0:T, :], small_col(C_Y, 1, T), None, ALU.mult).then_inc(on.x_scaled, 1)

            def keep_turned(f, T):
                dve.wait_ge(on.x_turned, f + 1)
                for half in range(2):
                    last = v.tensor_tensor(split(W[4][:, half * 4 * T:(half + 1) * 4 * T], 4), split(F[half][:, 0:4 * T], 4),
                                           spread_cols(ROW_GMIX + 4 * half, 4, T), ALU.mult)
                last.then_inc(on.xn_kept, 1)

            def square_latents(f, T):
                dve.wait_ge(on.lat_kept, f + 1)
                v.tensor_tensor(W[2][:, 0:5 * T], W[1][:, 0:5 * T], W[1][:, 0:5 * T], ALU.mult).then_inc(on.lat_squared, 1)

            def latents(own, f, T):
                dve.wait_ge(on.lat_summed, f + 1)
                after(dve, on.y_stored, f * 16)
                mean(W[3][:, 0:T], F[4][:, 0:T], QR)
                mean(W[3][:, T:2 * T], F[4][:, T:2 * T], KV).then_inc(on.lat_ms, 1)
                dve.wait_ge(on.kr_rotated, f + 1)
                dve.wait_ge(on.rope_loaded, (f + 1) * 2 * 16)
                own(v.tensor_tensor(kr_t[:, 1, 0:T], kr_t[:, 0, 0:T], cos_t[:, 0:T], ALU.mult))
                own(v.tensor_tensor(kr_t[:, 2, 0:T], F[5][0:ROPE, 0:T], sin_t[:, 0:T], ALU.mult))
                v.tensor_tensor(kr_t[:, 1, 0:T], kr_t[:, 1, 0:T], kr_t[:, 2, 0:T], ALU.add).then_inc(on.kr_roped, 1)
                dve.wait_ge(on.lat_ms, f + 1)
                dve.wait_ge(on.lat_rs, f + 1)
                rs = W[3][:, 256:256 + 2 * T]
                sharpen(own, W[3][:, 0:2 * T], rs, W[3][:, 512:512 + 2 * T])
                for c in range(5):
                    dst = W[1][:, c * T:(c + 1) * T] if c < 3 else ck_t[:, c - 3, 0:T]
                    last = v.scalar_tensor_tensor(out=dst, in0=W[1][:, c * T:(c + 1) * T], scalar=vec_cols[:, ROW_GQ + c:ROW_GQ + c + 1],
                                                  in1=rs[:, 0:T] if c < 3 else rs[:, T:2 * T], op0=ALU.mult, op1=ALU.mult)
                    if c == 2:
                        last.then_inc(on.cq_normed, 1)
                last.then_inc(on.kv_normed, 1)

            def conv_in(own, f, T):
                dve.wait_ge(on.zin_kept, f + 1)
                dve.wait_ge(on.w_used, f * PIECES + 7)
                v.tensor_tensor(z_ext[:, :, 2:2 + P] if T == P else z_s[:, :, 2, :], split(F[4][:, 0:4 * T], 4),
                                split(W[0][:, 0:4 * T], 4), ALU.mult).then_inc(on.z_kept, 1)
                dve.wait_ge(on.z_kept, f + 1)

            def conv(own, f, T):
                steps = [z_ext[:, :, k:k + P] for k in range(3)] if T == P else [z_s[:, :, k, :] for k in range(3)]
                y, t = split(W[3][:, 0:4 * T], 4), split(W[2][:, 0:4 * T], 4)
                own(v.tensor_tensor(y, steps[0], spread_cols(ROW_CONV, 4, T), ALU.mult))
                for k in (1, 2):
                    own(v.tensor_tensor(t, steps[k], spread_cols(ROW_CONV + 4 * k, 4, T), ALU.mult))
                    own(v.tensor_tensor(y, y, t, ALU.add))
                dve.wait_ge(on.zb_kept, f + 1)
                v.tensor_tensor(split(mix_raw[:, 4 * T:8 * T], 4), y, zb[:, :, 0:T], ALU.mult).then_inc(on.conv_done, 1)
                dve.wait_ge(on.conv_done, f + 1)
                if T == P:
                    own(v.tensor_copy(z_ext[:, :, 0:2], z_ext[:, :, P:P + 2]))

            def q_rope(own, f, T):
                dve.wait_ge(on.q_kept, f + 1)
                raw = split(W[4][0:ROPE, 512:512 + 4 * T], 4)
                t = split(W[2][0:ROPE, 0:4 * T], 4)
                c4 = cos_t[:, 0:T].unsqueeze(1).to_broadcast([ROPE, H, T])
                s4 = sin_t[:, 0:T].unsqueeze(1).to_broadcast([ROPE, H, T])
                own(v.tensor_tensor(q_ro[:, :, 0:T], raw, c4, ALU.mult))
                dve.wait_ge(on.qr_rotated, f + 1)
                own(v.tensor_tensor(t, split(F[2][0:ROPE, 0:4 * T], 4), s4, ALU.mult))
                v.tensor_tensor(q_ro[:, :, 0:T], q_ro[:, :, 0:T], t, ALU.add).then_inc(on.q_roped, 1)

            def head_start(own, f, h):
                n = f * H + h
                if h == 0:
                    own(v.tensor_copy(small_col(C_LIM), q_limit[:, bass.ds(f, 1)]))
                    own(v.tensor_scalar(small_col(C_LIM + 1), small_col(C_LIM), -512 * BIG, None, ALU.add))
                dve.wait_ge(on.scores_made, n + 1)
                for half in range(2):
                    last = v.scalar_tensor_tensor(out=W[0][:, half * 512:half * 512 + 512], in0=low_keys[:],
                                                  scalar=small_col(C_LIM + half), in1=F[half][:, :], op0=ALU.add, op1=ALU.min)
                last.then_inc(on.scores_masked, 1)
                dve.wait_ge(on.scores_masked, n + 1)
                own(v.tensor_reduce(small_col(C_MAX), W[0], AX.X, ALU.max))
                v.tensor_scalar(small_col(C_NMAX), small_col(C_MAX), -SCALE, None, ALU.mult).then_inc(on.max_made, 1)
                dve.wait_ge(on.exp_made, n + 1)
                own(v.reciprocal(small_col(C_RL), small_col(C_L)))
                v.tensor_scalar(W[0], W[0], small_col(C_RL), None, ALU.mult).then_inc(on.probs_made, 1)

            def head_end(own, f, h):
                n = f * H + h
                dve.wait_ge(on.probs_turned_a, n + 1)
                v.tensor_copy(W[1][:, 0:512], F[2][:, :]).then_inc(on.probs_kept_a, 1)

            def pages_stage(own, n):
                b, q = divmod(n, QUARTERS)
                if n == 0:
                    dve.wait_ge(on.s_new_made, 1)
                    v.tensor_copy(s_new[:], F[5][0:SB, 0:4 * SB]).then_inc(on.s_new_kept, 1)
                    dve.wait_ge(on.s_new_kept, 1)
                if q == 1 and b:
                    dve.wait_ge(on.page_gmax, b)
                    own(v.tensor_reduce(small_col(C_GM, 1, H), F[5][0:H, 0:P], AX.X, ALU.max))
                    v.tensor_scalar(gm_rows[:], ones[0:H, :], small_col(C_GM, 1, H), None, ALU.mult).then_inc(on.page_max_made, 1)
                if n < SB * QUARTERS:
                    dve.wait_ge(on.page_turned, n + 1)
                    v.tensor_copy(pages_T[:, 1, :], F[1][:, :])
                    v.tensor_copy(pages_T[0:ROPE, 2, :], F[2][0:ROPE, :]).then_inc(on.page_kept, 1)
                if q == 0 and b:
                    own(v.memset(page_s[:, 4 * NPAGES:], -BIG))
                    own(v.tensor_scalar(page_s[0:SB, 4 * NPAGES:], s_new[:, b - 1:4 * SB:SB], own_row[:, b - 1:b], None, ALU.add))
                    dve.wait_ge(on.page_scores_made, QUARTERS * b)
                    v.tensor_copy(page_s[:, 0:4 * NPAGES], F[4][:, COLS_SCORES:COLS_SCORES + 4 * NPAGES]).then_inc(on.page_scores_kept, 1)
                    dve.wait_ge(on.page_scores_kept, b)
                    v.tensor_reduce(small_col(C_PM, 4), page_s[:].rearrange("p (n h) -> p h n", h=H), AX.X, ALU.max)\
                        .then_inc(on.page_max_made, 1)
                if q == 1 and b:
                    dve.wait_ge(on.page_gmax_spread, b)
                    s3 = page_s[:].rearrange("p (n h) -> p n h", h=H)
                    v.tensor_tensor(s3, s3, F[5][:, 128:132].unsqueeze(1).to_broadcast([P, NPAGES + 1, H]), ALU.subtract)\
                        .then_inc(on.page_shifted, 1)
                if q == 3 and b:
                    dve.wait_ge(on.values_turned, b)
                    own(v.tensor_reduce(small_col(C_PL, 4), F[5][:, COLS_SUMS:COLS_SUMS + 4 * (NPAGES + 1)].rearrange("p (n h) -> p h n", h=H),
                                        AX.X, ALU.add))
                    own(v.reciprocal(small_col(C_PLS, 4), small_col(C_PL, 4)))
                    v.tensor_tensor(o_lat[:, 0:2 * H * SB].rearrange("p (c h t) -> p c h t", c=2, h=H)[:, :, :, b - 1],
                                    F[5][:, COLS_VALUES:COLS_VALUES + 2 * H].rearrange("p (c h) -> p c h", c=2),
                                    small_col(C_PLS, 4).unsqueeze(1).to_broadcast([P, 2, H]), ALU.mult).then_inc(on.olat_kept, 1)

            def square_mix(f, T):
                dve.wait_ge(on.attn_kept, f + 1)
                v.tensor_tensor(W[0][:, 0:8 * T], mix_raw[:, 0:8 * T], mix_raw[:, 0:8 * T], ALU.mult).then_inc(on.mix_squared, 1)

            def mix_norm(own, f, T):
                dve.wait_ge(on.mix_summed, f + 1)
                for half in range(2):
                    last = mean(W[0][:, half * 4 * T:(half + 1) * 4 * T], F[half][:, 0:4 * T], P)
                last.then_inc(on.mix_ms, 1)
                dve.wait_ge(on.mix_ms, f + 1)
                dve.wait_ge(on.mix_rs, f + 1)
                sharpen(own, W[0][:, 0:8 * T], W[1][:, 0:8 * T], W[2][:, 0:8 * T])
                own(v.tensor_tensor(W[2][:, 0:8 * T], mix_raw[:, 0:8 * T], W[1][:, 0:8 * T], ALU.mult))
                v.tensor_tensor(split(W[2][:, 0:8 * T], 8), split(W[2][:, 0:8 * T], 8), spread_cols(ROW_GOUT, 8, T), ALU.mult)\
                    .then_inc(on.mix_normed, 1)

            def mix_out(own, f, T):
                dve.wait_ge(on.w_used, f * PIECES + N_IN + N_OUT)
                after(dve, on.residual_in, f)
                for half in range(2):
                    cols = slice(half * 512, half * 512 + 512)
                    last = v.tensor_tensor(x1_next[0:T, cols], F[2 + half][0:T, :], x_t[0:T, cols], ALU.add)
                last.then_inc(on.x1_kept, 1)
                dve.wait_ge(on.x1_kept, f + 1)

            def ffn_norm(own, f, T):
                x1, xn = x1_next[0:T, :], xn2_next[0:T, :]
                own(v.tensor_tensor_reduce(W[0][0:T, :], x1, x1, 1.0, 0.0, ALU.mult, ALU.add, small_col(C_SS2, 1, T)))
                mean(small_col(C_MS2, 1, T), small_col(C_SS2, 1, T), D).then_inc(on.ffn_ms, 1)
                dve.wait_ge(on.ffn_rs, f + 1)
                sharpen(own, small_col(C_MS2, 1, T), small_col(C_Y2, 1, T), small_col(C_T2, 1, T))
                v.scalar_tensor_tensor(out=xn, in0=x1, scalar=small_col(C_Y2, 1, T), in1=g_ffn[0:T, :], op0=ALU.mult,
                                       op1=ALU.mult).then_inc(on.xn2_made, 1)

            def keep_ffn_turned(f, T):
                dve.wait_ge(on.xn2_turned, f + 1)
                for half in range(2):
                    last = v.tensor_copy(W[4][:, half * 4 * T:(half + 1) * 4 * T], F[4 + half][:, 0:4 * T])
                last.then_inc(on.xn2_kept, 1)

            def top16(own, values, scores, index):
                for r in range(2):
                    best = values[:, 8 * r:8 * r + 8]
                    own(v.max(best, scores), held=True)
                    last = v.max_index(index[:, 8 * r:8 * r + 8], best, scores)
                    if r == 0:
                        own(v.match_replace(scores, best, scores, LOW), held=True)
                return last

            def query(own, f, T, h):
                dve.wait_ge(on.key_scores_kept, f * PH + h + 1)
                waited(dve)
                for c in range(2):
                    last = top16(own, sv[0:T, h, c, :], keys_s[0:T, c, :], si_u[0:T, h, c, :])
                last.then_inc(on.top_keys_done, 1)
                dve.wait_ge(on.top_keys_done, f * PH + h + 1)
                grid = [T, TOPK, TOPK]
                scores = cand[0:T, h * 256:(h + 1) * 256]
                own(v.tensor_tensor(scores.rearrange("p (a b) -> p a b", a=TOPK), sv[0:T, h, 0, :].unsqueeze(2).to_broadcast(grid),
                                    sv[0:T, h, 1, :].unsqueeze(1).to_broadcast(grid), ALU.add), held=True)
                own(top16(own, top_s[0:T, h, :], scores, pos_u[0:T, h, :]))

            def look_up(own, T, half):
                hs = slice(half * PH // 2, (half + 1) * PH // 2)
                grid = [T, PH // 2, TOPK, TOPK]
                own(v.tensor_copy(si[0:T, hs], si_u[0:T, hs]))
                own(v.tensor_scalar(pos_ab[0:T, 0, hs], pos_u[0:T, hs], 4, None, ALU.logical_shift_right))
                own(v.tensor_scalar(pos_ab[0:T, 1, hs], pos_u[0:T, hs], TOPK - 1, None, ALU.bitwise_and))
                own(v.tensor_copy(pos_f[0:T, :, hs], pos_ab[0:T, :, hs]))
                for c in range(2):
                    own(v.tensor_tensor(hit[0:T], pos_f[0:T, c, hs].unsqueeze(3).to_broadcast(grid),
                                        iota16[0:T].unsqueeze(1).unsqueeze(1).to_broadcast(grid), ALU.is_equal))
                    own(v.tensor_tensor(hit[0:T], hit[0:T], si[0:T, hs, c].unsqueeze(2).to_broadcast(grid), ALU.mult))
                    own(v.tensor_reduce(picked_ab[0:T, c, hs], hit[0:T], AX.X, ALU.add))

            def select(own, f, T):
                gates = gate_next[0:T, :].rearrange("p (h k) -> p h k", h=PH)
                v.tensor_tensor(gates, top_s[0:T], top_s[0:T, :, 0:1].to_broadcast([T, PH, TOPK]), ALU.subtract)\
                    .then_inc(on.gate_max_made, 1)
                look_up(own, T, 1)
                dve.wait_ge(on.gate_exp_made, f + 1)
                total = small_col(C_GS, PH, T)
                own(v.tensor_reduce(total, gates, AX.X, ALU.add))
                own(v.reciprocal(small_col(C_GR, PH, T), total))
                own(v.tensor_tensor(gates, gates, small_col(C_GR, PH, T).unsqueeze(2).to_broadcast([T, PH, TOPK]), ALU.mult))
                dst = pick_next[0:T, :].rearrange("p (h k) -> p h k", h=PH) if T == P else picked_ab[0:T, 0]
                v.scalar_tensor_tensor(out=dst, in0=picked_ab[0:T, 0], scalar=float(KEYS), in1=picked_ab[0:T, 1],
                                       op0=ALU.mult, op1=ALU.add).then_inc(on.picked, 1)
                dve.wait_ge(on.picked, f + 1)
                if T == P:
                    if not isinstance(f, int):
                        dve.wait_ge(on.v_free, f * SLOTS - SLOTS // 2 + RING)
                    v.tensor_copy(pick_cur[:, 0:SLOTS // 2], pick_next[:, 0:SLOTS // 2]).then_inc(on.picked_moved, 1)

            def stage(own, f, T, name, n):
                if name == "norm":
                    norm_in(own, f, T)
                elif name == "turn":
                    keep_turned(f, T)
                elif name == "latent":
                    square_latents(f, T)
                elif name == "latent_norm":
                    latents(own, f, T)
                elif name == "z_gate":
                    conv_in(own, f, T)
                elif name == "conv":
                    conv(own, f, T)
                elif name == "q_latent":
                    q_rope(own, f, T)
                elif name == "head":
                    if n > 0:
                        head_end(own, f, n - 1)
                    if n < H:
                        head_start(own, f, n)
                elif name == "pages":
                    pages_stage(own, n)
                elif name == "attn":
                    square_mix(f, T)
                elif name == "mix_norm":
                    mix_norm(own, f, T)
                elif name == "mix_out":
                    mix_out(own, f, T)
                elif name == "ffn_norm":
                    ffn_norm(own, f, T)
                elif name == "ffn_turn":
                    keep_ffn_turned(f, T)
                elif name == "query":
                    if n > 0:
                        query(own, f, T, n - 1)
                elif name == "select":
                    if n == 0:
                        look_up(own, T, 0)
                    else:
                        select(own, f, T)

            def dot_group(it, g, first=0, end=G):
                for r in range(first, end):
                    slot = (g % 2) * G + r
                    dve.wait_ge(u_loaded[slot], (it * (GROUPS // 2) + g // 2 + 1) * 16)
                    v.tensor_tensor_reduce(u_ring[:, slot, :], u_ring[:, slot, :], xn2_cur[:], 1.0, 0.0, ALU.mult, ALU.add,
                                           dots[:, g * G + r:g * G + r + 1]).then_inc(on.u_free, 1)

            def weigh_group(it, g):
                dve.wait_ge(on.gelu_done, it * GROUPS + g + 1)
                s = slice(g * G, (g + 1) * G)
                v.tensor_tensor(wgt[:, s], gelu[:, s], gate_cur[:, s], ALU.mult).then_inc(on.w_made, 1)

            def sum_group(own, it, g):
                for s in range(g * G, (g + 1) * G):
                    if not by_vector(it, s):
                        continue
                    if vector_slots(it, s) == 1:
                        dve.wait_ge(on.q_kept, TILES + 1)
                        dve.wait_ge(on.w_made, it * GROUPS + g + 1)
                        own(v.memset(vector_acc, 0.0))
                    dve.wait_ge(on.w_made, it * GROUPS + g + 1)
                    dve.wait_ge(v_loaded[s % RING], (it * (GROUPS // 2) + g // 2 + 1) * 16)
                    if vector_slots(it, s) > 1:
                        dve.wait_ge(on.v_free_vector, vector_slots(it, s) - 1)
                    v.scalar_tensor_tensor(out=vector_acc, in0=v_ring[:, s % RING, :], scalar=wgt[:, s:s + 1], in1=vector_acc,
                                           op0=ALU.mult, op1=ALU.add).then_inc(on.v_free_vector, 1)

            def move_on(own, f):
                if not isinstance(f, int):
                    dve.wait_ge(on.w_made, f * GROUPS)
                    dve.wait_ge(on.u_free, f * SLOTS + RING)
                v.tensor_copy(gate_cur[:], gate_next[:])
                own(v.tensor_copy(xn2_cur[:], xn2_next))
                if not isinstance(f, int):
                    dve.wait_ge(on.v_free, f * SLOTS + RING)
                v.tensor_copy(pick_cur[:, SLOTS // 2:], pick_next[:, SLOTS // 2:]).then_inc(on.picks_moved, 1)

            def finalize(own, it, T):
                total = acc[0:T].rearrange("p a n -> p (a n)")
                dve.wait_ge(on.y_stored, (it + 1) * 16)
                if isinstance(it, int) and it == LAST:
                    own(v.tensor_tensor(y_t, total, vector_acc, ALU.add))
                else:
                    own(v.tensor_copy(y_t[0:T, :], total))
                v.tensor_tensor_reduce(total, y_t[0:T, :], y_t[0:T, :], 1.0, 0.0, ALU.mult, ALU.add, small_col(C_SS3, 1, T))\
                    .then_inc(on.acc_free, 1)
                dve.wait_ge(on.acc_free, it + 1)
                mean(small_col(C_MS3, 1, T), small_col(C_SS3, 1, T), D).then_inc(on.y_ms, 1)
                dve.wait_ge(on.y_ms, it + 1)
                dve.wait_ge(on.y_rs, it + 1)
                sharpen(own, small_col(C_MS3, 1, T), small_col(C_Y3, 1, T), small_col(C_T3, 1, T))
                v.scalar_tensor_tensor(out=y_t[0:T, :], in0=y_t[0:T, :], scalar=small_col(C_Y3, 1, T), in1=g_fin[0:T, :],
                                       op0=ALU.mult, op1=ALU.mult).then_inc(on.y_made, 1)

            def tile(it, T):
                own = Own(dve, on.dve_front, (it + 1) * DVE_FRONT)
                dot_group(it, 0)
                for g in range(GROUPS):
                    stages = beside(g, T)
                    half = G // 2 if has_pages(stages) else G
                    if g + 1 < GROUPS:
                        dot_group(it, g + 1, 0, half)
                    weigh_group(it, g)
                    before = 1 if has_pages(stages) else len(stages)
                    for name, n in stages[:before]:
                        stage(own, it + 1, T, name, n)
                    if g + 1 < GROUPS:
                        dot_group(it, g + 1, half, G)
                    sum_group(own, it, g)
                    for name, n in stages[before:]:
                        stage(own, it + 1, T, name, n)
                if T == P:
                    own.check(DVE_FRONT)
                own2 = Own(dve, on.dve_peer, it * DVE_PEER + 1)
                if T == P:
                    move_on(own2, it + 1)
                else:
                    dve.wait_ge(on.s_turned, 1)
                    v.tensor_copy(s_pick[:], F[0][:, 0:SB]).then_inc(on.s_slots, 1)
                    own2(v.tensor_copy(wgt[:, 0:SB], F[0][:, SB:2 * SB]))
                    dve.wait_ge(on.v_free, RING + tensor_slots(LAST, SLOTS - 1))
                    dve.wait_ge(on.v_free_vector, vector_slots(LAST, SLOTS - 1))
                finalize(own2, it, P)
                if T == P:
                    own2.check(DVE_PEER)

            own = Own(dve, on.dve_setup, 0)
            own(v.memset(z_ext[:, :, 0:2], 0.0))
            v.memset(s_fan[:], 0.0).then_inc(on.u_free, RING)
            v.memset(gelu[:], 0.0).then_inc(on.v_free, RING)
            v.memset(dots[:], 0.0).then_inc(on.y_stored, 16)
            dve.wait_ge(on.consts_ready, 6 * 16)
            front = Own(dve, on.dve_front, 0)
            for name, n in stages_of(P):
                if name == "head" and n == 0:
                    dve.wait_ge(on.gains_loaded, 3 * 16)
                stage(front, 0, P, name, n)
                if name == "norm":
                    dve.wait_ge(on.vec_turned, 1)
                    v.tensor_copy(vec_cols[:], acc[:, 0, 0:VEC_ROWS]).then_inc(on.vec_kept, 1)
                    dve.wait_ge(on.vec_kept, 1)
                elif name == "latent":
                    dve.wait_ge(on.uk_turned, 1)
                    for h in range(2):
                        last = v.tensor_copy(w_ukT[:, 2 * h:2 * h + 2, :], acc[:, h, :].rearrange("p (h r) -> p h r", h=2))
                    last.then_inc(on.uk_kept, 1)
                elif name == "z_in":
                    dve.wait_ge(on.sub_turned, 1)
                    own(v.tensor_copy(sub_keysT[:].rearrange("p c k -> p (c k)"), acc[:, 0, 0:2 * KEYS]))
                    dve.wait_ge(on.state_turned, 1)
                    for k in range(2):
                        last = v.tensor_copy(z_s[:, :, k, :], acc[:, 1, 0:8 * SB].rearrange("p (c b k) -> p c b k", c=4, k=2)[:, :, :, k])
                    last.then_inc(on.state_kept, 1)
            front.check(DVE_FRONT)
            move_on(Own(dve, on.dve_peer, 0), 0)
            with dve.Fori(0, TILES - 1) as it:
                tile(it, P)
            tile(TILES - 1, SB)
            own = Own(dve, on.dve_tail, 0)
            dve.wait_ge(on.srow_loaded, SB * 16)
            for t in range(SB):
                dve.wait_ge(u_loaded[t], (TILES * (GROUPS // 2) + 1) * 16)
                v.tensor_tensor_reduce(u_ring[:, t, :], u_ring[:, t, :], SPREAD[t], 1.0, 0.0, ALU.mult, ALU.add,
                                       dots[:, t:t + 1]).then_inc(on.s_dots, 1)
            dve.wait_ge(on.s_gelu, 1)
            v.tensor_tensor(s_fan[:].rearrange("p a b -> p (a b)")[:, 0:SB * SB:SB + 1], gelu[:, 0:SB], wgt[:, 0:SB], ALU.mult)\
                .then_inc(on.s_weights, 1)
            dve.wait_ge(on.v_free, RING + tensor_slots(LAST, SLOTS - 1) + 1)
            finalize(own, TILES, SB)

        @block.gpsimd
        def _(pool):
            pool.memset(ckv_rows[:], 0.0).then_inc(on.zeroed, 1)
            pool.memset(ckvT[:], 0.0).then_inc(on.zeroed, 1)
            pool.memset(krT[:], 0.0).then_inc(on.zeroed, 1)

            def gather(table, ring, slot, loaded, pick):
                pool.indirect_dma_start(ring[:, slot, :], None, a[table][0],
                                        bass.IndirectOffsetOnAxis(ap=pick, axis=0)).then_inc(loaded[slot], 16)

            def gather_group(it, g, table, ring, loaded):
                if g * G == SLOTS // 2:
                    pool.wait_ge(on.picks_moved, it + 1)
                for s in range(g * G, (g + 1) * G):
                    if table == "expert_u":
                        pool.wait_ge(on.u_free, it * SLOTS + s + 1)
                    elif by_vector(it, s - RING):
                        pool.wait_ge(on.v_free_vector, vector_slots(it, s - RING))
                    else:
                        pool.wait_ge(on.v_free, RING + tensor_slots(it, s - RING))
                    waited(pool)
                    gather(table, ring, s % RING, loaded, pick_cur[:, s:s + 1])

            def tile(it):
                pool.wait_ge(on.picked_moved, it + 1)
                gather_group(it, 0, "expert_u", u_ring, u_loaded)
                for g in range(GROUPS):
                    if g + 1 < GROUPS:
                        gather_group(it, g + 1, "expert_u", u_ring, u_loaded)
                    gather_group(it, g, "expert_v", v_ring, v_loaded)

            with pool.Fori(0, LAST) as it:
                tile(it)
            tile(LAST)
            pool.wait_ge(on.s_slots, 1)
            pool.wait_ge(on.u_free, TILES * SLOTS + RING)
            for t in range(SB):
                gather("expert_u", u_ring, t, u_loaded, s_pick[:, t:t + 1])
            pool.wait_ge(on.v_free, RING + tensor_slots(LAST, SLOTS - 1))
            pool.wait_ge(on.v_free_vector, vector_slots(LAST, SLOTS - 1))
            for t in range(SB):
                gather("expert_v", v_ring, t, v_loaded, s_pick[:, t:t + 1])


IN_NAMES = ["x_prompt", "x_sample", "cache_ckv", "cache_krope", "state_conv", "page_table", "g_mix_norm", "w_in", "g_q",
            "w_uq", "g_kv", "w_uk", "w_uv", "conv_w", "g_attn_out", "g_conv_out", "w_o", "g_ffn_norm", "w_query",
            "sub_keys", "expert_u", "expert_v", "g_final"]
OUT_SHAPES = {"y_prompt": (1, SEQ, D), "y_sample": (SB, 1, D), "new_ckv_prompt": (1, 1, SEQ, KV),
              "new_krope_prompt": (1, 1, SEQ, ROPE), "new_conv_prompt": (1, 1, 2, CW), "new_ckv_sample": (1, SB, 1, KV),
              "new_krope_sample": (1, SB, 1, ROPE), "new_conv_sample": (1, SB, 2, CW)}


def constants():
    import numpy as np

    f32 = np.float32
    rot = np.zeros((ROPE, ROPE), f32)
    for p in range(ROPE // 2):
        rot[p + ROPE // 2, p] = -1.0
        rot[p, p + ROPE // 2] = 1.0
    inv = (f32(10000.0) ** (-np.arange(0, ROPE, 2, dtype=f32) / f32(ROPE))).astype(f32)
    pos = np.concatenate([np.arange(SEQ), np.full(SB, PAST)]).astype(f32)
    ang = (pos[:, None] * inv[None, :]).astype(f32)
    table = np.stack([np.concatenate([t, t], axis=1).T for t in (np.cos(ang), np.sin(ang))])
    own = np.full((SB, SB), -BIG, f32)
    np.fill_diagonal(own, 0.0)
    return {
        "c_ident": np.eye(P, dtype=f32), "c_ones": np.ones((P, P), f32), "c_rot": rot,
        "c_limit": ((np.arange(TILES)[None, :] * P + np.arange(P)[:, None] + 0.5) * BIG).astype(f32),
        "c_iota16": np.tile(np.arange(TOPK, dtype=f32), (P, 1)), "c_own": own,
        "c_rope": np.ascontiguousarray(table.astype(f32)), "c_low": (-np.arange(512) * BIG).astype(f32),
    }


def kernel(**inputs):
    import numpy as np
    import concourse.bacc as bacc
    from concourse.bass_utils import run_bass_kernel_spmd

    nc = bacc.Bacc("TRN2", target_bir_lowering=False, num_devices=1)
    arrays = {n: np.ascontiguousarray(inputs[n]) for n in IN_NAMES}
    arrays.update(constants())
    a = {n: nc.dram_tensor(f"in_{n}", x.shape, mybir.dt.from_np(x.dtype), kind="ExternalInput").ap() for n, x in arrays.items()}
    a["scratch"] = nc.dram_tensor("scratch", (SB, D), F32, kind="Internal").ap()
    out = {n: nc.dram_tensor(f"out_{n}", s, F32, kind="ExternalOutput").ap() for n, s in OUT_SHAPES.items()}
    build(nc, a, out)
    r = run_bass_kernel_spmd(nc, [{f"in_{n}": x for n, x in arrays.items()}], core_ids=[0])
    return tuple(r.results[0][f"out_{n}"] for n in OUT_SHAPES)
```
